# Optimizing a Trainium2 kernel written in Bass

```python
import functools
import jax, jax.numpy as jnp
from jax import lax
import numpy as np

D_MODEL = 1024
BATCH = 1
SEQ = 1024
DEPTH = 1
DEC_BATCH = 8
DEC_SEQ = 8
PAST_LEN = 8192
PAGE_SIZE = 128

N_META = 16
H_R = 8
HD_R = 64
C_R = H_R * HD_R
D_W_LORA = 64
D_A_LORA = 64
D_G_LORA = 128
P_R = 3 * C_R + D_W_LORA + D_A_LORA + D_G_LORA
LNX_EPS = 64e-5
H_A = 8
H_KV = 4
HD_A = 64
C_A = H_A * HD_A
C_KV = H_KV * HD_A
H_IDX = 8
D_IDX = 64
TOPK_MAX = 256
P_A = C_A + 2 * C_KV + H_IDX * D_IDX + H_IDX + D_IDX
ROPE_THETA = 500000.0
ROT_FRAC = 4
Q_BLOCK = 128
P_G = 2 * D_MODEL
N_IN = P_R + P_A + P_G
D_FF = ((8 * D_MODEL // 3 + 127) // 128) * 128
CONV_W = 3
RMS_EPS = 1e-6

kernel_name = 'hybrid_rwkv7_dsa_step'

def rms_norm(x, g):
    xf = x.astype(jnp.float32)
    y = xf * lax.rsqrt(jnp.mean(xf * xf, axis=-1, keepdims=True) + RMS_EPS)
    return (y * g.astype(jnp.float32)).astype(x.dtype)

def rope_partial(x, pos):
    d = x.shape[-1]
    rot = d // ROT_FRAC
    half = rot // 2
    inv = ROPE_THETA ** (-jnp.arange(half, dtype=jnp.float32) / half)
    ang = pos.astype(jnp.float32)[:, None] * inv[None, :]
    ang = ang.reshape((1, pos.shape[0]) + (1,) * (x.ndim - 3) + (half,))
    cos, sin = jnp.cos(ang), jnp.sin(ang)
    xf = x.astype(jnp.float32)
    x1, x2, rest = xf[..., :half], xf[..., half:rot], xf[..., rot:]
    out = jnp.concatenate([x1 * cos - x2 * sin, x2 * cos + x1 * sin, rest], axis=-1)
    return out.astype(x.dtype)

def split_cols(p):
    o = 0
    p_r = p[..., o:o + P_R]; o += P_R
    p_a = p[..., o:o + P_A]; o += P_A
    g_r = p[..., o:o + D_MODEL]; o += D_MODEL
    g_a = p[..., o:o + D_MODEL]
    return p_r, p_a, g_r, g_a

def _rwkv7_step(S, inp):
    r, dec, k, v, kk, a = inp
    sa = jnp.einsum('bhvk,bhk->bhv', S, -kk)
    S = S * dec[:, :, None, :] + sa[..., None] * (kk * a)[:, :, None, :] + v[..., None] * k[:, :, None, :]
    y = jnp.einsum('bhvk,bhk->bhv', S, r)
    return S, y

def rwkv7_branch(p_r, shift_prev, s_prev, lp):
    B, T, _ = p_r.shape
    f32 = jnp.float32
    prev = jnp.concatenate([shift_prev[:, None, :].astype(p_r.dtype), p_r[:, :-1]], axis=1)
    pm = p_r + (prev - p_r) * lp['rwkv_mu']
    r = pm[..., :C_R]
    k = pm[..., C_R:2 * C_R]
    v = pm[..., 2 * C_R:3 * C_R]
    o = 3 * C_R
    wd = pm[..., o:o + D_W_LORA]; o += D_W_LORA
    ad = pm[..., o:o + D_A_LORA]; o += D_A_LORA
    gd = pm[..., o:o + D_G_LORA]
    w = -jax.nn.softplus(-(lp['rwkv_w0'] + jnp.tanh(wd) @ lp['rwkv_w_w2'])) - 0.5
    decay = jnp.exp(-jnp.exp(w.astype(f32)))
    a = jax.nn.sigmoid(lp['rwkv_a0'] + ad @ lp['rwkv_w_a2'])
    g = jax.nn.sigmoid(gd) @ lp['rwkv_w_g2']
    heads = lambda t: t.reshape(B, T, H_R, HD_R).astype(f32)
    kk = heads(k * lp['rwkv_k_k'])
    kk = kk * lax.rsqrt(jnp.maximum(jnp.sum(kk * kk, axis=-1, keepdims=True), 1e-24))
    k = k * (1 + (a - 1) * lp['rwkv_k_a'])
    rh, kh, vh, ah, dh = heads(r), heads(k), heads(v), heads(a), heads(decay)
    xs = tuple(jnp.moveaxis(t, 1, 0) for t in (rh, dh, kh, vh, kk, ah))
    s_fin, y = lax.scan(_rwkv7_step, s_prev.astype(f32), xs)
    y = jnp.moveaxis(y, 0, 1)
    mean = jnp.mean(y, axis=-1, keepdims=True)
    var = jnp.mean(jnp.square(y - mean), axis=-1, keepdims=True)
    y = ((y - mean) * lax.rsqrt(var + LNX_EPS)).reshape(B, T, C_R)
    y = y * lp['rwkv_lnx_g'] + lp['rwkv_lnx_b']
    y = y + (jnp.sum(rh * kh * lp['rwkv_r_k'], axis=-1, keepdims=True) * vh).reshape(B, T, C_R)
    out = (y * g.astype(f32)).astype(p_r.dtype)
    return out, s_fin, p_r[:, -1]

def dsa_project(p_a, pos):
    B, T, _ = p_a.shape
    o = 0
    q = p_a[..., o:o + C_A].reshape(B, T, H_A, HD_A); o += C_A
    k = p_a[..., o:o + C_KV].reshape(B, T, H_KV, HD_A); o += C_KV
    v = p_a[..., o:o + C_KV].reshape(B, T, H_KV, HD_A); o += C_KV
    qi = p_a[..., o:o + H_IDX * D_IDX].reshape(B, T, H_IDX, D_IDX); o += H_IDX * D_IDX
    wi = p_a[..., o:o + H_IDX] * (H_IDX ** -0.5); o += H_IDX
    ki = p_a[..., o:o + D_IDX]
    return (rope_partial(q, pos), rope_partial(k, pos), v,
            rope_partial(qi, pos), wi, rope_partial(ki, pos))

def indexer_topk(qi, wi, ki_all, q_pos, n_top):
    sc = jnp.einsum('bqhd,bsd->bqhs', qi, ki_all).astype(jnp.float32) * (D_IDX ** -0.5)
    score = jnp.einsum('bqhs,bqh->bqs', jax.nn.relu(sc), wi.astype(jnp.float32))
    key_pos = jnp.arange(ki_all.shape[1])
    vis = key_pos[None, None, :] <= q_pos[None, :, None]
    score = jnp.where(vis, score, -jnp.inf)
    _, idx = lax.top_k(score, n_top)
    valid = idx <= q_pos[None, :, None]
    return idx, valid

def sparse_attend(q, k_sel, v_sel, valid):
    B, Q = q.shape[:2]
    qg = q.reshape(B, Q, H_KV, H_A // H_KV, HD_A)
    s = jnp.einsum('bqngd,bqknd->bqngk', qg, k_sel).astype(jnp.float32) * (HD_A ** -0.5)
    s = jnp.where(valid[:, :, None, None, :], s, -jnp.inf)
    p = jax.nn.softmax(s, axis=-1)
    o = jnp.einsum('bqngk,bqknd->bqngd', p.astype(v_sel.dtype), v_sel)
    return o.reshape(B, Q, C_A)

def dsa_prompt(q, k, v, qi, wi, ki, n_top):
    B, T = q.shape[:2]
    n_blk = -(-T // Q_BLOCK)
    pad = n_blk * Q_BLOCK - T

    def blocks(t):
        t = jnp.pad(t, [(0, 0), (0, pad)] + [(0, 0)] * (t.ndim - 2))
        return jnp.moveaxis(t.reshape((B, n_blk, Q_BLOCK) + t.shape[2:]), 1, 0)

    pos_b = jnp.arange(n_blk * Q_BLOCK).reshape(n_blk, Q_BLOCK)
    bidx = jnp.arange(B)[:, None, None]

    def one_block(xs):
        qb, qib, wib, pb = xs
        idx, valid = indexer_topk(qib, wib, ki, pb, n_top)
        return sparse_attend(qb, k[bidx, idx], v[bidx, idx], valid)

    o = lax.map(one_block, (blocks(q), blocks(qi), blocks(wi), pos_b))
    return jnp.moveaxis(o, 0, 1).reshape(B, n_blk * Q_BLOCK, C_A)[:, :T]

def dsa_sample(q, k, v, qi, wi, ki, cache_k, cache_v, cache_kidx, page_table):
    B, Q = q.shape[:2]
    past = page_table.shape[1] * PAGE_SIZE
    ki_past = cache_kidx[page_table].reshape(B, past, D_IDX).astype(ki.dtype)
    ki_all = jnp.concatenate([ki_past, ki], axis=1)
    q_pos = past + jnp.arange(Q)
    n_top = min(TOPK_MAX, (past + Q) // 4)
    idx, valid = indexer_topk(qi, wi, ki_all, q_pos, n_top)
    bidx = jnp.arange(B)[:, None, None]
    in_past = idx < past
    s_p = jnp.minimum(idx, past - 1)
    phys = page_table[bidx, s_p // PAGE_SIZE]
    off = s_p % PAGE_SIZE
    s_n = jnp.clip(idx - past, 0, Q - 1)

    def select(pool, new):
        return jnp.where(in_past[..., None, None], pool[phys, off].astype(new.dtype), new[bidx, s_n])

    return sparse_attend(q, select(cache_k, k), select(cache_v, v), valid)

def conv_ffn(h, conv_prev, lp):
    B, T, _ = h.shape
    u = h @ lp['w_up']
    a, b = u[..., :D_FF], u[..., D_FF:]
    ext = jnp.concatenate([conv_prev.astype(a.dtype), a], axis=1)
    c = lp['conv_b'] + ext[:, 0:T] * lp['conv_w'][0]
    for j in range(1, CONV_W):
        c = c + ext[:, j:j + T] * lp['conv_w'][j]
    y = (jax.nn.gelu(c, approximate=False) * b) @ lp['w_down']
    return y, ext[:, T:]

def trunk_layer(x, pos, attend, shift_prev, s_prev, conv_prev, lp):
    h = rms_norm(x, lp['norm1_g']) @ lp['w_in']
    p_r, p_a, g_r, g_a = split_cols(h)
    y_r, s_fin, shift_last = rwkv7_branch(p_r, shift_prev, s_prev, lp)
    q, k, v, qi, wi, ki = dsa_project(p_a, pos)
    y_a = attend(q, k, v, qi, wi, ki)
    merged = (jax.nn.sigmoid(g_r) * (y_r @ lp['w_br_rwkv'])
              + jax.nn.sigmoid(g_a) * (y_a @ lp['w_br_attn']))
    x = x + merged @ lp['w_out']
    f, conv_last = conv_ffn(rms_norm(x, lp['norm2_g']), conv_prev, lp)
    x = x + f
    return x, (k, v, ki, s_fin, shift_last, conv_last)

def setup_inputs(seed: int = 0) -> dict:
    key = jax.random.key(seed)
    keys = iter(jax.random.split(key, 48))
    nrm = lambda shape, scale: jax.random.normal(next(keys), shape, jnp.float32) * scale
    uni = lambda shape, lo, hi: jax.random.uniform(next(keys), shape, jnp.float32, lo, hi)
    n_pages = PAST_LEN // PAGE_SIZE
    n_used = DEC_BATCH * n_pages
    n_pool = n_used + n_used // 4
    perm = jax.random.permutation(next(keys), n_pool)
    page_table = perm[:n_used].reshape(DEC_BATCH, n_pages).astype(jnp.int32)
    L = DEPTH
    return {
        'x_prompt': nrm((BATCH, SEQ, D_MODEL), 1.0),
        'x_sample': nrm((DEC_BATCH, DEC_SEQ, D_MODEL), 1.0),
        'cache_k': nrm((L, n_pool, PAGE_SIZE, H_KV, HD_A), 1.0),
        'cache_v': nrm((L, n_pool, PAGE_SIZE, H_KV, HD_A), 1.0),
        'cache_kidx': nrm((L, n_pool, PAGE_SIZE, D_IDX), 1.0),
        'state_rwkv': nrm((L, DEC_BATCH, H_R, HD_R, HD_R), 0.5),
        'state_rwkv_shift': nrm((L, DEC_BATCH, P_R), 1.0),
        'state_ffn_conv': nrm((L, DEC_BATCH, CONV_W - 1, D_FF), 1.0),
        'page_table': page_table,
        'meta_tokens': nrm((N_META, D_MODEL), 1.0),
        'norm1_g': 1.0 + nrm((L, D_MODEL), 0.02),
        'w_in': nrm((L, D_MODEL, N_IN), D_MODEL ** -0.5),
        'rwkv_mu': uni((L, P_R), 0.0, 1.0),
        'rwkv_w0': uni((L, C_R), -6.0, 0.0),
        'rwkv_w_w2': nrm((L, D_W_LORA, C_R), 0.1),
        'rwkv_a0': nrm((L, C_R), 0.1),
        'rwkv_w_a2': nrm((L, D_A_LORA, C_R), D_A_LORA ** -0.5),
        'rwkv_w_g2': nrm((L, D_G_LORA, C_R), D_G_LORA ** -0.5),
        'rwkv_k_k': 0.85 + nrm((L, C_R), 0.02),
        'rwkv_k_a': 1.0 + nrm((L, C_R), 0.02),
        'rwkv_r_k': nrm((L, H_R, HD_R), 0.1),
        'rwkv_lnx_g': 1.0 + nrm((L, C_R), 0.02),
        'rwkv_lnx_b': nrm((L, C_R), 0.02),
        'w_br_rwkv': nrm((L, C_R, D_MODEL), C_R ** -0.5),
        'w_br_attn': nrm((L, C_A, D_MODEL), C_A ** -0.5),
        'w_out': nrm((L, D_MODEL, D_MODEL), D_MODEL ** -0.5),
        'norm2_g': 1.0 + nrm((L, D_MODEL), 0.02),
        'w_up': nrm((L, D_MODEL, 2 * D_FF), D_MODEL ** -0.5),
        'conv_w': nrm((L, CONV_W, D_FF), CONV_W ** -0.5),
        'conv_b': nrm((L, D_FF), 0.02),
        'w_down': nrm((L, D_FF, D_MODEL), D_FF ** -0.5),
        'final_norm_g': 1.0 + nrm((D_MODEL,), 0.02),
    }

def reference(x_prompt, x_sample, cache_k, cache_v, cache_kidx, state_rwkv, state_rwkv_shift,
              state_ffn_conv, page_table, meta_tokens, norm1_g, w_in, rwkv_mu, rwkv_w0, rwkv_w_w2,
              rwkv_a0, rwkv_w_a2, rwkv_w_g2, rwkv_k_k, rwkv_k_a, rwkv_r_k, rwkv_lnx_g, rwkv_lnx_b,
              w_br_rwkv, w_br_attn, w_out, norm2_g, w_up, conv_w, conv_b, w_down, final_norm_g):
    B = x_prompt.shape[0]
    meta = jnp.broadcast_to(meta_tokens[None].astype(x_prompt.dtype), (B, N_META, x_prompt.shape[2]))
    xp = jnp.concatenate([meta, x_prompt], axis=1)
    T = xp.shape[1]
    xs = x_sample
    past = page_table.shape[1] * PAGE_SIZE
    pos_p = jnp.arange(T)
    pos_s = past + jnp.arange(xs.shape[1])
    n_top_p = min(TOPK_MAX, x_prompt.shape[1] // 4)
    new_p, new_s = [], []
    for l in range(DEPTH):
        lp = {
            'norm1_g': norm1_g[l], 'w_in': w_in[l], 'rwkv_mu': rwkv_mu[l], 'rwkv_w0': rwkv_w0[l],
            'rwkv_w_w2': rwkv_w_w2[l], 'rwkv_a0': rwkv_a0[l], 'rwkv_w_a2': rwkv_w_a2[l],
            'rwkv_w_g2': rwkv_w_g2[l], 'rwkv_k_k': rwkv_k_k[l], 'rwkv_k_a': rwkv_k_a[l],
            'rwkv_r_k': rwkv_r_k[l], 'rwkv_lnx_g': rwkv_lnx_g[l], 'rwkv_lnx_b': rwkv_lnx_b[l],
            'w_br_rwkv': w_br_rwkv[l], 'w_br_attn': w_br_attn[l], 'w_out': w_out[l],
            'norm2_g': norm2_g[l], 'w_up': w_up[l], 'conv_w': conv_w[l], 'conv_b': conv_b[l],
            'w_down': w_down[l],
        }
        xp, st_p = trunk_layer(
            xp, pos_p, functools.partial(dsa_prompt, n_top=n_top_p),
            jnp.zeros((B, P_R), xp.dtype), jnp.zeros((B, H_R, HD_R, HD_R), jnp.float32),
            jnp.zeros((B, CONV_W - 1, D_FF), xp.dtype), lp)
        xs, st_s = trunk_layer(
            xs, pos_s,
            functools.partial(dsa_sample, cache_k=cache_k[l], cache_v=cache_v[l],
                              cache_kidx=cache_kidx[l], page_table=page_table),
            state_rwkv_shift[l], state_rwkv[l], state_ffn_conv[l], lp)
        new_p.append(st_p)
        new_s.append(st_s)
    stk = lambda lst, i: jnp.stack([e[i] for e in lst], axis=0)
    y_prompt = rms_norm(xp, final_norm_g)[:, N_META:]
    y_sample = rms_norm(xs, final_norm_g)
    return (y_prompt, y_sample,
            stk(new_p, 0), stk(new_p, 1), stk(new_p, 2), stk(new_p, 3), stk(new_p, 4), stk(new_p, 5),
            stk(new_s, 0), stk(new_s, 1), stk(new_s, 2), stk(new_s, 3), stk(new_s, 4), stk(new_s, 5))


_drawn_inputs = setup_inputs


def setup_inputs(seed=0):
    import zlib

    import numpy as np

    out = dict(_drawn_inputs(seed))
    spreads = {}
    factors = {'rwkv_k_k': 2.702,
     'rwkv_k_a': 2.809,
     'rwkv_lnx_g': 8.0,
     'rwkv_lnx_b': 8.0,
     'norm2_g': 2.77,
     'conv_b': 5.433,
     'final_norm_g': 2.894}
    for name, (base, spread) in spreads.items():
        noise = np.random.default_rng([zlib.crc32(name.encode()), seed]).standard_normal(out[name].shape)
        drawn = base * np.exp(spread * noise) if base else spread * noise
        out[name] = __import__('jax').numpy.asarray(drawn.astype(out[name].dtype))
    for name, factor in factors.items():
        out[name] = (out[name] * factor).astype(out[name].dtype)
    return out
```

```python
import concourse.bass as bass
from concourse import mybir
from contextlib import ExitStack

F32 = mybir.dt.float32
I32 = mybir.dt.int32
U32 = mybir.dt.uint32
ALU = mybir.AluOpType
ACT = mybir.ActivationFunctionType
AX = mybir.AxisListType

D = 1024
KD = D // 128
N_META, SEQ = 16, 1024
TP = N_META + SEQ
NSEQ, QS = 8, 8
TS = NSEQ * QS
R = TP + TS
BLOCKS = [(r, min(128, R - r)) for r in range(0, R, 128)]
NB = len(BLOCKS)
EPS = 1e-6
HD = 64
P_R, P_A = 1792, 1608
CQ, CK, CQI, CKI, CV, CWI = 0, 512, 768, 1280, 1344, 1600
PAST, PAGE, NPAGES, NPOOL = 8192, 128, 64, 640
TOPK = 256
BIG = 1e30
LOW, TAKEN = -3.0e38, -3.3e38
DFF = 2816


def norm(nc, ctx, K, tag, x, gain, xT, ident):
    with ExitStack() as sc:
        sc.enter_context(nc.cleanup_on_exit())
        X = sc.enter_context(nc.sbuf_tensor(f"{tag}_X", [128, 3, D], F32))
        junk = sc.enter_context(nc.sbuf_tensor(f"{tag}_junk", [128, D], F32))
        ss = sc.enter_context(nc.sbuf_tensor(f"{tag}_ss", [128, NB], F32))
        mhalf = sc.enter_context(nc.sbuf_tensor(f"{tag}_mhalf", [128, 1], F32))
        rs = sc.enter_context(nc.sbuf_tensor(f"{tag}_rs", [128, NB], F32))
        g = sc.enter_context(nc.sbuf_tensor(f"{tag}_g", [128, KD], F32))
        PS = sc.enter_context(nc.psum_tensor(f"{tag}_PS", [128, 2, KD, 128], F32))
        loaded = [nc.alloc_semaphore(name=f"{tag}_loaded{i}") for i in range(3)]
        g_in, summed, rooted, scaled, turned, stored = (
            nc.alloc_semaphore(name=f"{tag}_{n}")
            for n in ("g_in", "summed", "rooted", "scaled", "turned", "stored"))
        with nc.Block() as block:
            @block.sync
            def _(sp):
                sp.dma_start(g[:, :], gain.rearrange("(k p) -> p k", p=128),
                             allow_slow_non_contiguous=True).then_inc(g_in, 16)
                for b, (r, n) in enumerate(BLOCKS):
                    if b >= 3:
                        sp.wait_ge(turned, b - 2)
                    sp.dma_start(X[0:n, b % 3, :], x[r:r + n, :]).then_inc(loaded[b % 3], 16)

            @block.scalar
            def _(act):
                for b, (r, n) in enumerate(BLOCKS):
                    act.wait_ge(loaded[b % 3], 16 * (b // 3 + 1))
                    act.activation(junk[0:n, :], X[0:n, b % 3, :], ACT.Square,
                                   accum_out=ss[0:n, b:b + 1]).then_inc(summed, 1)
                    act.drain()

            @block.gpsimd
            def _(pool):
                pool.memset(mhalf[:, :], -0.5)
                for b, (r, n) in enumerate(BLOCKS):
                    pool.wait_ge(summed, b + 1)
                    pool.tensor_scalar(rs[0:n, b:b + 1], ss[0:n, b:b + 1], 1.0 / D, EPS, ALU.mult, ALU.add)
                    pool.drain()
                    pool.tensor_tensor(rs[0:n, b:b + 1], rs[0:n, b:b + 1], mhalf[0:n, :],
                                       ALU.pow).then_inc(rooted, 1)

            @block.vector
            def _(dve):
                dve.wait_ge(g_in, 16)
                for b, (r, n) in enumerate(BLOCKS):
                    dve.wait_ge(rooted, b + 1)
                    dve.tensor_scalar(X[0:n, b % 3, :], X[0:n, b % 3, :], rs[0:n, b:b + 1], None,
                                      ALU.mult).then_inc(scaled, 1)
                    dve.wait_ge(turned, b + 1)
                    dve.tensor_tensor(xT[:, :, r:r + n], PS[:, b % 2, :, 0:n],
                                      g[:, :].rearrange("p (k a) -> p k a", a=1).to_broadcast([128, KD, n]),
                                      ALU.mult).then_inc(stored, 1)

            @block.tensor
            def _(pe):
                for b, (r, n) in enumerate(BLOCKS):
                    pe.wait_ge(scaled, b + 1)
                    if b >= 2:
                        pe.wait_ge(stored, b - 1)
                    for k in range(KD):
                        last = pe.transpose(PS[:, b % 2, k, 0:n], X[0:n, b % 3, 128 * k:128 * k + 128],
                                            ident[0:n, 0:n])
                    last.then_inc(turned, 1)


def dsa_project(nc, w_in, cos, sin, xT, ident, T, k_out, v_out, ki_out, S):
    NC4 = P_A // 4
    with ExitStack() as sc:
        sc.enter_context(nc.cleanup_on_exit())
        W = sc.enter_context(nc.sbuf_tensor("pa_W", [128, KD, P_A], F32))
        H = sc.enter_context(nc.sbuf_tensor("pa_H", [128, 2, P_A], F32))
        KID = sc.enter_context(nc.sbuf_tensor("pa_KID", [128, 2, 128], F32))
        cs = sc.enter_context(nc.sbuf_tensor("pa_cs", [128, NB, 2, 8], F32))
        t = sc.enter_context(nc.sbuf_tensor("pa_t", [128, 4, 21, 8], F32))
        PG = sc.enter_context(nc.psum_tensor("pa_PG", [128, 4, 512], F32))
        PT = sc.enter_context(nc.psum_tensor("pa_PT", [128, 12, 128], F32))
        w_loaded = [nc.alloc_semaphore(name=f"pa_w_loaded{k}") for k in range(KD)]
        written = [nc.alloc_semaphore(name=f"pa_written{i}") for i in range(2)]
        cs_in, gemm_done, copied, roped, turned, stored, spilled = (
            nc.alloc_semaphore(name=f"pa_{n}")
            for n in ("cs_in", "gemm_done", "copied", "roped", "turned", "stored", "spilled"))
        pieces = [(CK, 512, 256), (CQI, 1024, 512), (CKI, 1544, 64), (CV, 768, 256), (CWI, 1536, 8)]
        with nc.Block() as block:
            @block.sync
            def _(sp):
                for k in range(KD):
                    for dst, src, w in pieces:
                        sp.dma_start(W[:, k, dst:dst + w],
                                     w_in[128 * k:128 * k + 128, P_R + src:P_R + src + w]
                                     ).then_inc(w_loaded[k], 16)
                    src = w_in[128 * k:128 * k + 128, P_R:P_R + 512].rearrange(
                        "p (m h g d) -> p m g h d", m=2, h=2, g=2)
                    for m in range(2):
                        for g in range(2):
                            c = CQ + 256 * m + 128 * g
                            sp.dma_start(W[:, k, c:c + 128].rearrange("p (h d) -> p h d", h=2),
                                         src[:, m, g]).then_inc(w_loaded[k], 16)
                    if k == 0:
                        for j, c in enumerate((cos, sin)):
                            sp.dma_start(cs[:, :, j, :], c).then_inc(cs_in, 16)
                for b, (r, n) in enumerate(BLOCKS):
                    sp.wait_ge(roped, b + 1)
                    for dst, c, w in ((k_out, CK, 256), (v_out, CV, 256), (ki_out, CKI, 64)):
                        sp.dma_start(dst[r:r + n, :], H[0:n, b % 2, c:c + w]).then_inc(written[b % 2], 16)
                for i in range(2):
                    sp.wait_ge(written[i], 48 * ((NB + 1 - i) // 2))
                sp.wait_ge(stored, NB)
                sp.dma_start(S["qT"], T["QT"][:, :, TP:R]).then_inc(spilled, 16)
                sp.dma_start(S["qiT"], T["QIT"][:, :, TP:R]).then_inc(spilled, 16)
                sp.dma_start(S["kT"], T["KT"][:, :, TP:R]).then_inc(spilled, 16)
                sp.dma_start(S["kiT"], T["KIT"][:, TP:R]).then_inc(spilled, 16)
                sp.dma_start(S["wi"], T["WI"][TP % 128:TP % 128 + TS, NB - 1, :]).then_inc(spilled, 16)
                sp.wait_ge(spilled, 80)

            @block.tensor
            def _(pe):
                for b, (r, n) in enumerate(BLOCKS):
                    if b >= 1:
                        pe.wait_ge(copied, 4 * b)
                    for c in range(4):
                        for k in range(KD):
                            if b == 0 and c == 0:
                                pe.wait_ge(w_loaded[k], 16 * (len(pieces) + 4))
                            last = pe.matmul(PG[0:n, c, 0:NC4], xT[:, k, r:r + n],
                                             W[:, k, NC4 * c:NC4 * c + NC4], start=k == 0, stop=k == KD - 1)
                        last.then_inc(gemm_done, 1)
                    pe.wait_ge(roped, b + 1)
                    if b >= 1:
                        pe.wait_ge(stored, b)
                    for j in range(4):
                        pe.transpose(PT[:, j, 0:n], H[0:n, b % 2, CQ + 128 * j:CQ + 128 * j + 128],
                                     ident[0:n, 0:n])
                        pe.transpose(PT[:, 4 + j, 0:n], H[0:n, b % 2, CQI + 128 * j:CQI + 128 * j + 128],
                                     ident[0:n, 0:n])
                    for j in range(2):
                        pe.transpose(PT[:, 8 + j, 0:n], H[0:n, b % 2, CK + 128 * j:CK + 128 * j + 128],
                                     ident[0:n, 0:n])
                    pe.transpose(PT[:, 10, 0:n], KID[0:n, b % 2, :], ident[0:n, 0:n]).then_inc(turned, 1)

            @block.scalar
            def _(act):
                for b, (r, n) in enumerate(BLOCKS):
                    if b >= 2:
                        act.wait_ge(turned, b - 1)
                        act.wait_ge(written[b % 2], 48 * (b // 2))
                    for c in range(4):
                        act.wait_ge(gemm_done, 4 * b + c + 1)
                        act.activation(H[0:n, b % 2, NC4 * c:NC4 * c + NC4], PG[0:n, c, 0:NC4],
                                       ACT.Copy).then_inc(copied, 1)
                    act.wait_ge(turned, b + 1)
                    act.activation(T["QT"][:, :, r:r + n], PT[:, 0:4, 0:n], ACT.Copy)
                    act.activation(T["QIT"][:, :, r:r + n], PT[:, 4:8, 0:n], ACT.Copy)
                    act.activation(T["KT"][:, :, r:r + n], PT[:, 8:10, 0:n], ACT.Copy)
                    act.activation(T["KIT"][:, r:r + n], PT[:, 10, 0:n], ACT.Copy).then_inc(stored, 1)

            @block.vector
            def _(dve):
                dve.wait_ge(cs_in, 32)
                for b, (r, n) in enumerate(BLOCKS):
                    dve.wait_ge(copied, 4 * b + 4)
                    heads = H[0:n, b % 2, 0:CV].rearrange("p (h d) -> p h d", d=HD)
                    x1, x2 = heads[:, :, 0:8], heads[:, :, 8:16]
                    c, s = (cs[0:n, b, j:j + 1, :].to_broadcast([n, 21, 8]) for j in range(2))
                    dve.tensor_tensor(t[0:n, 0], x1, c, ALU.mult)
                    dve.tensor_tensor(t[0:n, 1], x2, s, ALU.mult)
                    dve.tensor_tensor(t[0:n, 2], x2, c, ALU.mult)
                    dve.tensor_tensor(t[0:n, 3], x1, s, ALU.mult)
                    dve.drain()
                    dve.tensor_tensor(x1, t[0:n, 0], t[0:n, 1], ALU.subtract)
                    dve.tensor_tensor(x2, t[0:n, 2], t[0:n, 3], ALU.add)
                    dve.drain()
                    if b >= 2:
                        dve.wait_ge(turned, b - 1)
                    for j in range(2):
                        dve.tensor_copy(KID[0:n, b % 2, HD * j:HD * j + HD], H[0:n, b % 2, CKI:CKI + HD])
                    dve.tensor_copy(T["V"][0:n, b, :], H[0:n, b % 2, CV:CV + 256])
                    dve.tensor_scalar(T["WI"][0:n, b, :], H[0:n, b % 2, CWI:CWI + 8], 8 ** -0.5 * HD ** -0.5,
                                      None, ALU.mult).then_inc(roped, 1)
                    dve.drain()


def dsa_prompt(nc, T, yaT, ident):
    QB = [(i, min(128, TP - 128 * i), min(128 * (i + 1), TP)) for i in range(-(-TP // 128))]
    chunks = lambda m: [(c, min(512, m - c)) for c in range(0, m, 512)]
    with ExitStack() as sc:
        sc.enter_context(nc.cleanup_on_exit())
        RL = sc.enter_context(nc.sbuf_tensor("dp_RL", [128, 4, 512], F32))
        SCORE = sc.enter_context(nc.sbuf_tensor("dp_SCORE", [128, TP], F32))
        MASK = sc.enter_context(nc.sbuf_tensor("dp_MASK", [128, TP], F32))
        top8 = sc.enter_context(nc.sbuf_tensor("dp_top8", [128, 8], F32))
        P = sc.enter_context(nc.sbuf_tensor("dp_P", [128, 2, TP], F32))
        PTS = sc.enter_context(nc.sbuf_tensor("dp_PTS", [128, 2, 9, 128], F32))
        peak = sc.enter_context(nc.sbuf_tensor("dp_peak", [128, 2], F32))
        npeak = sc.enter_context(nc.sbuf_tensor("dp_npeak", [128, 2], F32))
        den = sc.enter_context(nc.sbuf_tensor("dp_den", [128, 8], F32))
        OROW = sc.enter_context(nc.sbuf_tensor("dp_OROW", [128, 512], F32))
        PI = sc.enter_context(nc.psum_tensor("dp_PI", [128, 2, 512], F32))
        PSC = sc.enter_context(nc.psum_tensor("dp_PSC", [128, 1536], F32))
        PT = sc.enter_context(nc.psum_tensor("dp_PT", [128, 2, 4, 128], F32))
        PO = sc.enter_context(nc.psum_tensor("dp_PO", [128, 512], F32))
        dotted, rectified, weighted, filled, chosen, masked, scored, peaked, expd, tiled, untiled, summed, \
            normed, flipped, stored = (
                nc.alloc_semaphore(name=f"dp_{n}") for n in (
                    "dotted", "rectified", "weighted", "filled", "chosen", "masked", "scored", "peaked",
                    "expd", "tiled", "untiled", "summed", "normed", "flipped", "stored"))
        groups = lambda m: [(t, min(4, -(-m // 128) - t)) for t in range(0, -(-m // 128), 4)]
        with nc.Block() as block:
            @block.tensor
            def _(pe):
                dots = tiles = 0
                for i, n, m in QB:
                    q = 128 * i
                    for c, w in chunks(m):
                        for h in range(8):
                            if dots >= 2:
                                pe.wait_ge(rectified, dots - 1)
                            a = HD * (h % 2)
                            pe.matmul(PI[0:n, dots % 2, 0:w], T["QIT"][a:a + HD, h // 2, q:q + n],
                                      T["KIT"][a:a + HD, c:c + w], start=True, stop=True).then_inc(dotted, 1)
                            dots += 1
                    for h in range(8):
                        u, a, kv = 8 * i + h, HD * (h % 2), h // 4
                        if u >= 1:
                            pe.wait_ge(peaked, u)
                        for c, w in chunks(m):
                            last = pe.matmul(PSC[0:n, c:c + w], T["QT"][a:a + HD, h // 2, q:q + n],
                                             T["KT"][a:a + HD, kv, c:c + w], start=True, stop=True)
                        last.then_inc(scored, 1)
                        pe.wait_ge(expd, u + 1)
                        for t, k in groups(m):
                            if tiles >= 2:
                                pe.wait_ge(untiled, tiles - 1)
                            for j in range(k):
                                w = min(128, m - 128 * (t + j))
                                last = pe.transpose(PT[0:w, tiles % 2, j, 0:n],
                                                    P[0:n, u % 2, 128 * (t + j):128 * (t + j) + w],
                                                    ident[0:n, 0:n])
                            last.then_inc(tiled, 1)
                            tiles += 1
                        pe.wait_ge(untiled, tiles)
                        if h == 0 and i > 0:
                            pe.wait_ge(normed, i)
                        for t in range(-(-m // 128)):
                            w = min(128, m - 128 * t)
                            v = 128 * kv + a
                            last = pe.matmul(PO[0:n, HD * h:HD * h + HD], PTS[0:w, u % 2, t, 0:n],
                                             T["V"][0:w, t, v:v + HD], start=t == 0, stop=128 * t + w == m)
                        last.then_inc(summed, 1)
                    pe.wait_ge(normed, i + 1)
                    if tiles >= 2:
                        pe.wait_ge(untiled, tiles - 1)
                    for j in range(4):
                        last = pe.transpose(PT[:, tiles % 2, j, 0:n], OROW[0:n, 128 * j:128 * j + 128],
                                            ident[0:n, 0:n])
                    last.then_inc(tiled, 1)
                    tiles += 1

            @block.scalar
            def _(act):
                dots = tiles = 0
                for i, n, m in QB:
                    for c, w in chunks(m):
                        for h in range(8):
                            act.wait_ge(dotted, dots + 1)
                            if dots >= 4:
                                act.wait_ge(weighted, dots - 3)
                            act.activation(RL[0:n, dots % 4, 0:w], PI[0:n, dots % 2, 0:w],
                                           ACT.Relu).then_inc(rectified, 1)
                            dots += 1
                    for h in range(8):
                        u = 8 * i + h
                        act.wait_ge(peaked, u + 1)
                        act.activation(P[0:n, u % 2, 0:m], P[0:n, u % 2, 0:m], ACT.Exp,
                                       bias=npeak[0:n, u % 2:u % 2 + 1], scale=HD ** -0.5,
                                       accum_out=den[0:n, h:h + 1])
                        act.drain().then_inc(expd, 1)
                        if u >= 2:
                            act.wait_ge(summed, u - 1)
                        for t, k in groups(m):
                            act.wait_ge(tiled, tiles + 1)
                            full = min(k, (m - 128 * t) // 128)
                            if full:
                                act.activation(PTS[:, u % 2, t:t + full, 0:n], PT[:, tiles % 2, 0:full, 0:n],
                                               ACT.Copy)
                            if full < k:
                                w = m - 128 * (t + full)
                                act.activation(PTS[0:w, u % 2, t + full, 0:n], PT[0:w, tiles % 2, full, 0:n],
                                               ACT.Copy)
                            act.drain().then_inc(untiled, 1)
                            tiles += 1
                    act.wait_ge(tiled, tiles + 1)
                    act.activation(yaT[:, :, 128 * i:128 * i + n], PT[:, tiles % 2, :, 0:n],
                                   ACT.Copy).then_inc(untiled, 1)
                    tiles += 1

            @block.gpsimd
            def _(pool):
                for i, n, m in QB:
                    w = m - 128 * i
                    if m > TOPK:
                        pool.wait_ge(weighted, sum(8 * len(chunks(x)) for _, _, x in QB[:i + 1]))
                        pool.affine_select(SCORE[0:n, 128 * i:m], SCORE[0:n, 128 * i:m], [[-1, w]],
                                           ALU.is_ge, LOW, base=0, channel_multiplier=1).then_inc(filled, 1)
                    pool.wait_ge(chosen, i + 1)
                    pool.affine_select(MASK[0:n, 128 * i:m], MASK[0:n, 128 * i:m], [[-1, w]],
                                       ALU.is_ge, -BIG, base=0, channel_multiplier=1).then_inc(masked, 1)

            @block.vector
            def _(dve):
                dots = fills = 0
                for i, n, m in QB:
                    for c, w in chunks(m):
                        for h in range(8):
                            dve.wait_ge(rectified, dots + 1)
                            rl, wi = RL[0:n, dots % 4, 0:w], T["WI"][0:n, i, h:h + 1]
                            if h == 0:
                                dve.tensor_scalar(SCORE[0:n, c:c + w], rl, wi, None, ALU.mult)
                            else:
                                dve.scalar_tensor_tensor(SCORE[0:n, c:c + w], rl, wi, SCORE[0:n, c:c + w],
                                                         ALU.mult, ALU.add)
                            dve.drain().then_inc(weighted, 1)
                            dots += 1
                    if i > 0:
                        dve.wait_ge(peaked, 8 * i)
                    if m > TOPK:
                        fills += 1
                        dve.wait_ge(filled, fills)
                        with dve.Fori(0, TOPK // 8):
                            dve.max(top8[0:n, :], SCORE[0:n, 0:m])
                            dve.drain()
                            dve.match_replace(SCORE[0:n, 0:m], top8[0:n, :], SCORE[0:n, 0:m], TAKEN)
                            dve.drain()
                        dve.tensor_scalar(MASK[0:n, 0:m], SCORE[0:n, 0:m], TAKEN, -BIG, ALU.not_equal,
                                          ALU.mult)
                    else:
                        dve.memset(MASK[0:n, 0:m], 0.0)
                    dve.drain().then_inc(chosen, 1)
                    dve.wait_ge(masked, i + 1)
                    for h in range(8):
                        u = 8 * i + h
                        dve.wait_ge(scored, u + 1)
                        if u >= 2:
                            dve.wait_ge(summed, u - 1)
                        dve.tensor_tensor_reduce(out=P[0:n, u % 2, 0:m], in0=PSC[0:n, 0:m], in1=MASK[0:n, 0:m],
                                                 scale=1.0, scalar=-3.4e38, op0=ALU.add, op1=ALU.max,
                                                 accum_out=peak[0:n, u % 2:u % 2 + 1])
                        dve.drain()
                        dve.tensor_scalar(npeak[0:n, u % 2:u % 2 + 1], peak[0:n, u % 2:u % 2 + 1],
                                          -HD ** -0.5, None, ALU.mult)
                        dve.drain().then_inc(peaked, 1)
                    dve.wait_ge(summed, 8 * i + 8)
                    dve.reciprocal(den[0:n, :], den[0:n, :])
                    dve.drain()
                    dve.tensor_tensor(OROW[0:n, :].rearrange("p (h d) -> p h d", h=8),
                                      PO[0:n, :].rearrange("p (h d) -> p h d", h=8),
                                      den[0:n, :].rearrange("p (h a) -> p h a", a=1).to_broadcast([n, 8, HD]),
                                      ALU.mult)
                    dve.drain().then_inc(normed, 1)


HALF = (PAST + QS) // 2
NCH = 17


def sample_scores(nc, S, I, SC, ident):
    with ExitStack() as sc:
        sc.enter_context(nc.cleanup_on_exit())
        def sb(name, shape, dt=F32):
            return sc.enter_context(nc.sbuf_tensor(f"ss_{name}", shape, dt))
        KX = sb("KX", [128, 2, 64 * HD])
        KXI = sb("KXI", [128, 64, 2, HD])
        KTC = sb("KTC", [128, 2, 512])
        RL = sb("RL", [128, 2, 512])
        SC16 = sb("SC16", [16, PAST + QS])
        QB = sb("QB", [128, 4, 8, 2, 8])
        WB = sb("WB", [128, 4, 16])
        sel = sb("sel", [128, 16])
        wcol = sb("wcol", [128, 4])
        KIT = sb("KIT", [128, TS])
        pt = sb("pt", [128, 8], I32)
        half = sb("half", [128, 1])
        idx = sb("idx", [128, 8], I32)
        late = sb("late", [128, QS])
        PK = sc.enter_context(nc.psum_tensor("ss_PK", [128, 2, 4, 128], F32))
        PS = sc.enter_context(nc.psum_tensor("ss_PS", [128, 2, 512], F32))
        PW = sc.enter_context(nc.psum_tensor("ss_PW", [16, 2, 512], F32))
        small_in, q_in, zeroed, ready, idx_ready, woven, turned, evacuated, dotted, rectified, weighted, \
            placed, sent, late_done = (
                nc.alloc_semaphore(name=f"ss_{n}") for n in (
                    "small_in", "q_in", "zeroed", "ready", "idx_ready", "woven", "turned", "evacuated",
                    "dotted", "rectified", "weighted", "placed", "sent", "late_done"))
        kx_in = [nc.alloc_semaphore(name=f"ss_kx_in{i}") for i in range(2)]
        with nc.Block() as block:
            @block.sync
            def _(sp):
                for dst, src in ((pt[:, :], I["pt_half"]), (half[:, :], I["half"]), (KIT[:, :], S["kiT"]),
                                 (sel[:, :], I["sel16"]), (late[:, :], I["late"])):
                    sp.dma_start(dst, src).then_inc(small_in, 16)
                wi = S["wi"].rearrange("(p s q) h -> s h q p", s=2, q=8)
                for s in range(2):
                    for h in range(8):
                        sp.dma_start(wcol[16 * h + 8 * s:16 * h + 8 * s + 8, :], wi[s, h],
                                     allow_slow_non_contiguous=True).then_inc(small_in, 16)
                sp.wait_ge(zeroed, 1)
                qi = S["qiT"].rearrange("(g d) j (p s q) -> s g d j p q", g=2, s=2, q=8)
                for s in range(2):
                    for g in range(2):
                        for p in range(4):
                            sp.dma_start(QB[64 * s:64 * s + 64, p, g::2, s, :],
                                         qi[s, g, :, :, p]).then_inc(q_in, 16)
                for p in range(4):
                    sp.wait_ge(placed, NCH * (p + 1))
                    for h in range(2):
                        sp.dma_start(SC[64 * h + 16 * p:64 * h + 16 * p + 16, :],
                                     SC16[:, HALF * h:HALF * h + HALF]).then_inc(sent, 16)
                    sp.wait_ge(sent, 32 * (p + 1))

            @block.gpsimd
            def _(pool):
                pool.memset(QB[:, :], 0.0).then_inc(zeroed, 1)
                pool.wait_ge(idx_ready, 1)
                for b in range(NSEQ):
                    if b >= 2:
                        pool.wait_ge(woven, b - 1)
                    pool.indirect_dma_start(
                        out=KX[:, b % 2, :], out_offset=None, in_=I["cache_kidx"],
                        in_offset=bass.IndirectOffsetOnAxis(ap=idx[:, b:b + 1], axis=0)
                    ).then_inc(kx_in[b % 2], 16)

            @block.scalar
            def _(act):
                def weave(p):
                    for s in range(2):
                        act.wait_ge(kx_in[s], 16 * (p + 1))
                        if p >= 1:
                            act.wait_ge(turned, 16 * p)
                        act.activation(KXI[:, :, s, :], KX[:, s, :].rearrange("p (o d) -> p o d", d=HD),
                                       ACT.Copy).then_inc(woven, 1)

                weave(0)
                for p in range(4):
                    for c in range(NCH):
                        g = NCH * p + c
                        w = 512 if c < 16 else QS
                        act.wait_ge(dotted, g + 1)
                        if g >= 2:
                            act.wait_ge(weighted, g - 1)
                        act.activation(RL[:, g % 2, 0:w], PS[:, g % 2, 0:w], ACT.Relu).then_inc(rectified, 1)
                        if c == 14 and p < 3:
                            weave(p + 1)

            @block.tensor
            def _(pe):
                pe.wait_ge(q_in, 16 * 16)
                pe.wait_ge(ready, 1)
                for g in range(4 * NCH + 2):
                    if g < 4 * NCH and g % NCH < 16:
                        p, c = g // NCH, g % NCH
                        if c == 0:
                            pe.wait_ge(woven, 2 * p + 2)
                        if g >= 2:
                            pe.wait_ge(evacuated, g - 1)
                        for o in range(4):
                            last = pe.transpose(PK[:, g % 2, o, :],
                                                KXI[:, 4 * c + o, :, :].rearrange("p s d -> p (s d)"),
                                                ident[:, :])
                        last.then_inc(turned, 1)
                    if 1 <= g <= 4 * NCH:
                        e = g - 1
                        w = 512 if e % NCH < 16 else QS
                        pe.wait_ge(evacuated, e + 1)
                        if e >= 2:
                            pe.wait_ge(rectified, e - 1)
                        pe.matmul(PS[:, e % 2, 0:w],
                                  QB[:, e // NCH].rearrange("p h s q -> p (h s q)"),
                                  KTC[:, e % 2, 0:w], start=True, stop=True).then_inc(dotted, 1)
                    if g >= 2:
                        e = g - 2
                        w = 512 if e % NCH < 16 else QS
                        pe.wait_ge(rectified, e + 1)
                        if e >= 2:
                            pe.wait_ge(placed, e - 1)
                        pe.matmul(PW[:, e % 2, 0:w], WB[:, e // NCH, :], RL[:, e % 2, 0:w],
                                  start=True, stop=True).then_inc(weighted, 1)

            @block.vector
            def _(dve):
                dve.wait_ge(small_in, 16 * 21)
                dve.tensor_scalar(idx[:, :], pt[:, :], 2.0, half[:, 0:1], ALU.mult, ALU.add)
                dve.drain().then_inc(idx_ready, 1)
                for p in range(4):
                    dve.tensor_scalar(WB[:, p, :], sel[:, :], wcol[:, p:p + 1], None, ALU.mult)
                dve.drain().then_inc(ready, 1)

                def place(e):
                    p, c = e // NCH, e % NCH
                    dve.wait_ge(weighted, e + 1)
                    if c == 0 and p >= 1:
                        dve.wait_ge(sent, 32 * p)
                    if c < 16:
                        dve.tensor_copy(
                            SC16[:, 0:PAST].rearrange("q (l o) -> q o l", o=64)[:, 4 * c:4 * c + 4, :],
                            PW[:, e % 2, :].rearrange("q (o l) -> q o l", o=4)).then_inc(placed, 1)
                    else:
                        dve.tensor_copy(SC16[:, PAST:PAST + QS], PW[:, e % 2, 0:QS]).then_inc(placed, 1)

                for g in range(4 * NCH):
                    p, c = g // NCH, g % NCH
                    if g >= 2:
                        dve.wait_ge(dotted, g - 1)
                    if c < 16:
                        dve.wait_ge(turned, 16 * p + c + 1)
                        dve.tensor_copy(KTC[:, g % 2, :],
                                        PK[:, g % 2].rearrange("p o l -> p (o l)")).then_inc(evacuated, 1)
                    else:
                        for s in range(2):
                            b = 2 * p + s
                            last = dve.tensor_copy(KTC[64 * s:64 * s + 64, g % 2, 0:QS],
                                                   KIT[64 * s:64 * s + 64, 8 * b:8 * b + 8])
                        last.then_inc(evacuated, 1)
                    if g >= 3:
                        place(g - 3)
                for e in range(4 * NCH - 3, 4 * NCH):
                    place(e)
                dve.wait_ge(sent, 128)
                dve.tensor_tensor(SC[64:128, HALF - QS:HALF], SC[64:128, HALF - QS:HALF], late[64:128, :],
                                  ALU.add).then_inc(late_done, 1)


def sample_topk(nc, S, I, SC, PHT, NM, ident):
    with ExitStack() as sc:
        sc.enter_context(nc.cleanup_on_exit())
        def sb(name, shape, dt=F32):
            return sc.enter_context(nc.sbuf_tensor(f"st_{name}", shape, dt))
        v8 = sb("v8", [128, 8])
        i8 = sb("i8", [128, 8], U32)
        VAL = sb("VAL", [128, TOPK])
        IDX = sb("IDX", [128, TOPK])
        VB = sb("VB", [64, TOPK])
        IB = sb("IB", [64, TOPK])
        keep = sb("keep", [64, TOPK])
        key = sb("key", [64, TOPK])
        keyi = sb("keyi", [64, TOPK], I32)
        pgi = sb("pgi", [64, TOPK], I32)
        pg = sb("pg", [64, TOPK])
        hit = sb("hit", [64, 2, TOPK])
        row = sb("row", [64, TOPK])
        pti = sb("pti", [64, NPAGES], I32)
        ptf = sb("ptf", [64, NPAGES])
        cnt = sb("cnt", [64, QS])
        PP = sc.enter_context(nc.psum_tensor("st_PP", [128, 2, 64], F32))
        pt_in, listed, moved, rows_done, turned, done = (
            nc.alloc_semaphore(name=f"st_{n}")
            for n in ("pt_in", "listed", "moved", "rows_done", "turned", "done"))
        with nc.Block() as block:
            @block.sync
            def _(sp):
                sp.dma_start(pti[:, :], I["pt_query"]).then_inc(pt_in, 16)
                sp.wait_ge(listed, 1)
                sp.dma_start(VB[:, :], VAL[64:128, :]).then_inc(moved, 16)
                sp.dma_start(IB[:, :], IDX[64:128, :]).then_inc(moved, 16)
                sp.wait_ge(moved, 32)

            @block.tensor
            def _(pe):
                pe.wait_ge(rows_done, 1)
                for t in range(2):
                    last = pe.transpose(PP[:, t, :], row[:, 128 * t:128 * t + 128], ident[0:64, 0:64])
                last.then_inc(turned, 1)

            @block.vector
            def _(dve):
                with dve.Fori(0, TOPK // 8) as i:
                    dve.max(v8[:, :], SC[:, :])
                    dve.drain()
                    dve.max_index(i8[:, :], v8[:, :], SC[:, :])
                    dve.drain()
                    dve.match_replace(SC[:, :], v8[:, :], SC[:, :], TAKEN)
                    dve.tensor_copy(VAL[:, bass.ds(i * 8, 8)], v8[:, :])
                    dve.tensor_copy(IDX[:, bass.ds(i * 8, 8)], i8[:, :])
                    dve.drain()
                dve.tensor_scalar(IDX[64:128, :], IDX[64:128, :], float(HALF), None, ALU.add)
                dve.drain().then_inc(listed, 1)
                dve.wait_ge(pt_in, 16)
                dve.tensor_copy(ptf[:, :], pti[:, :])
                dve.wait_ge(moved, 32)
                dve.tensor_tensor(keep[:, :], VAL[0:64, :], VB[:, ::-1], ALU.is_ge)
                dve.tensor_tensor(key[:, :], IDX[0:64, :], IB[:, ::-1], ALU.subtract)
                dve.drain()
                dve.tensor_tensor(key[:, :], key[:, :], keep[:, :], ALU.mult)
                dve.drain()
                dve.tensor_tensor(key[:, :], key[:, :], IB[:, ::-1], ALU.add)
                dve.drain()
                dve.tensor_copy(keyi[:, :], key[:, :])
                dve.drain()
                dve.tensor_scalar(pgi[:, :], keyi[:, :], 7, None, ALU.logical_shift_right)
                dve.drain()
                dve.tensor_copy(pg[:, :], pgi[:, :])
                dve.tensor_scalar(NM[:, 0:TOPK], key[:, :], float(PAST), -BIG, ALU.is_ge, ALU.mult)
                dve.drain()
                dve.scalar_tensor_tensor(row[:, :], pg[:, :], -float(PAGE), key[:, :], ALU.mult, ALU.add)
                dve.drain()
                dve.tensor_scalar(ptf[:, :], ptf[:, :], float(PAGE), None, ALU.mult)
                dve.drain()
                for c in range(NPAGES):
                    dve.tensor_scalar(hit[:, c % 2], pg[:, :], float(c), ptf[:, c:c + 1], ALU.is_equal,
                                      ALU.mult)
                    dve.drain()
                    dve.tensor_tensor(row[:, :], row[:, :], hit[:, c % 2], ALU.add)
                dve.drain().then_inc(rows_done, 1)
                for j in range(QS):
                    dve.tensor_scalar(hit[:, j % 2], key[:, :], float(PAST + j), None, ALU.is_equal)
                    dve.drain()
                    dve.reduce_sum(cnt[:, j:j + 1], hit[:, j % 2], AX.X)
                dve.drain()
                dve.tensor_scalar(NM[:, TOPK:TOPK + QS], cnt[:, :], BIG, -BIG, ALU.mult, ALU.add)
                dve.wait_ge(turned, 1)
                dve.tensor_copy(PHT[:, :, :], PP[:, :, :])
                dve.drain().then_inc(done, 1)


def sample_attend(nc, S, I, PHT, NM, ya, v_out, ident):
    NK = TOPK + QS
    with ExitStack() as sc:
        sc.enter_context(nc.cleanup_on_exit())
        def sb(name, shape, dt=F32):
            return sc.enter_context(nc.sbuf_tensor(f"sa_{name}", shape, dt))
        KG = sb("KG", [128, 16, 2, 256])
        VG = sb("VG", [128, 16, 2, 256])
        KGT = sb("KGT", [128, 2, 2, 256])
        QTS = sb("QTS", [128, 4, TS])
        KTS = sb("KTS", [128, 2, TS])
        VN = sb("VN", [QS, NSEQ, 256])
        QF = sb("QF", [128, 2, 2, 64])
        QZ = sb("QZ", [128, 2, 2, 8, 64])
        E8 = sb("E8", [64, NSEQ, 64])
        P = sb("P", [64, 2, NK])
        PTS = sb("PTS", [128, 2, 3, 64])
        st = sb("st", [64, 2, 4])
        YAS = sb("YAS", [128, 4, TS])
        PKT = sc.enter_context(nc.psum_tensor("sa_PKT", [128, 2, 2, 256], F32))
        PSS = sc.enter_context(nc.psum_tensor("sa_PSS", [64, 2, 512], F32))
        PPT = sc.enter_context(nc.psum_tensor("sa_PPT", [128, 2, 4, 128], F32))
        PY = sc.enter_context(nc.psum_tensor("sa_PY", [128, 2, 512], F32))
        small_in, zeroed, q_ready, turned, evacuated, scored, peaked, expd, normed, tiled, untiled, summed, \
            y_done, sent = (
                nc.alloc_semaphore(name=f"sa_{n}") for n in (
                    "small_in", "zeroed", "q_ready", "turned", "evacuated", "scored", "peaked", "expd",
                    "normed", "tiled", "untiled", "summed", "y_done", "sent"))
        k_in = [nc.alloc_semaphore(name=f"sa_k_in{i}") for i in range(4)]
        v_in = [nc.alloc_semaphore(name=f"sa_v_in{i}") for i in range(2)]
        with nc.Block() as block:
            @block.sync
            def _(sp):
                for dst, src in ((QTS[:, :, :], S["qT"]), (KTS[:, :, :], S["kT"]), (E8[:, :, :], I["expand8"]),
                                 (VN[:, :, :], v_out[TP:R, :].rearrange("(b q) c -> q b c", q=QS))):
                    sp.dma_start(dst, src).then_inc(small_in, 16)
                sp.wait_ge(y_done, NSEQ)
                sp.dma_start(ya[:, :, TP:R], YAS[:, :, :]).then_inc(sent, 16)
                sp.wait_ge(sent, 16)

            @block.gpsimd
            def _(pool):
                pool.memset(QF[:, :, :, :], 0.0)
                pool.memset(QZ[:, :, :, :, :], 0.0).then_inc(zeroed, 1)
                for n in range(TS):
                    if n >= 16 and n % 8 == 0:
                        pool.wait_ge(summed, n // 8 - 1)
                    for arrived, G, cache in ((k_in[n // 4 % 4], KG, "cache_k"),
                                              (v_in[n // 8 % 2], VG, "cache_v")):
                        for t in range(2):
                            pool.indirect_dma_start(
                                out=G[:, n % 16, t, :], out_offset=None, in_=I[cache],
                                in_offset=bass.IndirectOffsetOnAxis(ap=PHT[:, t, n:n + 1], axis=0)
                            ).then_inc(arrived, 16)

            @block.tensor
            def _(pe):
                pe.wait_ge(small_in, 64)

                def turn(n):
                    if n % 4 == 0:
                        pe.wait_ge(k_in[n // 4 % 4], 128 * (n // 16 + 1))
                    if n >= 2:
                        pe.wait_ge(evacuated, n - 1)
                    for m in range(2):
                        for t in range(2):
                            last = pe.transpose(PKT[:, n % 2, m, 128 * t:128 * t + 128],
                                                KG[:, n % 16, t, 128 * m:128 * m + 128], ident[:, :])
                    last.then_inc(turned, 1)

                turn(0)
                for b in range(NSEQ):
                    s = b % 2
                    pe.wait_ge(q_ready, b + 1)
                    if b >= 2:
                        pe.wait_ge(peaked, b - 1)
                        pe.wait_ge(expd, b - 1)
                    pe.matmul(PSS[:, s, 0:NK], E8[:, b, :], NM[:, :], start=True, stop=False)
                    for m in range(2):
                        pe.matmul(PSS[:, s, TOPK:NK], QF[:, s, m, :], KTS[:, m, 8 * b:8 * b + 8],
                                  start=False, stop=False)
                    for q in range(8):
                        n = 8 * b + q
                        if n + 1 < TS:
                            turn(n + 1)
                        pe.wait_ge(evacuated, n + 1)
                        for m in range(2):
                            last = pe.matmul(PSS[:, s, 0:TOPK], QZ[:, s, m, q, :], KGT[:, n % 2, m, :],
                                             start=False, stop=q == 7 and m == 1)
                        last.then_inc(scored, 1)
                    pe.wait_ge(normed, b + 1)
                    if b >= 2:
                        pe.wait_ge(untiled, b - 1)
                    for t, w in ((0, 128), (1, 128), (2, QS)):
                        last = pe.transpose(PPT[0:w, s, t, 0:64], P[:, s, 128 * t:128 * t + w],
                                            ident[0:64, 0:64])
                    last.then_inc(tiled, 1)
                    pe.wait_ge(untiled, b + 1)
                    if b >= 2:
                        pe.wait_ge(y_done, b - 1)
                    for m in range(2):
                        pe.matmul(PY[:, s, 64 * m:64 * m + 64], VN[:, b, 128 * m:128 * m + 128],
                                  PTS[0:QS, s, 2, :], start=m == 0, stop=False, skip_group_check=True)
                    pe.wait_ge(v_in[s], 256 * (b // 2 + 1))
                    for q in range(8):
                        n = 8 * b + q
                        for m in range(2):
                            for t in range(2):
                                last = pe.matmul(PY[:, s, 64 * m + 8 * q:64 * m + 8 * q + 8],
                                                 VG[:, n % 16, t, 128 * m:128 * m + 128],
                                                 PTS[:, s, t, 8 * q:8 * q + 8], start=False,
                                                 stop=q == 7 and m == 1 and t == 1, skip_group_check=True)
                    last.then_inc(summed, 1)

            @block.scalar
            def _(act):
                for b in range(NSEQ):
                    s = b % 2
                    for q in range(8):
                        n = 8 * b + q
                        act.wait_ge(turned, n + 1)
                        if n >= 2:
                            act.wait_ge(scored, n - 1)
                        act.activation(KGT[:, n % 2], PKT[:, n % 2], ACT.Copy).then_inc(evacuated, 1)
                    act.wait_ge(peaked, b + 1)
                    if b >= 2:
                        act.wait_ge(tiled, b - 1)
                    act.activation(P[:, s, :], PSS[:, s, 0:NK], ACT.Exp, bias=st[:, s, 1:2],
                                   scale=HD ** -0.5, accum_out=st[:, s, 2:3])
                    act.drain().then_inc(expd, 1)
                    act.wait_ge(tiled, b + 1)
                    if b >= 2:
                        act.wait_ge(summed, b - 1)
                    act.activation(PTS[:, s, 0:2, :], PPT[:, s, 0:2, 0:64], ACT.Copy)
                    act.activation(PTS[0:QS, s, 2, :], PPT[0:QS, s, 2, 0:64], ACT.Copy)
                    act.drain().then_inc(untiled, 1)

            @block.vector
            def _(dve):
                dve.wait_ge(small_in, 64)
                dve.wait_ge(zeroed, 1)

                def queries(b):
                    s = b % 2
                    if b >= 2:
                        dve.wait_ge(scored, 8 * (b - 1))
                    for m in range(2):
                        for g in range(2):
                            for h in range(2):
                                dve.tensor_copy(
                                    QF[64 * h:64 * h + 64, s, m, :].rearrange("p (q c) -> p c q", c=8)[
                                        :, 4 * m + 2 * h + g, :],
                                    QTS[64 * h:64 * h + 64, 2 * m + g, 8 * b:8 * b + 8])
                    dve.drain()
                    for m in range(2):
                        last = dve.tensor_copy(
                            QZ[:, s, m].rearrange("p q c -> p (q c)")[:, 0:504].rearrange(
                                "p (q c) -> p q c", c=72)[:, :, 0:8],
                            QF[:, s, m, 0:56].rearrange("p (q c) -> p q c", c=8))
                        last = dve.tensor_copy(QZ[:, s, m, 7, 56:64], QF[:, s, m, 56:64])
                    dve.drain().then_inc(q_ready, 1)

                queries(0)
                for b in range(NSEQ):
                    s = b % 2
                    if b + 1 < NSEQ:
                        queries(b + 1)
                    dve.wait_ge(scored, 8 * b + 8)
                    dve.reduce_max(st[:, s, 0:1], PSS[:, s, 0:NK], AX.X)
                    dve.drain()
                    dve.tensor_scalar(st[:, s, 1:2], st[:, s, 0:1], -HD ** -0.5, None, ALU.mult)
                    dve.drain().then_inc(peaked, 1)
                    dve.wait_ge(expd, b + 1)
                    dve.reciprocal(st[:, s, 3:4], st[:, s, 2:3])
                    dve.drain()
                    dve.tensor_scalar(P[:, s, :], P[:, s, :], st[:, s, 3:4], None, ALU.mult).then_inc(normed, 1)
                    dve.wait_ge(summed, b + 1)
                    for m in range(2):
                        for h in range(2):
                            y = PY[64 * h:64 * h + 64, s, 64 * m:64 * m + 64].rearrange("p (q c) -> p c q", c=8)
                            dve.tensor_copy(YAS[64 * h:64 * h + 64, 2 * m:2 * m + 2, 8 * b:8 * b + 8],
                                            y[:, 4 * m + 2 * h:4 * m + 2 * h + 2, :])
                    dve.drain().then_inc(y_done, 1)


CH = 64
COLS = [(0, 368), (368, 368), (736, 368)]


def rwkv_project(nc, I, xT, PM, PML, shift_out):
    NT = P_R // 128
    with ExitStack() as sc:
        sc.enter_context(nc.cleanup_on_exit())
        def sb(name, shape, dt=F32):
            return sc.enter_context(nc.sbuf_tensor(f"rp_{name}", shape, dt))
        W = sb("W", [128, 2, KD, 256])
        PX = sb("PX", [128, 2, 1 + TP + NSEQ * 9])
        DF = sb("DF", [128, R])
        mu = sb("mu", [128, NT])
        sh = sb("sh", [128, NT, NSEQ])
        SH = sb("SH", [128, NT, 1 + NSEQ])
        PG = sc.enter_context(nc.psum_tensor("rp_PG", [128, 6, 512], F32))
        w_in = [nc.alloc_semaphore(name=f"rp_w_in{i}") for i in range(2)]
        small_in, zeroed, product, copied, mixed, sent = (
            nc.alloc_semaphore(name=f"rp_{n}")
            for n in ("small_in", "zeroed", "product", "copied", "mixed", "sent"))
        with nc.Block() as block:
            @block.sync
            def _(sp):
                sp.dma_start(mu[:, :], I["mu"]).then_inc(small_in, 16)
                sp.dma_start(sh[:, :, :], I["shift"]).then_inc(small_in, 16)
                for u in range(NT // 2):
                    if u >= 2:
                        sp.wait_ge(product, 6 * (u - 1))
                    sp.dma_start(W[:, u % 2], I["w_in"].rearrange("(k p) n -> p k n", p=128)[
                        :, :, 256 * u:256 * u + 256]).then_inc(w_in[u % 2], 16)
                sp.wait_ge(mixed, NT)
                sp.dma_start(shift_out, SH[:, :, :]).then_inc(sent, 16)
                sp.wait_ge(sent, 16)

            @block.tensor
            def _(pe):
                for t in range(NT):
                    pe.wait_ge(w_in[t // 2 % 2], 16 * (t // 4 + 1))
                    for j, (c, w) in enumerate(COLS):
                        if t >= 2:
                            pe.wait_ge(copied, 3 * (t - 2) + j + 1)
                        for k in range(KD):
                            last = pe.matmul(PG[:, 3 * (t % 2) + j, 0:w],
                                             W[:, t // 2 % 2, k, 128 * (t % 2):128 * (t % 2) + 128],
                                             xT[:, k, c:c + w], start=k == 0, stop=k == KD - 1)
                        last.then_inc(product, 1)

            @block.scalar
            def _(act):
                act.wait_ge(zeroed, 1)
                act.wait_ge(small_in, 32)
                for t in range(NT):
                    if t >= 2:
                        act.wait_ge(mixed, t - 1)
                    px = PX[:, t % 2]
                    seqs = px[:, 1 + TP:].rearrange("p (b q) -> p b q", q=9)
                    act.activation(seqs[:, :, 0], sh[:, t], ACT.Copy)
                    for j, (c, w) in enumerate(COLS):
                        act.wait_ge(product, 3 * t + j + 1)
                        pg = PG[:, 3 * (t % 2) + j]
                        if c + w <= TP:
                            act.activation(px[:, 1 + c:1 + c + w], pg[:, 0:w], ACT.Copy).then_inc(copied, 1)
                        else:
                            act.activation(px[:, 1 + c:1 + TP], pg[:, 0:TP - c], ACT.Copy)
                            act.activation(seqs[:, :, 1:9], pg[:, TP - c:w].rearrange("p (b q) -> p b q", q=8),
                                           ACT.Copy)
                            act.drain().then_inc(copied, 1)

            @block.vector
            def _(dve):
                for i in range(2):
                    dve.memset(PX[:, i, 0:1], 0.0)
                dve.drain().then_inc(zeroed, 1)
                dve.wait_ge(small_in, 32)
                for t in range(NT):
                    px = PX[:, t % 2]
                    pm = PM[:, t] if t < 12 else PML[:, t - 12]
                    seqs = px[:, 1 + TP:].rearrange("p (b q) -> p b q", q=9)
                    dseq = DF[:, TP:R].rearrange("p (b q) -> p b q", q=8)
                    dve.wait_ge(copied, 3 * t + 3)
                    dve.tensor_tensor(DF[:, 0:TP], px[:, 0:TP], px[:, 1:1 + TP], ALU.subtract)
                    dve.tensor_tensor(dseq, seqs[:, :, 0:8], seqs[:, :, 1:9], ALU.subtract)
                    dve.drain()
                    dve.scalar_tensor_tensor(pm[:, 0:TP], DF[:, 0:TP], mu[:, t:t + 1], px[:, 1:1 + TP],
                                             ALU.mult, ALU.add)
                    dve.scalar_tensor_tensor(pm[:, TP:R].rearrange("p (b q) -> p b q", q=8), dseq,
                                             mu[:, t:t + 1], seqs[:, :, 1:9], ALU.mult, ALU.add)
                    dve.tensor_copy(SH[:, t, 0:1], px[:, TP:TP + 1])
                    dve.tensor_copy(SH[:, t, 1:], seqs[:, :, 8])
                    dve.drain().then_inc(mixed, 1)


def rwkv_factors(nc, I, PM, PML, F, PL):
    with ExitStack() as sc:
        sc.enter_context(nc.cleanup_on_exit())
        def sb(name, shape, dt=F32):
            return sc.enter_context(nc.sbuf_tensor(f"rf_{name}", shape, dt))
        vec = sb("vec", [128, 6, 4])
        wa2 = sb("wa2", [128, 512])
        g2 = sb("g2", [128, 512])
        keep = sb("keep", [128, R])
        ones = sb("ones", [128, 128])
        t1, t2, t3, E = (sb(f"t{i}", [128, R]) for i in range(4))
        PA = sc.enter_context(nc.psum_tensor("rf_PA", [128, 3, 512], F32))
        PB = sc.enter_context(nc.psum_tensor("rf_PB", [128, 3, 512], F32))
        small_in, squashed, w_done, w_read, a_done, a_read, g_done, g_read, squared, sq_done, rooted, \
            summed_log, exps, factored, root_done = (
                nc.alloc_semaphore(name=f"rf_{n}") for n in (
                    "small_in", "squashed", "w_done", "w_read", "a_done", "a_read", "g_done", "g_read",
                    "squared", "sq_done", "rooted", "summed_log", "exps", "factored", "root_done"))
        with nc.Block() as block:
            @block.sync
            def _(sp):
                for dst, src in ((vec[:, 0:4, :], I["rvec"][:, 0:4, :]), (vec[:, 5, :], I["rvec"][:, 4, :]),
                                 (wa2[0:64, :], I["w_w2"]), (wa2[64:128, :], I["w_a2"]), (g2[:, :], I["w_g2"]),
                                 (keep[:, :], I["keep"]), (ones[:, :], I["ones_pair"])):
                    sp.dma_start(dst, src).then_inc(small_in, 16)

            def product(pe, out, lhsT, rhs):
                for j, (c, w) in enumerate(COLS):
                    last = pe.matmul(out[:, j, 0:w], lhsT, rhs[:, c:c + w], start=True, stop=True)
                return last

            @block.tensor
            def _(pe):
                pe.wait_ge(small_in, 16 * 7)
                pe.wait_ge(squashed, 1)
                for c in range(4):
                    ch = slice(128 * c, 128 * c + 128)
                    if c >= 1:
                        pe.wait_ge(g_read, c)
                    product(pe, PA, wa2[0:64, ch], PML[0:64, 0]).then_inc(w_done, 1)
                    if c >= 1:
                        pe.wait_ge(rooted, c)
                    product(pe, PB, wa2[64:128, ch], PML[64:128, 0]).then_inc(a_done, 1)
                    pe.wait_ge(w_read, c + 1)
                    product(pe, PA, g2[:, ch], PML[:, 1]).then_inc(g_done, 1)
                    pe.wait_ge(a_read, c + 1)
                    pe.wait_ge(squared, c + 1)
                    product(pe, PB, ones[:, :], t1).then_inc(sq_done, 1)

            def evac(act, out, ps, func, bias=0.0, scale=1.0):
                for j, (c, w) in enumerate(COLS):
                    last = act.activation(out[:, c:c + w], ps[:, j, 0:w], func, bias=bias, scale=scale)
                return last

            @block.scalar
            def _(act):
                act.wait_ge(small_in, 16 * 7)
                act.activation(PML[0:64, 0, :], PML[0:64, 0, :], ACT.Tanh)
                act.activation(PML[:, 1, :], PML[:, 1, :], ACT.Sigmoid)
                act.drain().then_inc(squashed, 1)
                for c in range(4):
                    act.wait_ge(w_done, c + 1)
                    if c >= 1:
                        act.wait_ge(factored, c)
                    evac(act, E, PA, ACT.Sigmoid, bias=vec[:, 0, c:c + 1]).then_inc(w_read, 1)
                    act.wait_ge(a_done, c + 1)
                    evac(act, F["B"][:, c], PB, ACT.Sigmoid, bias=vec[:, 1, c:c + 1]).then_inc(a_read, 1)
                    act.activation(t1[:, :], PM[:, 4 + c, :], ACT.Square,
                                   scale=vec[:, 2, c:c + 1]).then_inc(squared, 1)
                    act.wait_ge(g_done, c + 1)
                    evac(act, F["G"][:, c], PA, ACT.Copy).then_inc(g_read, 1)
                    act.wait_ge(rooted, c + 1)
                    act.activation(t1[:, :], t1[:, :], ACT.Sqrt).then_inc(root_done, 1)
                    act.wait_ge(summed_log, c + 1)
                    act.activation(E[:, :], t2[:, :], ACT.Exp)
                    act.activation(t2[:, :], t2[:, :], ACT.Exp, scale=-1.0)
                    act.activation(t3[:, :], t3[:, :], ACT.Exp)
                    act.drain().then_inc(exps, 1)

            @block.vector
            def _(dve):
                dve.wait_ge(small_in, 16 * 7)
                dve.tensor_scalar(vec[:, 4, :], vec[:, 3, :], -1.0, 1.0, ALU.mult, ALU.add)
                dve.drain()
                for c in range(4):
                    r, k, B, A = PM[:, c], PM[:, 4 + c], F["B"][:, c], F["A"][:, c]
                    dve.wait_ge(sq_done, c + 1)
                    for j, (s, w) in enumerate(COLS):
                        dve.tensor_scalar(t1[:, s:s + w], PB[:, j, 0:w], 1e-24, None, ALU.max)
                    dve.drain().then_inc(rooted, 1)
                    dve.wait_ge(squared, c + 1)
                    dve.tensor_scalar(A, k, vec[:, 2, c:c + 1], None, ALU.mult)
                    dve.wait_ge(w_read, c + 1)
                    dve.tensor_scalar(E[:, :], E[:, :], -float(2.718281828459045 ** -0.5), None, ALU.mult)
                    dve.drain()
                    dve.tensor_tensor_scan(t2[:, :], keep[:, :], E[:, :], 0.0, ALU.mult, ALU.add)
                    dve.drain()
                    dve.tensor_tensor(t3[:, :], t2[:, :], E[:, :], ALU.subtract)
                    dve.drain().then_inc(summed_log, 1)
                    dve.wait_ge(root_done, c + 1)
                    dve.reciprocal(t1[:, :], t1[:, :])
                    dve.wait_ge(a_read, c + 1)
                    kf = F["RKK"][:, c]
                    dve.tensor_scalar(kf, B, vec[:, 3, c:c + 1], vec[:, 4, c:c + 1], ALU.mult, ALU.add)
                    dve.drain()
                    dve.tensor_tensor(A, A, t1[:, :], ALU.mult)
                    dve.tensor_tensor(k, k, kf, ALU.mult)
                    dve.drain()
                    dve.tensor_tensor(B, B, A, ALU.mult)
                    dve.scalar_tensor_tensor(kf, r, vec[:, 5, c:c + 1], k, ALU.mult, ALU.mult)
                    dve.drain()
                    dve.wait_ge(exps, c + 1)
                    dve.scalar_tensor_tensor(A, A, -1.0, t3[:, :], ALU.mult, ALU.mult)
                    dve.tensor_tensor(B, B, t2[:, :], ALU.mult)
                    dve.tensor_tensor(k, k, t2[:, :], ALU.mult)
                    dve.tensor_tensor(r, r, E[:, :], ALU.mult)
                    dve.tensor_copy(PL[:, c, 0:16], E[:, CH - 1:SEQ:CH])
                    dve.tensor_copy(PL[:, c, 16:17], E[:, TP - 1:TP])
                    dve.tensor_copy(PL[:, c, 17:25], E[:, TP + QS - 1:R:QS])
                    dve.drain().then_inc(factored, 1)


def rwkv_chunks(nc, I, PM, F, PL, s_out, ss_out, ident):
    with ExitStack() as sc:
        sc.enter_context(nc.cleanup_on_exit())
        def sb(name, shape, dt=F32):
            return sc.enter_context(nc.sbuf_tensor(f"rc_{name}", shape, dt))
        EX = sb("EX", [128, 2, 6, 4, 2, CH])
        masks = sb("masks", [128, 14, 128])
        Mlo, Z, ZT, Q, NTm, RKm, RBm, brow, krow = (sb(n, [128, 4, 128]) for n in (
            "Mlo", "Z", "ZT", "Q", "NTm", "RKm", "RBm", "brow", "krow"))
        V, W1, U, Y, Y2 = (sb(n, [128, 4, CH]) for n in ("V", "W1", "U", "Y", "Y2"))
        YE = sb("YE", [128, 4, 2, CH])
        ST = sb("ST", [128, 4, CH])
        SS = sb("SS", [128, 4, NSEQ, CH])
        big = sb("big", [128, NSEQ, CH])
        big2 = sb("big2", [128, NSEQ, CH])
        seqm = sb("seqm", [128, NSEQ])
        lng, lnb = sb("lng", [128, 4, CH]), sb("lnb", [128, 4, CH])
        mhalf = sb("mhalf", [128, 4])
        stat = sb("stat", [128, 4, 4])
        stack = sb("stack", [128, CH])
        ones = sb("ones", [128, 1])
        P0, P1, P2, P3, P4, P5, P6, P7 = (
            sc.enter_context(nc.psum_tensor(f"rc_P{i}", [128, 512], F32)) for i in range(8))
        names = ("small_in", "started", "expanded", "gram_m", "gram_r", "rows", "rows_read", "z_ready",
                 "masked", "q_done", "q_read", "zq_done", "zq_read", "w1_done", "w1_read", "u_done",
                 "u_read", "y_done", "y_read", "s_done", "s_read", "var_done", "rstd_done", "ye_done",
                 "yt_done", "yt_read", "picked", "big_done", "big_read", "spread", "sent", "bonus_read")
        (small_in, started, expanded, gram_m, gram_r, rows, rows_read, z_ready, masked, q_done, q_read,
         zq_done, zq_read, w1_done, w1_read, u_done, u_read, y_done, y_read, s_done, s_read, var_done,
         rstd_done, ye_done, yt_done, yt_read, picked, big_done, big_read, spread, sent, bonus_read) = (
            nc.alloc_semaphore(name=f"rc_{n}") for n in names)
        MU, ML, MI, M1, M1T, MID, MQ, SMU = 0, 1, 2, 3, 4, 5, 6, 11
        pair = lambda P: P[:, :].rearrange("p (c n) -> p c n", c=4)
        half = lambda P: P[:, 0:4 * CH].rearrange("p (c n) -> p c n", c=4)
        SAMPLE = 17
        NCK = 18
        levels = lambda c: 2 if c == SAMPLE else 5
        before = lambda c: sum(levels(x) for x in range(c))
        row0 = lambda c: TP if c == SAMPLE else CH * c
        width = lambda c: 16 if c == 16 else CH

        with nc.Block() as block:
            @block.sync
            def _(sp):
                for dst, src in ((masks[:, :, :], I["masks"]), (SS[:, :, :, :], I["state"]),
                                 (seqm[:, :], I["seqm"]), (lng[:, :, :], I["lng"]), (lnb[:, :, :], I["lnb"]),
                                 (stack[:, :], I["stack"])):
                    sp.dma_start(dst, src).then_inc(small_in, 16)
                sp.wait_ge(s_read, 17)
                sp.dma_start(s_out, ST[:, :, :]).then_inc(sent, 16)
                sp.wait_ge(s_read, 18)
                sp.dma_start(ss_out, SS[:, :, :, :]).then_inc(sent, 16)
                sp.wait_ge(sent, 32)

            @block.gpsimd
            def _(pool):
                pool.memset(EX[:, :], 0.0)
                pool.memset(YE[:, :], 0.0)
                pool.memset(ST[:, :], 0.0)
                pool.memset(ones[:, :], 1.0)
                pool.memset(mhalf[:, :], -0.5)
                pool.drain().then_inc(started, 1)

                def expand(c):
                    if c >= 2:
                        pool.wait_ge(s_done, c - 1)
                        pool.wait_ge(y_done, c - 1)
                    if width(c) < CH:
                        pool.memset(EX[:, c % 2], 0.0)
                        pool.drain()
                    r, w = row0(c), width(c)
                    for h in range(2):
                        for o, src in enumerate((F["A"], F["B"], PM[:, 4:8], PM[:, 0:4], PM[:, 8:12],
                                                 F["RKK"])):
                            pool.tensor_copy(EX[64 * h:64 * h + 64, c % 2, o, :, h, 0:w],
                                             src[64 * h:64 * h + 64, :, r:r + w])
                        last = pool.drain()
                    last.then_inc(expanded, 1)

                expand(0)
                for c in range(NCK):
                    if c + 1 < NCK:
                        expand(c + 1)
                    pool.wait_ge(var_done, c + 1)
                    pool.tensor_tensor(stat[:, 2, :], stat[:, 1, :], mhalf[:, :], ALU.pow)
                    pool.drain().then_inc(rstd_done, 1)

            @block.tensor
            def _(pe):
                pe.wait_ge(small_in, 16 * 6)
                pe.wait_ge(started, 1)
                for c in range(NCK):
                    al, be, ka, rh, vv, rk = (EX[:, c % 2, o].rearrange("p c h n -> p c (h n)") for o in range(6))

                    def each(out, lhsT, rhs, n=128):
                        for p in range(4):
                            last = pe.matmul(out[:, n * p:n * p + n], lhsT[:, p], rhs[:, p], start=True, stop=True)
                        return last

                    pe.wait_ge(expanded, c + 1)
                    each(P0, be, al)
                    each(P1, al, be).then_inc(gram_m, 1)
                    each(P2, ka, al)
                    each(P3, ka, rh)
                    if c >= 1:
                        pe.wait_ge(masked, c)
                    each(P4, be, rh).then_inc(gram_r, 1)
                    if c >= 1:
                        pe.wait_ge(yt_read, c)
                        pe.wait_ge(y_read, c)
                        pe.wait_ge(s_read, c)
                    for p in range(4):
                        pe.transpose(P5[:, 128 * p:128 * p + 128], be[:, p], ident[:, :])
                        pe.transpose(P6[:, 128 * p:128 * p + 128], ka[:, p], ident[:, :])
                    for p in range(4):
                        pe.matmul(P7[:, CH * p:CH * p + CH], vv[:, p], stack[:, :], start=True, stop=True)
                        last = pe.matmul(P7[:, 256 + p:257 + p], rk[:, p], ones[:, :], start=True, stop=True)
                    last.then_inc(rows, 1)
                    pe.wait_ge(masked, c + 1)
                    pe.wait_ge(rows_read, c + 1)
                    for l in range(levels(c)):
                        n = before(c) + l
                        pe.wait_ge(z_ready, c + 1)
                        if l:
                            pe.wait_ge(zq_read, n)
                        each(P0, Mlo, Z).then_inc(q_done, 1)
                        pe.wait_ge(q_read, n + 1)
                        last = each(P1, ZT, Q)
                        if l < levels(c) - 1:
                            last = each(P2, Q, ZT)
                        last.then_inc(zq_done, 1)
                    n = before(c + 1)
                    if c < SAMPLE:
                        for p in range(4):
                            pe.matmul(P5[:, CH * p:CH * p + CH], al[:, p], ST[:, p], start=True, stop=False)
                            last = pe.matmul(P5[:, CH * p:CH * p + CH], NTm[:, p], V[:, p], start=False, stop=True)
                        last.then_inc(w1_done, 1)
                    else:
                        each(P5, NTm, V, CH).then_inc(w1_done, 1)
                        for j, x in enumerate((al, rh)):
                            for p in range(4):
                                i = 4 * j + p
                                if i >= 1:
                                    pe.wait_ge(big_read, i)
                                pe.matmul(P4[:, :], x[:, p], SS[:, p].rearrange("k b v -> k (b v)"),
                                          start=True, stop=True).then_inc(big_done, 1)
                    pe.wait_ge(w1_read, c + 1)
                    pe.wait_ge(zq_read, n)
                    each(P6, Z, W1, CH).then_inc(u_done, 1)
                    pe.wait_ge(u_read, c + 1)
                    for p in range(4):
                        o = slice(CH * p, CH * p + CH)
                        if c < SAMPLE:
                            pe.matmul(P7[:, o], rh[:, p], ST[:, p], start=True, stop=False)
                        pe.matmul(P7[:, o], RBm[:, p], U[:, p], start=c == SAMPLE, stop=False)
                        last = pe.matmul(P7[:, o], RKm[:, p], V[:, p], start=False, stop=True)
                    last.then_inc(y_done, 1)
                    if c < SAMPLE:
                        for p in range(4):
                            o = slice(CH * p, CH * p + CH)
                            pe.matmul(P6[:, o], brow[:, p], U[:, p], start=True, stop=False)
                            last = pe.matmul(P6[:, o], krow[:, p], V[:, p], start=False, stop=True)
                        last.then_inc(s_done, 1)
                    else:
                        for p in range(4):
                            pe.wait_ge(spread, p + 1)
                            pe.matmul(P6[:, :], brow[:, p], big[:, :].rearrange("k b v -> k (b v)"),
                                      start=True, stop=False)
                            last = pe.matmul(P6[:, :], krow[:, p], big2[:, :].rearrange("k b v -> k (b v)"),
                                             start=False, stop=True)
                            last.then_inc(s_done, 1)
                    pe.wait_ge(ye_done, c + 1)
                    for p in range(4):
                        last = pe.matmul(P5[:, CH * p:CH * p + CH], YE[:, p].rearrange("t h v -> t (h v)"),
                                         stack[:, :], start=True, stop=True)
                    last.then_inc(yt_done, 1)

            @block.scalar
            def _(act):
                for c in range(NCK):
                    act.wait_ge(rows, c + 1)
                    act.activation(brow[:, :, :], pair(P5), ACT.Copy)
                    act.activation(krow[:, :, :], pair(P6), ACT.Copy)
                    if c >= 1:
                        act.wait_ge(ye_done, c)
                    act.activation(V[:, :, :], half(P7), ACT.Copy)
                    act.activation(stat[:, 3, :], P7[:, 256:260], ACT.Copy)
                    act.drain().then_inc(rows_read, 1)
                    if c < SAMPLE:
                        act.wait_ge(w1_done, c + 1)
                        act.activation(W1[:, :, :], half(P5), ACT.Copy).then_inc(w1_read, 1)
                    act.wait_ge(u_done, c + 1)
                    act.activation(U[:, :, :], half(P6), ACT.Copy).then_inc(u_read, 1)

            @block.vector
            def _(dve):
                dve.wait_ge(small_in, 16 * 6)
                dve.wait_ge(started, 1)
                mask = lambda i: masks[:, i:i + 1, :].to_broadcast([128, 4, 128])
                wide = lambda t, i: t[:, i].rearrange("p (c a) -> p c a", a=1).to_broadcast([128, 4, CH])
                for c in range(NCK):
                    mu, ml, mi = (SMU, SMU + 1, SMU + 2) if c == SAMPLE else (MU, ML, MI)
                    dve.wait_ge(gram_m, c + 1)
                    dve.tensor_tensor(Z[:, :, :], pair(P0), mask(M1), ALU.mult)
                    dve.tensor_tensor(ZT[:, :, :], pair(P1), mask(M1T), ALU.mult)
                    dve.tensor_tensor(Mlo[:, :, :], pair(P1), mask(ml), ALU.mult)
                    dve.drain()
                    dve.tensor_tensor(Z[:, :, :], Z[:, :, :], mask(MID), ALU.add)
                    dve.tensor_tensor(ZT[:, :, :], ZT[:, :, :], mask(MID), ALU.add)
                    dve.drain().then_inc(z_ready, 1)
                    dve.wait_ge(gram_r, c + 1)
                    dve.tensor_tensor(NTm[:, :, :], pair(P2), mask(mu), ALU.mult)
                    dve.tensor_tensor(RKm[:, :, :], pair(P3), mask(mi), ALU.mult)
                    dve.tensor_tensor(RBm[:, :, :], pair(P4), mask(mi), ALU.mult)
                    dve.drain().then_inc(masked, 1)
                    for l in range(levels(c)):
                        n = before(c) + l
                        dve.wait_ge(q_done, n + 1)
                        dve.tensor_tensor(Q[:, :, :], pair(P0), mask(MQ + l), ALU.mult)
                        dve.drain().then_inc(q_read, 1)
                        dve.wait_ge(zq_done, n + 1)
                        dve.tensor_tensor(Z[:, :, :], Z[:, :, :], pair(P1), ALU.add)
                        if l < levels(c) - 1:
                            dve.tensor_tensor(ZT[:, :, :], ZT[:, :, :], pair(P2), ALU.add)
                        dve.drain().then_inc(zq_read, 1)
                    if c == SAMPLE:
                        own = seqm[:, :].rearrange("p (b a) -> p b a", a=1).to_broadcast([128, NSEQ, CH])
                        dve.wait_ge(w1_done, c + 1)
                        for i in range(8):
                            j, p = i // 4, i % 4
                            dve.wait_ge(big_done, i + 1)
                            dve.tensor_tensor(big[:, :, :], P4[:, :].rearrange("p (b v) -> p b v", b=8), own,
                                              ALU.mult)
                            dve.drain().then_inc(big_read, 1)
                            dve.tensor_reduce((W1, Y2)[j][:, p], big[:, :, :].rearrange("p b v -> p v b"),
                                              AX.X, ALU.add)
                            dve.drain()
                        dve.tensor_tensor(W1[:, :, :], W1[:, :, :], half(P5), ALU.add)
                        dve.drain().then_inc(w1_read, 1)
                    dve.wait_ge(y_done, c + 1)
                    if c == SAMPLE:
                        dve.tensor_tensor(Y[:, :, :], Y2[:, :, :], half(P7), ALU.add)
                    else:
                        dve.tensor_copy(Y[:, :, :], half(P7))
                    dve.drain().then_inc(y_read, 1)
                    if c < SAMPLE:
                        dve.wait_ge(s_done, c + 1)
                        dve.tensor_tensor(ST[:, :, :], ST[:, :, :], half(P6), ALU.add)
                        dve.drain()
                        dve.tensor_tensor(ST[:, :, :], ST[:, :, :],
                                          PL[:, :, c:c + 1].to_broadcast([128, 4, CH]), ALU.mult)
                        dve.drain().then_inc(s_read, 1)
                    else:
                        for p in range(4):
                            if p:
                                dve.wait_ge(s_done, SAMPLE + p)
                            for dst, src in ((big, U), (big2, V)):
                                dve.tensor_tensor(dst[:, :, :], src[:, p:p + 1, :].to_broadcast([128, NSEQ, CH]),
                                                  own, ALU.mult)
                            dve.drain().then_inc(spread, 1)
                            dve.wait_ge(s_done, SAMPLE + p + 1)
                            dve.tensor_tensor(SS[:, p], SS[:, p], P6[:, :].rearrange("p (b v) -> p b v", b=8),
                                              ALU.add)
                            dve.drain()
                            dve.tensor_tensor(SS[:, p], SS[:, p],
                                              PL[:, p, 17:25].rearrange("p (b a) -> p b a", a=1)
                                              .to_broadcast([128, NSEQ, CH]), ALU.mult)
                            last = dve.drain()
                        last.then_inc(s_read, 1)
                    dve.reduce_sum(stat[:, 0, :], Y[:, :, :], AX.X)
                    dve.drain()
                    dve.tensor_scalar(stat[:, 0, :], stat[:, 0, :], -1.0 / CH, None, ALU.mult)
                    dve.drain()
                    dve.tensor_tensor(Y[:, :, :], Y[:, :, :], wide(stat, 0), ALU.add)
                    dve.drain()
                    dve.tensor_tensor(Y2[:, :, :], Y[:, :, :], Y[:, :, :], ALU.mult)
                    dve.drain()
                    dve.reduce_sum(stat[:, 1, :], Y2[:, :, :], AX.X)
                    dve.drain()
                    dve.tensor_scalar(stat[:, 1, :], stat[:, 1, :], 1.0 / CH, 64e-5, ALU.mult, ALU.add)
                    dve.drain().then_inc(var_done, 1)
                    dve.tensor_tensor(Y[:, :, :], Y[:, :, :], lng[:, :, :], ALU.mult)
                    dve.tensor_tensor(Y2[:, :, :], V[:, :, :], wide(stat, 3), ALU.mult)
                    dve.drain()
                    dve.tensor_tensor(Y2[:, :, :], Y2[:, :, :], lnb[:, :, :], ALU.add)
                    dve.wait_ge(rstd_done, c + 1)
                    dve.tensor_tensor(Y[:, :, :], Y[:, :, :], wide(stat, 2), ALU.mult)
                    dve.drain()
                    for h in range(2):
                        s = slice(64 * h, 64 * h + 64)
                        dve.tensor_tensor(YE[s, :, h, :], Y[s, :, :], Y2[s, :, :], ALU.add)
                    dve.drain().then_inc(ye_done, 1)
                    dve.wait_ge(yt_done, c + 1)
                    r, w = row0(c), width(c)
                    dve.tensor_tensor(F["G"][:, :, r:r + w], half(P5)[:, :, 0:w], F["G"][:, :, r:r + w], ALU.mult)
                    dve.drain().then_inc(yt_read, 1)


def merge(nc, I, xT, yr_dram, ya_dram, x1):
    with ExitStack() as sc:
        sc.enter_context(nc.cleanup_on_exit())
        def sb(name, shape, dt=F32):
            return sc.enter_context(nc.sbuf_tensor(f"mg_{name}", shape, dt))
        WG = sb("WG", [128, 2, KD, 2, 128])
        WB = sb("WB", [128, 2, 4, D])
        WO = sb("WO", [128, KD, D])
        YT = sb("YT", [128, 2, 4, R])
        MT = sb("MT", [128, KD, R])
        G = sb("G", [128, 2, R])
        X = sb("X", [128, 2, D])
        PG = sc.enter_context(nc.psum_tensor("mg_PG", [128, 3, 512], F32))
        PB = sc.enter_context(nc.psum_tensor("mg_PB", [128, 3, 512], F32))
        PO = sc.enter_context(nc.psum_tensor("mg_PO", [128, 2, 512], F32))
        wg_in = [nc.alloc_semaphore(name=f"mg_wg_in{i}") for i in range(2)]
        x_in = [nc.alloc_semaphore(name=f"mg_x_in{i}") for i in range(2)]
        x_out = [nc.alloc_semaphore(name=f"mg_x_out{i}") for i in range(2)]
        branch_in, wo_in, gated, gate_read, branched, branch_read, projected, added = (
            nc.alloc_semaphore(name=f"mg_{n}") for n in (
                "branch_in", "wo_in", "gated", "gate_read", "branched", "branch_read", "projected", "added"))
        with nc.Block() as block:
            @block.sync
            def _(sp):
                g0 = P_R + P_A
                wv = I["w_in"].rearrange("(k p) n -> p k n", p=128)
                for t in range(KD):
                    if t >= 2:
                        sp.wait_ge(branched, 2 * (t - 1))
                    for j in range(2):
                        c = g0 + D * j + 128 * t
                        sp.dma_start(WG[:, t % 2, :, j, :], wv[:, :, c:c + 128]).then_inc(wg_in[t % 2], 16)
                    if t == 0:
                        sp.dma_start(YT[:, 0], yr_dram).then_inc(branch_in, 16)
                        sp.dma_start(WB[:, 0], I["w_br_rwkv"].rearrange("(k p) n -> p k n", p=128)
                                     ).then_inc(branch_in, 16)
                        sp.dma_start(YT[:, 1], ya_dram).then_inc(branch_in, 16)
                        wa = I["w_br_attn"].rearrange("(m h g d) n -> h d m g n", m=2, h=2, g=2)
                        for h in range(2):
                            for m in range(2):
                                sp.dma_start(WB[64 * h:64 * h + 64, 1, 2 * m:2 * m + 2, :],
                                             wa[h, :, m]).then_inc(branch_in, 16)
                    if t == 1:
                        sp.dma_start(WO[:, :, :], I["w_out"].rearrange("(k p) n -> p k n", p=128)
                                     ).then_inc(wo_in, 16)
                for b, (r, n) in enumerate(BLOCKS):
                    if b >= 2:
                        sp.wait_ge(x_out[b % 2], 16 * (b // 2))
                    sp.dma_start(X[0:n, b % 2, :], I["x"][r:r + n, :]).then_inc(x_in[b % 2], 16)
                    if b >= 1:
                        q, m = BLOCKS[b - 1]
                        sp.wait_ge(x_in[(b - 1) % 2], 16 * ((b + 1) // 2))
                        sp.wait_ge(added, b)
                        sp.dma_start(x1[q:q + m, :], X[0:m, (b - 1) % 2, :]).then_inc(x_out[(b - 1) % 2], 16)
                q, m = BLOCKS[NB - 1]
                sp.wait_ge(x_in[(NB - 1) % 2], 16 * ((NB + 1) // 2))
                sp.wait_ge(added, NB)
                sp.dma_start(x1[q:q + m, :], X[0:m, (NB - 1) % 2, :]).then_inc(x_out[(NB - 1) % 2], 16)
                for i in range(2):
                    sp.wait_ge(x_out[i], 16 * ((NB + 1 - i) // 2))

            @block.tensor
            def _(pe):
                for t in range(KD):
                    pe.wait_ge(wg_in[t % 2], 32 * (t // 2 + 1))
                    for j in range(2):
                        u = 2 * t + j
                        if u >= 1:
                            pe.wait_ge(gate_read, u)
                        for i, (c, w) in enumerate(COLS):
                            for k in range(KD):
                                last = pe.matmul(PG[:, i, 0:w], WG[:, t % 2, k, j, :], xT[:, k, c:c + w],
                                                 start=k == 0, stop=k == KD - 1)
                        last.then_inc(gated, 1)
                        if u == 0:
                            pe.wait_ge(branch_in, 16 * 7)
                        if u >= 1:
                            pe.wait_ge(branch_read, u)
                        for i, (c, w) in enumerate(COLS):
                            for k in range(4):
                                last = pe.matmul(PB[:, i, 0:w], WB[:, j, k, 128 * t:128 * t + 128],
                                                 YT[:, j, k, c:c + w], start=k == 0, stop=k == 3)
                        last.then_inc(branched, 1)
                pe.wait_ge(wo_in, 16)
                pe.wait_ge(branch_read, 2 * KD)
                for b, (r, n) in enumerate(BLOCKS):
                    if b >= 1:
                        pe.wait_ge(added, b)
                    for j in range(2):
                        for k in range(KD):
                            last = pe.matmul(PO[0:n, j, :], MT[:, k, r:r + n], WO[:, k, 512 * j:512 * j + 512],
                                             start=k == 0, stop=k == KD - 1)
                    last.then_inc(projected, 1)

            @block.scalar
            def _(act):
                for u in range(2 * KD):
                    act.wait_ge(gated, u + 1)
                    if u >= 2:
                        act.wait_ge(branch_read, u - 1)
                    for i, (c, w) in enumerate(COLS):
                        last = act.activation(G[:, u % 2, c:c + w], PG[:, i, 0:w], ACT.Sigmoid)
                    last.then_inc(gate_read, 1)

            @block.vector
            def _(dve):
                for u in range(2 * KD):
                    t, j = u // 2, u % 2
                    dve.wait_ge(gate_read, u + 1)
                    dve.wait_ge(branched, u + 1)
                    for i, (c, w) in enumerate(COLS):
                        out = (MT[:, t, c:c + w], G[:, 1, c:c + w])[j]
                        dve.tensor_tensor(out, G[:, j, c:c + w], PB[:, i, 0:w], ALU.mult)
                    dve.drain()
                    if j:
                        dve.tensor_tensor(MT[:, t, :], MT[:, t, :], G[:, 1, :], ALU.add)
                        dve.drain()
                    dve.drain().then_inc(branch_read, 1)
                for b, (r, n) in enumerate(BLOCKS):
                    dve.wait_ge(x_in[b % 2], 16 * (b // 2 + 1))
                    dve.wait_ge(projected, b + 1)
                    dve.tensor_tensor(X[0:n, b % 2, :].rearrange("p (j c) -> p j c", j=2),
                                      X[0:n, b % 2, :].rearrange("p (j c) -> p j c", j=2), PO[0:n],
                                      ALU.add).then_inc(added, 1)


NF = DFF // 128


def ffn_up(nc, I, xT, HT, conv_out):
    with ExitStack() as sc:
        sc.enter_context(nc.cleanup_on_exit())
        def sb(name, shape, dt=F32):
            return sc.enter_context(nc.sbuf_tensor(f"fu_{name}", shape, dt))
        W = sb("W", [128, 2, KD, 2, 128])
        AX = sb("AX", [128, 2, 2 + TP + NSEQ * 10])
        C = sb("C", [128, 2, R])
        cw = sb("cw", [128, 4, NF])
        cst = sb("cst", [128, NF, NSEQ, 2])
        CL = sb("CL", [128, NF, 1 + NSEQ, 2])
        PA = sc.enter_context(nc.psum_tensor("fu_PA", [128, 3, 512], F32))
        PB = sc.enter_context(nc.psum_tensor("fu_PB", [128, 3, 512], F32))
        w_in = [nc.alloc_semaphore(name=f"fu_w_in{i}") for i in range(2)]
        small_in, zeroed, a_done, a_read, b_done, convolved, curved, finished, sent = (
            nc.alloc_semaphore(name=f"fu_{n}") for n in (
                "small_in", "zeroed", "a_done", "a_read", "b_done", "convolved", "curved", "finished", "sent"))
        with nc.Block() as block:
            @block.sync
            def _(sp):
                sp.dma_start(cw[:, :, :], I["conv_wb"]).then_inc(small_in, 16)
                sp.dma_start(cst[:, :, :, :], I["conv_state"]).then_inc(small_in, 16)
                wv = I["w_up"].rearrange("(k p) n -> p k n", p=128)
                for t in range(NF):
                    if t >= 2:
                        sp.wait_ge(b_done, t - 1)
                    for j in range(2):
                        c = DFF * j + 128 * t
                        sp.dma_start(W[:, t % 2, :, j, :], wv[:, :, c:c + 128]).then_inc(w_in[t % 2], 16)
                sp.wait_ge(convolved, NF)
                sp.dma_start(conv_out, CL[:, :, :, :]).then_inc(sent, 16)
                sp.wait_ge(sent, 16)

            @block.tensor
            def _(pe):
                for t in range(NF):
                    pe.wait_ge(w_in[t % 2], 32 * (t // 2 + 1))
                    for j, (P, done, free) in enumerate(((PA, a_done, a_read), (PB, b_done, finished))):
                        if t >= 1:
                            pe.wait_ge(free, t)
                        for i, (c, w) in enumerate(COLS):
                            for k in range(KD):
                                last = pe.matmul(P[:, i, 0:w], W[:, t % 2, k, j, :], xT[:, k, c:c + w],
                                                 start=k == 0, stop=k == KD - 1)
                        last.then_inc(done, 1)

            @block.scalar
            def _(act):
                act.wait_ge(zeroed, 1)
                act.wait_ge(small_in, 32)

                def curve(t):
                    act.wait_ge(convolved, t + 1)
                    act.activation(C[:, t % 2, :], C[:, t % 2, :], ACT.Gelu).then_inc(curved, 1)

                for t in range(NF):
                    ax = AX[:, t % 2]
                    seqs = ax[:, 2 + TP:].rearrange("p (b q) -> p b q", q=10)
                    if t >= 2:
                        act.wait_ge(convolved, t - 1)
                    act.activation(seqs[:, :, 0:2], cst[:, t], ACT.Copy)
                    act.wait_ge(a_done, t + 1)
                    for i, (c, w) in enumerate(COLS):
                        if c + w <= TP:
                            act.activation(ax[:, 2 + c:2 + c + w], PA[:, i, 0:w], ACT.Copy)
                        else:
                            act.activation(ax[:, 2 + c:2 + TP], PA[:, i, 0:TP - c], ACT.Copy)
                            act.activation(seqs[:, :, 2:10], PA[:, i, TP - c:w].rearrange(
                                "p (b q) -> p b q", q=8), ACT.Copy)
                    act.drain().then_inc(a_read, 1)
                    curve(t)

            @block.vector
            def _(dve):
                for i in range(2):
                    dve.memset(AX[:, i, 0:2], 0.0)
                dve.drain().then_inc(zeroed, 1)
                dve.wait_ge(small_in, 32)
                for t in range(NF):
                    ax = AX[:, t % 2]
                    seqs = ax[:, 2 + TP:].rearrange("p (b q) -> p b q", q=10)
                    cseq = C[:, t % 2, TP:R].rearrange("p (b q) -> p b q", q=8)
                    dve.wait_ge(a_read, t + 1)
                    dve.tensor_scalar(C[:, t % 2, 0:TP], ax[:, 0:TP], cw[:, 0, t:t + 1], cw[:, 3, t:t + 1],
                                      ALU.mult, ALU.add)
                    dve.tensor_scalar(cseq, seqs[:, :, 0:8], cw[:, 0, t:t + 1], cw[:, 3, t:t + 1],
                                      ALU.mult, ALU.add)
                    dve.drain()
                    for j in (1, 2):
                        dve.scalar_tensor_tensor(C[:, t % 2, 0:TP], ax[:, j:j + TP], cw[:, j, t:t + 1],
                                                 C[:, t % 2, 0:TP], ALU.mult, ALU.add)
                        dve.scalar_tensor_tensor(cseq, seqs[:, :, j:j + 8], cw[:, j, t:t + 1], cseq,
                                                 ALU.mult, ALU.add)
                        dve.drain()
                    dve.tensor_copy(CL[:, t, 0, :], ax[:, TP:TP + 2])
                    dve.tensor_copy(CL[:, t, 1:, :], seqs[:, :, 8:10])
                    dve.drain().then_inc(convolved, 1)
                    dve.wait_ge(curved, t + 1)
                    dve.wait_ge(b_done, t + 1)
                    for i, (c, w) in enumerate(COLS):
                        last = dve.tensor_tensor(HT[:, t, c:c + w], C[:, t % 2, c:c + w], PB[:, i, 0:w], ALU.mult)
                    dve.drain().then_inc(finished, 1)


def ffn_down(nc, I, HT, x1, y):
    with ExitStack() as sc:
        sc.enter_context(nc.cleanup_on_exit())
        def sb(name, shape, dt=F32):
            return sc.enter_context(nc.sbuf_tensor(f"fd_{name}", shape, dt))
        W = sb("W", [128, NF, D])
        X = sb("X", [128, 2, D])
        gain = sb("gain", [128, D])
        ss = sb("ss", [128, NB])
        mhalf = sb("mhalf", [128, 1])
        PO = sc.enter_context(nc.psum_tensor("fd_PO", [128, 2, 2, 512], F32))
        PJ = sc.enter_context(nc.psum_tensor("fd_PJ", [128, 2, 512], F32))
        lots = [(f, min(2, NF - f)) for f in range(0, NF, 2)]
        w_in = [nc.alloc_semaphore(name=f"fd_w_in{i}") for i in range(len(lots))]
        x_in = [nc.alloc_semaphore(name=f"fd_x_in{i}") for i in range(2)]
        y_out = [nc.alloc_semaphore(name=f"fd_y_out{i}") for i in range(2)]
        gain_in, product, added, squared, rooted, scaled = (
            nc.alloc_semaphore(name=f"fd_{n}") for n in (
                "gain_in", "product", "added", "squared", "rooted", "scaled"))
        with nc.Block() as block:
            @block.sync
            def _(sp):
                sp.dma_start(X[:, 0, :], x1[0:128, :]).then_inc(x_in[0], 16)
                sp.dma_start(gain[:, :], I["final_g"].rearrange("(a n) -> a n", a=1).to_broadcast([128, D])
                             ).then_inc(gain_in, 16)
                for i, (f, k) in enumerate(lots):
                    sp.dma_start(W[:, f:f + k, :], I["w_down"][128 * f:128 * (f + k), :].rearrange(
                        "(k p) n -> p k n", p=128)).then_inc(w_in[i], 16)
                for b, (r, n) in enumerate(BLOCKS):
                    if b + 1 < NB:
                        q, m = BLOCKS[b + 1]
                        if b >= 1:
                            sp.wait_ge(y_out[(b + 1) % 2], 16 * ((b + 1) // 2))
                        sp.dma_start(X[0:m, (b + 1) % 2, :], x1[q:q + m, :]).then_inc(x_in[(b + 1) % 2], 16)
                    sp.wait_ge(x_in[b % 2], 16 * (b // 2 + 1))
                    sp.wait_ge(scaled, b + 1)
                    sp.dma_start(y[r:r + n, :], X[0:n, b % 2, :]).then_inc(y_out[b % 2], 16)
                for i in range(2):
                    sp.wait_ge(y_out[i], 16 * ((NB + 1 - i) // 2))

            @block.tensor
            def _(pe):
                for b, (r, n) in enumerate(BLOCKS):
                    if b >= 2:
                        pe.wait_ge(added, b - 1)
                    for f in range(NF):
                        if b == 0 and f % 2 == 0:
                            pe.wait_ge(w_in[f // 2], 16)
                        for j in range(2):
                            last = pe.matmul(PO[0:n, b % 2, j, :], HT[:, f, r:r + n],
                                             W[:, f, 512 * j:512 * j + 512], start=f == 0, stop=f == NF - 1)
                    last.then_inc(product, 1)

            @block.scalar
            def _(act):
                for b, (r, n) in enumerate(BLOCKS):
                    act.wait_ge(added, b + 1)
                    act.activation(PJ[0:n].rearrange("p j c -> p (j c)"), X[0:n, b % 2, :], ACT.Square,
                                   accum_out=ss[0:n, b:b + 1])
                    act.drain().then_inc(squared, 1)

            @block.gpsimd
            def _(pool):
                pool.memset(mhalf[:, :], -0.5)
                pool.drain()
                for b, (r, n) in enumerate(BLOCKS):
                    pool.wait_ge(squared, b + 1)
                    pool.tensor_scalar(ss[0:n, b:b + 1], ss[0:n, b:b + 1], 1.0 / D, EPS, ALU.mult, ALU.add)
                    pool.drain()
                    pool.tensor_tensor(ss[0:n, b:b + 1], ss[0:n, b:b + 1], mhalf[0:n, :],
                                       ALU.pow).then_inc(rooted, 1)

            @block.vector
            def _(dve):
                dve.wait_ge(gain_in, 16)
                for b, (r, n) in enumerate(BLOCKS):
                    dve.wait_ge(x_in[b % 2], 16 * (b // 2 + 1))
                    dve.wait_ge(product, b + 1)
                    halves = X[0:n, b % 2, :].rearrange("p (j c) -> p j c", j=2)
                    dve.tensor_tensor(halves, halves, PO[0:n, b % 2], ALU.add)
                    dve.drain().then_inc(added, 1)
                    dve.wait_ge(rooted, b + 1)
                    dve.scalar_tensor_tensor(X[0:n, b % 2, :], X[0:n, b % 2, :], ss[0:n, b:b + 1],
                                             gain[0:n, :], ALU.mult, ALU.mult).then_inc(scaled, 1)


def program(nc, I, O, stop=99):
    ctx = ExitStack()
    with ctx:
        def sb(name, shape, dt=F32):
            return ctx.enter_context(nc.sbuf_tensor(name, shape, dt))

        def scratch(name, shape):
            return nc.dram_tensor(name, shape, F32).ap()

        ident = sb("ident", [128, 128])
        S = {"qT": scratch("qT", (128, 4, TS)), "qiT": scratch("qiT", (128, 4, TS)),
             "kT": scratch("kT", (128, 2, TS)), "kiT": scratch("kiT", (128, TS)), "wi": scratch("wi", (TS, 8))}
        ya = O["dbg"] if stop in (2, 3) else scratch("yaT_dram", (128, 4, R))
        c_in = ctx.enter_context(nc.semaphore("c_in"))
        with nc.Block() as block:
            @block.sync
            def _(sp):
                sp.dma_start(ident[:, :], I["ident"]).then_inc(c_in, 16)
                sp.wait_ge(c_in, 16)
        xT_dram = scratch("xT_dram", (128, KD, R))
        yr_dram = O["dbg"] if stop == 4 else scratch("yr_dram", (128, 4, R))
        with ExitStack() as hold:
            def sr(name, shape):
                return hold.enter_context(nc.sbuf_tensor(name, shape, F32))
            PM = sr("PM", [128, 12, R])
            with ExitStack() as inner:
                PML = inner.enter_context(nc.sbuf_tensor("PML", [128, 2, R], F32))
                with ExitStack() as first:
                    xT = first.enter_context(nc.sbuf_tensor("xT", [128, KD, R], F32))
                    norm(nc, ctx, KD, "n1", I["x"], I["norm1_g"], xT, ident)
                    if stop != 3:
                        rwkv_project(nc, I, xT, PM, PML, O["shift"])
                    dump(nc, first, xT[:, :, :], xT_dram, "xT_out")
                if stop != 3:
                    F = {n: inner.enter_context(nc.sbuf_tensor(f"F{n}", [128, 4, R], F32)) for n in ("A", "B", "G", "RKK")}
                    PL = inner.enter_context(nc.sbuf_tensor("PL", [128, 4, 25], F32))
                    rwkv_factors(nc, I, PM, PML, F, PL)
                    rwkv_chunks(nc, I, PM, F, PL, O["state_p"], O["state_s"], ident)
                    dump(nc, inner, F["G"][:, :, :], yr_dram, "yr_out")
            if stop == 4:
                return
        with ExitStack() as hold:
            def sh(name, shape):
                return hold.enter_context(nc.sbuf_tensor(name, shape, F32))
            xT = sh("xT2", [128, KD, R])
            dump(nc, hold, xT_dram, xT[:, :, :], "xT_in")
            T = {"QT": sh("QT", [128, 4, R]), "QIT": sh("QIT", [128, 4, R]), "KT": sh("KT", [128, 2, R]),
                 "KIT": sh("KIT", [128, R]), "V": sh("V", [128, NB, 256]), "WI": sh("WI", [128, NB, 8])}
            dsa_project(nc, I["w_in"], I["cos"], I["sin"], xT, ident, T, O["k"], O["v"], O["ki"], S)
            if stop != 3:
                yaT = sh("yaT", [128, 4, TP])
                dsa_prompt(nc, T, yaT, ident)
                dump(nc, hold, yaT[:, :, :], ya[:, :, 0:TP], "ya_out")
        with ExitStack() as hold:
            def sh(name, shape, dt=F32):
                return hold.enter_context(nc.sbuf_tensor(name, shape, dt))
            PHT = sh("PHT", [128, 2, TS], I32)
            NM = sh("NM", [TS, TOPK + QS])
            with ExitStack() as inner:
                SC = inner.enter_context(nc.sbuf_tensor("SC", [128, HALF], F32))
                sample_scores(nc, S, I, SC, ident)
                sample_topk(nc, S, I, SC, PHT, NM, ident)
            sample_attend(nc, S, I, PHT, NM, ya, O["v"], ident)
        if stop in (2, 3):
            return
        x1 = scratch("x1_dram", (R, D))
        with ExitStack() as hold:
            xT = hold.enter_context(nc.sbuf_tensor("xT3", [128, KD, R], F32))
            dump(nc, hold, xT_dram, xT[:, :, :], "xT_in2")
            merge(nc, I, xT, yr_dram, ya, x1)
        HT = sb("HT", [128, NF, R])
        with ExitStack() as hold:
            xT = hold.enter_context(nc.sbuf_tensor("xT4", [128, KD, R], F32))
            norm(nc, hold, KD, "n2", x1, I["norm2_g"], xT, ident)
            ffn_up(nc, I, xT, HT, O["conv"])
        ffn_down(nc, I, HT, x1, O["y"])


def dump(nc, ctx, t, o, name):
    with nc.cleanup_on_exit():
        d = nc.alloc_semaphore(name=name)
        with nc.Block() as block:
            @block.sync
            def _(sp):
                sp.dma_start(o, t).then_inc(d, 16)
                sp.wait_ge(d, 16)


def shape_constants():
    import numpy as np
    f = np.float32
    half = HD // 8
    inv = f(500000.0) ** (-np.arange(half, dtype=f) / half)
    pos = np.concatenate([np.arange(TP), np.tile(PAST + np.arange(QS), NSEQ)]).astype(f)
    angle = pos[:, None] * inv.astype(f)[None, :]

    def by_block(a):
        out = np.zeros((NB * 128, half), f)
        out[:R] = a
        return out.reshape(NB, 128, half).transpose(1, 0, 2)

    p = np.arange(128)
    h, s, q = p // 16, p // 8 % 2, p % 8
    expand = np.zeros((NSEQ, QS, NSEQ, QS, 8), f)
    for b in range(NSEQ):
        for i in range(QS):
            expand[b, i, b, i, :] = 1
    head, row = p // 64, p % 64
    S1, T1 = row[:, None], row[None, :]
    same = head[:, None] == head[None, :]
    beside = lambda b: same & (S1 // b % 2 == 0) & (T1 // b == S1 // b + 1)
    seq = S1 // QS == T1 // QS
    masks = [same & (S1 < T1), same & (S1 > T1), same & (S1 <= T1), beside(1), beside(1).T,
             np.eye(128, dtype=bool)] + [beside(2 ** l) for l in range(1, 6)]
    masks += [m & seq for m in masks[:3]]
    keep = np.ones(R, f)
    keep[0:TP:CH] = 0
    keep[TP:R:QS] = 0
    return {
        "cos": by_block(np.cos(angle)), "sin": by_block(np.sin(angle)), "ident": np.eye(128, dtype=f),
        "half": (p % 2).astype(f)[:, None], "sel16": ((s * 8 + q)[:, None] == np.arange(16)).astype(f),
        "late": np.where(np.arange(QS)[None, :] > (p % QS)[:, None], f(LOW), f(0)),
        "expand8": expand.reshape(TS, NSEQ, TS), "masks": np.stack(masks, 1).astype(f),
        "seqm": (row[:, None] // QS == np.arange(NSEQ)).astype(f),
        "stack": (row[:, None] == np.arange(CH)).astype(f), "ones_pair": same.astype(f),
        "keep": np.tile(keep, (128, 1)),
    }


def laid_out(a):
    import numpy as np
    col = lambda v, n: v.reshape(n, 128).T
    by_head_row = lambda v: np.repeat(v.reshape(4, 2, 64).transpose(1, 0, 2), 64, 0)
    pt = a["page_table"]
    vecs = [a[n][0].reshape(-1) for n in ("rwkv_w0", "rwkv_a0", "rwkv_k_k", "rwkv_k_a", "rwkv_r_k")]
    return {
        "x": np.concatenate([a["meta_tokens"], a["x_prompt"][0], a["x_sample"].reshape(TS, D)]),
        "norm1_g": a["norm1_g"][0], "norm2_g": a["norm2_g"][0], "final_g": a["final_norm_g"],
        "w_in": a["w_in"][0], "w_br_rwkv": a["w_br_rwkv"][0], "w_br_attn": a["w_br_attn"][0],
        "w_out": a["w_out"][0], "w_up": a["w_up"][0], "w_down": a["w_down"][0],
        "w_w2": a["rwkv_w_w2"][0], "w_a2": a["rwkv_w_a2"][0], "w_g2": a["rwkv_w_g2"][0],
        "cache_kidx": a["cache_kidx"].reshape(NPOOL * 2, PAGE // 2 * HD),
        "cache_k": a["cache_k"].reshape(NPOOL * PAGE, 256),
        "cache_v": a["cache_v"].reshape(NPOOL * PAGE, 256),
        "pt_half": pt[:, np.arange(128) // 2].T, "pt_query": np.repeat(pt, QS, 0),
        "mu": col(a["rwkv_mu"][0], 14),
        "shift": a["state_rwkv_shift"][0].reshape(NSEQ, 14, 128).transpose(2, 1, 0),
        "rvec": np.stack([col(v, 4) for v in vecs], 1),
        "lng": by_head_row(a["rwkv_lnx_g"][0]), "lnb": by_head_row(a["rwkv_lnx_b"][0]),
        "state": a["state_rwkv"][0].reshape(NSEQ, 4, 2, 64, 64).transpose(2, 4, 1, 0, 3).reshape(128, 4, NSEQ, 64),
        "conv_wb": np.stack([col(a["conv_w"][0, j], NF) for j in range(3)] + [col(a["conv_b"][0], NF)], 1),
        "conv_state": a["state_ffn_conv"][0].reshape(NSEQ, 2, NF, 128).transpose(3, 2, 0, 1),
    }


_OUTS = {"y": (R, D), "k": (R, 256), "v": (R, 256), "ki": (R, 64), "shift": (128, 14, 1 + NSEQ),
         "state_p": (128, 4, 64), "state_s": (128, 4, NSEQ, 64), "conv": (128, NF, 1 + NSEQ, 2)}


def kernel(**inputs):
    import numpy as np
    import concourse.bacc as bacc
    from concourse.bass_utils import run_bass_kernel_spmd

    nc = bacc.Bacc("TRN2", target_bir_lowering=False, num_devices=1)
    arrays, args = {}, {}
    given = {n: np.asarray(v) for n, v in inputs.items()}
    for name, v in {**shape_constants(), **laid_out(given)}.items():
        v = np.ascontiguousarray(v)
        arrays[f"in_{name}"] = v
        args[name] = nc.dram_tensor(f"in_{name}", v.shape, mybir.dt.from_np(v.dtype), kind="ExternalInput").ap()
    outs = {n: nc.dram_tensor(f"out_{n}", s, F32, kind="ExternalOutput").ap() for n, s in _OUTS.items()}
    program(nc, args, outs)
    got = run_bass_kernel_spmd(nc, [arrays], core_ids=[0]).results[0]
    y, k, v, ki, shift, sp, ss, conv = (np.asarray(got[f"out_{n}"]) for n in _OUTS)
    shift = shift.transpose(2, 1, 0).reshape(1 + NSEQ, P_R)
    sp = sp.reshape(2, 64, 4, 64).transpose(2, 0, 3, 1).reshape(1, 1, 8, 64, 64)
    ss = ss.reshape(2, 64, 4, NSEQ, 64).transpose(3, 2, 0, 4, 1).reshape(1, NSEQ, 8, 64, 64)
    conv = conv.transpose(2, 3, 1, 0).reshape(1 + NSEQ, 2, DFF)
    c = np.ascontiguousarray
    return (c(y[N_META:TP]).reshape(1, SEQ, D), c(y[TP:]).reshape(NSEQ, QS, D),
            c(k[:TP]).reshape(1, 1, TP, 4, 64), c(v[:TP]).reshape(1, 1, TP, 4, 64),
            c(ki[:TP]).reshape(1, 1, TP, 64), c(sp), c(shift[:1]).reshape(1, 1, P_R),
            c(conv[:1]).reshape(1, 1, 2, DFF),
            c(k[TP:]).reshape(1, NSEQ, QS, 4, 64), c(v[TP:]).reshape(1, NSEQ, QS, 4, 64),
            c(ki[TP:]).reshape(1, NSEQ, QS, 64), c(ss), c(shift[1:]).reshape(1, NSEQ, P_R),
            c(conv[1:]).reshape(1, NSEQ, 2, DFF))
```

```python
import concourse.bass as bass
from concourse import mybir
from contextlib import ExitStack

F32 = mybir.dt.float32
I32 = mybir.dt.int32
U32 = mybir.dt.uint32
ALU = mybir.AluOpType
ACT = mybir.ActivationFunctionType
AX = mybir.AxisListType

D = 1024
KD = D // 128
N_META, SEQ = 16, 1024
TP = N_META + SEQ
NSEQ, QS = 8, 8
TS = NSEQ * QS
R = TP + TS
BLOCKS = [(r, min(128, R - r)) for r in range(0, R, 128)]
NB = len(BLOCKS)
EPS = 1e-6
HD = 64
P_R, P_A = 1792, 1608
CQ, CK, CQI, CKI, CV, CWI = 0, 512, 768, 1280, 1344, 1600
PAST, PAGE, NPAGES, NPOOL = 8192, 128, 64, 640
TOPK = 256
BIG = 1e30
LOW, TAKEN = -3.0e38, -3.3e38
DFF = 2816


def norm(nc, ctx, K, tag, x, gain, xT, ident):
    with ExitStack() as sc:
        sc.enter_context(nc.cleanup_on_exit())
        X = sc.enter_context(nc.sbuf_tensor(f"{tag}_X", [128, 3, D], F32))
        junk = sc.enter_context(nc.sbuf_tensor(f"{tag}_junk", [128, D], F32))
        ss = sc.enter_context(nc.sbuf_tensor(f"{tag}_ss", [128, NB], F32))
        mhalf = sc.enter_context(nc.sbuf_tensor(f"{tag}_mhalf", [128, 1], F32))
        rs = sc.enter_context(nc.sbuf_tensor(f"{tag}_rs", [128, NB], F32))
        g = sc.enter_context(nc.sbuf_tensor(f"{tag}_g", [128, KD], F32))
        PS = sc.enter_context(nc.psum_tensor(f"{tag}_PS", [128, 2, KD, 128], F32))
        loaded = [nc.alloc_semaphore(name=f"{tag}_loaded{i}") for i in range(3)]
        g_in, summed, rooted, scaled, turned, stored = (
            nc.alloc_semaphore(name=f"{tag}_{n}")
            for n in ("g_in", "summed", "rooted", "scaled", "turned", "stored"))
        with nc.Block() as block:
            @block.sync
            def _(sp):
                sp.dma_start(g[:, :], gain.rearrange("(k p) -> p k", p=128),
                             allow_slow_non_contiguous=True).then_inc(g_in, 16)
                for b, (r, n) in enumerate(BLOCKS):
                    if b >= 3:
                        sp.wait_ge(turned, b - 2)
                    sp.dma_start(X[0:n, b % 3, :], x[r:r + n, :]).then_inc(loaded[b % 3], 16)

            @block.scalar
            def _(act):
                for b, (r, n) in enumerate(BLOCKS):
                    act.wait_ge(loaded[b % 3], 16 * (b // 3 + 1))
                    act.activation(junk[0:n, :], X[0:n, b % 3, :], ACT.Square,
                                   accum_out=ss[0:n, b:b + 1]).then_inc(summed, 1)
                    act.drain()

            @block.gpsimd
            def _(pool):
                pool.memset(mhalf[:, :], -0.5)
                for b, (r, n) in enumerate(BLOCKS):
                    pool.wait_ge(summed, b + 1)
                    pool.tensor_scalar(rs[0:n, b:b + 1], ss[0:n, b:b + 1], 1.0 / D, EPS, ALU.mult, ALU.add)
                    pool.drain()
                    pool.tensor_tensor(rs[0:n, b:b + 1], rs[0:n, b:b + 1], mhalf[0:n, :],
                                       ALU.pow).then_inc(rooted, 1)

            @block.vector
            def _(dve):
                dve.wait_ge(g_in, 16)
                for b, (r, n) in enumerate(BLOCKS):
                    dve.wait_ge(rooted, b + 1)
                    dve.tensor_scalar(X[0:n, b % 3, :], X[0:n, b % 3, :], rs[0:n, b:b + 1], None,
                                      ALU.mult).then_inc(scaled, 1)
                    dve.wait_ge(turned, b + 1)
                    dve.tensor_tensor(xT[:, :, r:r + n], PS[:, b % 2, :, 0:n],
                                      g[:, :].rearrange("p (k a) -> p k a", a=1).to_broadcast([128, KD, n]),
                                      ALU.mult).then_inc(stored, 1)

            @block.tensor
            def _(pe):
                for b, (r, n) in enumerate(BLOCKS):
                    pe.wait_ge(scaled, b + 1)
                    if b >= 2:
                        pe.wait_ge(stored, b - 1)
                    for k in range(KD):
                        last = pe.transpose(PS[:, b % 2, k, 0:n], X[0:n, b % 3, 128 * k:128 * k + 128],
                                            ident[0:n, 0:n])
                    last.then_inc(turned, 1)


def dsa_project(nc, w_in, cos, sin, xT, xT_dram, ident, T, k_out, v_out, ki_out, S):
    NC4 = P_A // 4
    with ExitStack() as sc:
        sc.enter_context(nc.cleanup_on_exit())
        W = sc.enter_context(nc.sbuf_tensor("pa_W", [128, KD, P_A], F32))
        H = sc.enter_context(nc.sbuf_tensor("pa_H", [128, 2, P_A], F32))
        KID = sc.enter_context(nc.sbuf_tensor("pa_KID", [128, 2, 128], F32))
        cs = sc.enter_context(nc.sbuf_tensor("pa_cs", [128, NB, 2, 8], F32))
        t = sc.enter_context(nc.sbuf_tensor("pa_t", [128, 4, 21, 8], F32))
        PG = sc.enter_context(nc.psum_tensor("pa_PG", [128, 4, 512], F32))
        PT = sc.enter_context(nc.psum_tensor("pa_PT", [128, 12, 128], F32))
        w_loaded = [nc.alloc_semaphore(name=f"pa_w_loaded{k}") for k in range(KD)]
        written = [nc.alloc_semaphore(name=f"pa_written{i}") for i in range(2)]
        xT_out = nc.alloc_semaphore(name="pa_xT_out")
        cs_in, gemm_done, copied, roped, turned, stored, spilled = (
            nc.alloc_semaphore(name=f"pa_{n}")
            for n in ("cs_in", "gemm_done", "copied", "roped", "turned", "stored", "spilled"))
        pieces = [(CK, 512, 256), (CQI, 1024, 512), (CKI, 1544, 64), (CV, 768, 256), (CWI, 1536, 8)]
        with nc.Block() as block:
            @block.sync
            def _(sp):
                for k in range(KD):
                    for dst, src, w in pieces:
                        sp.dma_start(W[:, k, dst:dst + w],
                                     w_in[128 * k:128 * k + 128, P_R + src:P_R + src + w]
                                     ).then_inc(w_loaded[k], 16)
                    src = w_in[128 * k:128 * k + 128, P_R:P_R + 512].rearrange(
                        "p (m h g d) -> p m g h d", m=2, h=2, g=2)
                    for m in range(2):
                        for g in range(2):
                            c = CQ + 256 * m + 128 * g
                            sp.dma_start(W[:, k, c:c + 128].rearrange("p (h d) -> p h d", h=2),
                                         src[:, m, g]).then_inc(w_loaded[k], 16)
                    if k == 0:
                        for j, c in enumerate((cos, sin)):
                            sp.dma_start(cs[:, :, j, :], c).then_inc(cs_in, 16)
                sp.dma_start(xT_dram, xT[:, :, :]).then_inc(xT_out, 16)
                for b, (r, n) in enumerate(BLOCKS):
                    sp.wait_ge(roped, b + 1)
                    for dst, c, w in ((k_out, CK, 256), (v_out, CV, 256), (ki_out, CKI, 64)):
                        sp.dma_start(dst[r:r + n, :], H[0:n, b % 2, c:c + w]).then_inc(written[b % 2], 16)
                for i in range(2):
                    sp.wait_ge(written[i], 48 * ((NB + 1 - i) // 2))
                sp.wait_ge(stored, NB)
                sp.dma_start(S["qT"], T["QT"][:, :, TP:R]).then_inc(spilled, 16)
                sp.dma_start(S["qiT"], T["QIT"][:, :, TP:R]).then_inc(spilled, 16)
                sp.dma_start(S["kT"], T["KT"][:, :, TP:R]).then_inc(spilled, 16)
                sp.dma_start(S["kiT"], T["KIT"][:, TP:R]).then_inc(spilled, 16)
                sp.dma_start(S["wi"], T["WI"][TP % 128:TP % 128 + TS, NB - 1, :]).then_inc(spilled, 16)
                sp.wait_ge(spilled, 80)
                sp.wait_ge(xT_out, 16)

            @block.tensor
            def _(pe):
                for b, (r, n) in enumerate(BLOCKS):
                    if b >= 1:
                        pe.wait_ge(copied, 4 * b)
                    for c in range(4):
                        for k in range(KD):
                            if b == 0 and c == 0:
                                pe.wait_ge(w_loaded[k], 16 * (len(pieces) + 4))
                            last = pe.matmul(PG[0:n, c, 0:NC4], xT[:, k, r:r + n],
                                             W[:, k, NC4 * c:NC4 * c + NC4], start=k == 0, stop=k == KD - 1)
                        last.then_inc(gemm_done, 1)
                    pe.wait_ge(roped, b + 1)
                    if b >= 1:
                        pe.wait_ge(stored, b)
                    for j in range(4):
                        pe.transpose(PT[:, j, 0:n], H[0:n, b % 2, CQ + 128 * j:CQ + 128 * j + 128],
                                     ident[0:n, 0:n])
                        pe.transpose(PT[:, 4 + j, 0:n], H[0:n, b % 2, CQI + 128 * j:CQI + 128 * j + 128],
                                     ident[0:n, 0:n])
                    for j in range(2):
                        pe.transpose(PT[:, 8 + j, 0:n], H[0:n, b % 2, CK + 128 * j:CK + 128 * j + 128],
                                     ident[0:n, 0:n])
                    pe.transpose(PT[:, 10, 0:n], KID[0:n, b % 2, :], ident[0:n, 0:n]).then_inc(turned, 1)

            @block.scalar
            def _(act):
                for b, (r, n) in enumerate(BLOCKS):
                    if b >= 2:
                        act.wait_ge(turned, b - 1)
                        act.wait_ge(written[b % 2], 48 * (b // 2))
                    for c in range(4):
                        act.wait_ge(gemm_done, 4 * b + c + 1)
                        act.activation(H[0:n, b % 2, NC4 * c:NC4 * c + NC4], PG[0:n, c, 0:NC4],
                                       ACT.Copy).then_inc(copied, 1)
                    act.wait_ge(turned, b + 1)
                    act.activation(T["QT"][:, :, r:r + n], PT[:, 0:4, 0:n], ACT.Copy)
                    act.activation(T["QIT"][:, :, r:r + n], PT[:, 4:8, 0:n], ACT.Copy)
                    act.activation(T["KT"][:, :, r:r + n], PT[:, 8:10, 0:n], ACT.Copy)
                    act.activation(T["KIT"][:, r:r + n], PT[:, 10, 0:n], ACT.Copy).then_inc(stored, 1)

            @block.vector
            def _(dve):
                dve.wait_ge(cs_in, 32)
                for b, (r, n) in enumerate(BLOCKS):
                    dve.wait_ge(copied, 4 * b + 4)
                    heads = H[0:n, b % 2, 0:CV].rearrange("p (h d) -> p h d", d=HD)
                    x1, x2 = heads[:, :, 0:8], heads[:, :, 8:16]
                    c, s = (cs[0:n, b, j:j + 1, :].to_broadcast([n, 21, 8]) for j in range(2))
                    dve.tensor_tensor(t[0:n, 0], x1, c, ALU.mult)
                    dve.tensor_tensor(t[0:n, 1], x2, s, ALU.mult)
                    dve.tensor_tensor(t[0:n, 2], x2, c, ALU.mult)
                    dve.tensor_tensor(t[0:n, 3], x1, s, ALU.mult)
                    dve.drain()
                    dve.tensor_tensor(x1, t[0:n, 0], t[0:n, 1], ALU.subtract)
                    dve.tensor_tensor(x2, t[0:n, 2], t[0:n, 3], ALU.add)
                    dve.drain()
                    if b >= 2:
                        dve.wait_ge(turned, b - 1)
                    for j in range(2):
                        dve.tensor_copy(KID[0:n, b % 2, HD * j:HD * j + HD], H[0:n, b % 2, CKI:CKI + HD])
                    dve.tensor_copy(T["V"][0:n, b, :], H[0:n, b % 2, CV:CV + 256])
                    dve.tensor_scalar(T["WI"][0:n, b, :], H[0:n, b % 2, CWI:CWI + 8], 8 ** -0.5 * HD ** -0.5,
                                      None, ALU.mult).then_inc(roped, 1)
                    dve.drain()


def dsa_prompt(nc, T, yaT, ident):
    QB = [(i, min(128, TP - 128 * i), min(128 * (i + 1), TP)) for i in (1, 8, 7, 6, 5, 4, 3, 2, 0)]
    chunks = lambda m: [(c, min(512, m - c)) for c in range(0, m, 512)]
    with ExitStack() as sc:
        sc.enter_context(nc.cleanup_on_exit())
        EACH = 3
        NR = 24
        RL = sc.enter_context(nc.sbuf_tensor("dp_RL", [128, NR, 512], F32))
        SCORE = sc.enter_context(nc.sbuf_tensor("dp_SCORE", [128, TP], F32))
        MASK = sc.enter_context(nc.sbuf_tensor("dp_MASK", [128, TP], F32))
        top8 = sc.enter_context(nc.sbuf_tensor("dp_top8", [128, 8], F32))
        P = sc.enter_context(nc.sbuf_tensor("dp_P", [128, 2, TP], F32))
        PTS = sc.enter_context(nc.sbuf_tensor("dp_PTS", [128, 2, 9, 128], F32))
        peak = sc.enter_context(nc.sbuf_tensor("dp_peak", [128, 2], F32))
        npeak = sc.enter_context(nc.sbuf_tensor("dp_npeak", [128, 2], F32))
        den = sc.enter_context(nc.sbuf_tensor("dp_den", [128, 2, 8], F32))
        OROW = sc.enter_context(nc.sbuf_tensor("dp_OROW", [128, 512], F32))
        PI = sc.enter_context(nc.psum_tensor("dp_PI", [128, 2, 512], F32))
        PSC = sc.enter_context(nc.psum_tensor("dp_PSC", [128, 1536], F32))
        PT = sc.enter_context(nc.psum_tensor("dp_PT", [128, 2, 4, 128], F32))
        PO = sc.enter_context(nc.psum_tensor("dp_PO", [128, 512], F32))
        dotted, rectified, weighted, filled, chosen, masked, scored, peaked, expd, tiled, untiled, summed, \
            normed, flipped, stored = (
                nc.alloc_semaphore(name=f"dp_{n}") for n in (
                    "dotted", "rectified", "weighted", "filled", "chosen", "masked", "scored", "peaked",
                    "expd", "tiled", "untiled", "summed", "normed", "flipped", "stored"))
        groups = lambda m: [(t, min(4, -(-m // 128) - t)) for t in range(0, -(-m // 128), 4)]
        NQ = len(QB)
        dots0 = [sum(8 * len(chunks(x)) for _, _, x in QB[:j]) for j in range(NQ + 1)]
        tiles0 = [sum(8 * len(groups(x)) + 1 for _, _, x in QB[:j]) for j in range(NQ + 1)]
        fills = [sum(x > TOPK for _, _, x in QB[:j + 1]) for j in range(NQ)]
        with nc.Block() as block:
            @block.tensor
            def _(pe):
                def dot_products(j):
                    i, n, m = QB[j]
                    dots = dots0[j]
                    for c, w in chunks(m):
                        for h in range(8):
                            if dots >= 2:
                                pe.wait_ge(rectified, dots - 1)
                            a = HD * (h % 2)
                            pe.matmul(PI[0:n, dots % 2, 0:w], T["QIT"][a:a + HD, h // 2, 128 * i:128 * i + n],
                                      T["KIT"][a:a + HD, c:c + w], start=True, stop=True).then_inc(dotted, 1)
                            dots += 1

                def attention(j):
                    i, n, m = QB[j]
                    tiles = tiles0[j]

                    def scores(h):
                        u, a, kv = 8 * j + h, HD * (h % 2), h // 4
                        if u >= 1:
                            pe.wait_ge(peaked, u)
                        for c, w in chunks(m):
                            last = pe.matmul(PSC[0:n, c:c + w], T["QT"][a:a + HD, h // 2, 128 * i:128 * i + n],
                                             T["KT"][a:a + HD, kv, c:c + w], start=True, stop=True)
                        last.then_inc(scored, 1)

                    scores(0)
                    for h in range(8):
                        u, a, kv = 8 * j + h, HD * (h % 2), h // 4
                        if h < 7:
                            scores(h + 1)
                        pe.wait_ge(expd, u + 1)
                        for t, k in groups(m):
                            if tiles >= 2:
                                pe.wait_ge(untiled, tiles - 1)
                            for e in range(k):
                                w = min(128, m - 128 * (t + e))
                                last = pe.transpose(PT[0:w, tiles % 2, e, 0:n],
                                                    P[0:n, u % 2, 128 * (t + e):128 * (t + e) + w],
                                                    ident[0:n, 0:n])
                            last.then_inc(tiled, 1)
                            tiles += 1
                        pe.wait_ge(untiled, tiles)
                        if h == 0 and j > 0:
                            pe.wait_ge(normed, j)
                        for t in range(-(-m // 128)):
                            w = min(128, m - 128 * t)
                            v = 128 * kv + a
                            last = pe.matmul(PO[0:n, HD * h:HD * h + HD], PTS[0:w, u % 2, t, 0:n],
                                             T["V"][0:w, t, v:v + HD], start=t == 0, stop=128 * t + w == m)
                        last.then_inc(summed, 1)

                def flip(j):
                    i, n, m = QB[j]
                    tiles = tiles0[j + 1] - 1
                    pe.wait_ge(normed, j + 1)
                    pe.wait_ge(untiled, tiles - 1)
                    for e in range(4):
                        last = pe.transpose(PT[:, tiles % 2, e, 0:n], OROW[0:n, 128 * e:128 * e + 128],
                                            ident[0:n, 0:n])
                    last.then_inc(tiled, 1)

                dot_products(0)
                for j in range(NQ):
                    if j + 1 < NQ:
                        dot_products(j + 1)
                    if j >= 1:
                        flip(j - 1)
                    attention(j)
                flip(NQ - 1)

            @block.scalar
            def _(act):
                def rectify(j):
                    i, n, m = QB[j]
                    dots = dots0[j]
                    for c, w in chunks(m):
                        for h in range(8):
                            act.wait_ge(dotted, dots + 1)
                            if dots >= NR:
                                act.wait_ge(weighted, dots - NR + 1)
                            act.activation(RL[0:n, dots % NR, 0:w], PI[0:n, dots % 2, 0:w],
                                           ACT.Relu).then_inc(rectified, 1)
                            dots += 1

                def attention(j):
                    i, n, m = QB[j]
                    tiles = tiles0[j]

                    def exponential(h):
                        u = 8 * j + h
                        act.wait_ge(peaked, u + 1)
                        act.activation(P[0:n, u % 2, 0:m], P[0:n, u % 2, 0:m], ACT.Exp,
                                       bias=npeak[0:n, u % 2:u % 2 + 1], scale=HD ** -0.5,
                                       accum_out=den[0:n, j % 2, h:h + 1])
                        act.drain().then_inc(expd, 1)

                    for h in range(8):
                        u = 8 * j + h
                        exponential(h)
                        if u >= 2:
                            act.wait_ge(summed, u - 1)
                        for t, k in groups(m):
                            act.wait_ge(tiled, tiles + 1)
                            full = min(k, (m - 128 * t) // 128)
                            if full:
                                act.activation(PTS[:, u % 2, t:t + full, 0:n], PT[:, tiles % 2, 0:full, 0:n],
                                               ACT.Copy)
                            if full < k:
                                w = m - 128 * (t + full)
                                act.activation(PTS[0:w, u % 2, t + full, 0:n], PT[0:w, tiles % 2, full, 0:n],
                                               ACT.Copy)
                            act.drain().then_inc(untiled, 1)
                            tiles += 1

                def place(j):
                    i, n, m = QB[j]
                    tiles = tiles0[j + 1] - 1
                    act.wait_ge(tiled, tiles + 1)
                    act.activation(yaT[:, :, 128 * i:128 * i + n], PT[:, tiles % 2, :, 0:n],
                                   ACT.Copy).then_inc(untiled, 1)

                rectify(0)
                for j in range(NQ):
                    if j + 1 < NQ:
                        rectify(j + 1)
                    if j >= 1:
                        place(j - 1)
                    attention(j)
                place(NQ - 1)

            @block.gpsimd
            def _(pool):
                for j, (i, n, m) in enumerate(QB):
                    w = m - 128 * i
                    if m > TOPK:
                        pool.wait_ge(weighted, dots0[j + 1])
                        pool.affine_select(SCORE[0:n, 128 * i:m], SCORE[0:n, 128 * i:m], [[-1, w]],
                                           ALU.is_ge, LOW, base=0, channel_multiplier=1).then_inc(filled, 1)
                    pool.wait_ge(chosen, j + 1)
                    pool.affine_select(MASK[0:n, 128 * i:m], MASK[0:n, 128 * i:m], [[-1, w]],
                                       ALU.is_ge, -BIG, base=0, channel_multiplier=1).then_inc(masked, 1)

            @block.vector
            def _(dve):
                def weigh(j):
                    i, n, m = QB[j]
                    dots = dots0[j]
                    for c, w in chunks(m):
                        for h in range(8):
                            dve.wait_ge(rectified, dots + 1)
                            rl, wi = RL[0:n, dots % NR, 0:w], T["WI"][0:n, i, h:h + 1]
                            if h == 0:
                                dve.tensor_scalar(SCORE[0:n, c:c + w], rl, wi, None, ALU.mult)
                            else:
                                dve.scalar_tensor_tensor(SCORE[0:n, c:c + w], rl, wi, SCORE[0:n, c:c + w],
                                                         ALU.mult, ALU.add)
                            dve.drain().then_inc(weighted, 1)
                            dots += 1

                def take(j, rounds):
                    i, n, m = QB[j]
                    with dve.Fori(0, rounds):
                        dve.max(top8[0:n, :], SCORE[0:n, 0:m])
                        dve.drain()
                        dve.match_replace(SCORE[0:n, 0:m], top8[0:n, :], SCORE[0:n, 0:m], TAKEN)
                        dve.drain()

                def choose(j):
                    i, n, m = QB[j]
                    if m > TOPK:
                        dve.tensor_scalar(MASK[0:n, 0:m], SCORE[0:n, 0:m], TAKEN, -BIG, ALU.not_equal,
                                          ALU.mult)
                    else:
                        dve.memset(MASK[0:n, 0:m], 0.0)
                    dve.drain().then_inc(chosen, 1)

                def peak_of(j, h):
                    i, n, m = QB[j]
                    u = 8 * j + h
                    if h == 0:
                        dve.wait_ge(masked, j + 1)
                    dve.wait_ge(scored, u + 1)
                    if u >= 2:
                        dve.wait_ge(summed, u - 1)
                    dve.tensor_tensor_reduce(out=P[0:n, u % 2, 0:m], in0=PSC[0:n, 0:m], in1=MASK[0:n, 0:m],
                                             scale=1.0, scalar=-3.4e38, op0=ALU.add, op1=ALU.max,
                                             accum_out=peak[0:n, u % 2:u % 2 + 1])
                    dve.drain()
                    dve.tensor_scalar(npeak[0:n, u % 2:u % 2 + 1], peak[0:n, u % 2:u % 2 + 1],
                                      -HD ** -0.5, None, ALU.mult)
                    dve.drain().then_inc(peaked, 1)

                def normalise(j):
                    i, n, m = QB[j]
                    dn = den[0:n, j % 2, :]
                    dve.wait_ge(summed, 8 * j + 8)
                    dve.reciprocal(dn, dn)
                    dve.drain()
                    dve.tensor_tensor(OROW[0:n, :].rearrange("p (h d) -> p h d", h=8),
                                      PO[0:n, :].rearrange("p (h d) -> p h d", h=8),
                                      dn.rearrange("p (h a) -> p h a", a=1).to_broadcast([n, 8, HD]),
                                      ALU.mult)
                    dve.drain().then_inc(normed, 1)

                weigh(0)
                if QB[0][2] > TOPK:
                    dve.wait_ge(filled, fills[0])
                    take(0, TOPK // 8)
                choose(0)
                for j in range(NQ):
                    ahead = j + 1 < NQ and QB[j + 1][2] > TOPK
                    if j + 1 < NQ:
                        weigh(j + 1)
                    for h in range(8):
                        peak_of(j, h)
                        if ahead:
                            if h == 0:
                                dve.wait_ge(filled, fills[j + 1])
                            take(j + 1, EACH if h < 7 else TOPK // 8 - 7 * EACH)
                    normalise(j)
                    if j + 1 < NQ:
                        choose(j + 1)


HALF = (PAST + QS) // 2
NCH = 17


def sample_scores(nc, S, I, SC, ident):
    with ExitStack() as sc:
        sc.enter_context(nc.cleanup_on_exit())
        def sb(name, shape, dt=F32):
            return sc.enter_context(nc.sbuf_tensor(f"ss_{name}", shape, dt))
        KX = sb("KX", [128, 2, 64 * HD])
        KXI = sb("KXI", [128, 64, 2, HD])
        KTC = sb("KTC", [128, 2, 512])
        RL = sb("RL", [128, 2, 512])
        SC16 = sb("SC16", [16, PAST + QS])
        QB = sb("QB", [128, 4, 8, 2, 8])
        WB = sb("WB", [128, 4, 16])
        sel = sb("sel", [128, 16])
        wcol = sb("wcol", [128, 4])
        KIT = sb("KIT", [128, TS])
        pt = sb("pt", [128, 8], I32)
        half = sb("half", [128, 1])
        idx = sb("idx", [128, 8], I32)
        late = sb("late", [128, QS])
        PK = sc.enter_context(nc.psum_tensor("ss_PK", [128, 2, 4, 128], F32))
        PS = sc.enter_context(nc.psum_tensor("ss_PS", [128, 2, 512], F32))
        PW = sc.enter_context(nc.psum_tensor("ss_PW", [16, 2, 512], F32))
        small_in, q_in, zeroed, ready, idx_ready, woven, turned, evacuated, dotted, rectified, weighted, \
            placed, sent, late_done = (
                nc.alloc_semaphore(name=f"ss_{n}") for n in (
                    "small_in", "q_in", "zeroed", "ready", "idx_ready", "woven", "turned", "evacuated",
                    "dotted", "rectified", "weighted", "placed", "sent", "late_done"))
        kx_in = [nc.alloc_semaphore(name=f"ss_kx_in{i}") for i in range(2)]
        with nc.Block() as block:
            @block.sync
            def _(sp):
                for dst, src in ((pt[:, :], I["pt_half"]), (half[:, :], I["half"]), (KIT[:, :], S["kiT"]),
                                 (sel[:, :], I["sel16"]), (late[:, :], I["late"])):
                    sp.dma_start(dst, src).then_inc(small_in, 16)
                wi = S["wi"].rearrange("(p s q) h -> s h q p", s=2, q=8)
                for s in range(2):
                    for h in range(8):
                        sp.dma_start(wcol[16 * h + 8 * s:16 * h + 8 * s + 8, :], wi[s, h],
                                     allow_slow_non_contiguous=True).then_inc(small_in, 16)
                sp.wait_ge(zeroed, 1)
                qi = S["qiT"].rearrange("(g d) j (p s q) -> s g d j p q", g=2, s=2, q=8)
                for s in range(2):
                    for g in range(2):
                        for p in range(4):
                            sp.dma_start(QB[64 * s:64 * s + 64, p, g::2, s, :],
                                         qi[s, g, :, :, p]).then_inc(q_in, 16)
                for p in range(4):
                    sp.wait_ge(placed, NCH * (p + 1))
                    for h in range(2):
                        sp.dma_start(SC[64 * h + 16 * p:64 * h + 16 * p + 16, :],
                                     SC16[:, HALF * h:HALF * h + HALF]).then_inc(sent, 16)
                    sp.wait_ge(sent, 32 * (p + 1))

            @block.gpsimd
            def _(pool):
                pool.memset(QB[:, :], 0.0).then_inc(zeroed, 1)
                pool.wait_ge(idx_ready, 1)
                for b in range(NSEQ):
                    if b >= 2:
                        pool.wait_ge(woven, b - 1)
                    pool.indirect_dma_start(
                        out=KX[:, b % 2, :], out_offset=None, in_=I["cache_kidx"],
                        in_offset=bass.IndirectOffsetOnAxis(ap=idx[:, b:b + 1], axis=0)
                    ).then_inc(kx_in[b % 2], 16)

            @block.scalar
            def _(act):
                def weave(p):
                    for s in range(2):
                        act.wait_ge(kx_in[s], 16 * (p + 1))
                        if p >= 1:
                            act.wait_ge(turned, 16 * p)
                        act.activation(KXI[:, :, s, :], KX[:, s, :].rearrange("p (o d) -> p o d", d=HD),
                                       ACT.Copy).then_inc(woven, 1)

                weave(0)
                for p in range(4):
                    for c in range(NCH):
                        g = NCH * p + c
                        w = 512 if c < 16 else QS
                        act.wait_ge(dotted, g + 1)
                        if g >= 2:
                            act.wait_ge(weighted, g - 1)
                        act.activation(RL[:, g % 2, 0:w], PS[:, g % 2, 0:w], ACT.Relu).then_inc(rectified, 1)
                        if c == 14 and p < 3:
                            weave(p + 1)

            @block.tensor
            def _(pe):
                pe.wait_ge(q_in, 16 * 16)
                pe.wait_ge(ready, 1)
                for g in range(4 * NCH + 2):
                    if g < 4 * NCH and g % NCH < 16:
                        p, c = g // NCH, g % NCH
                        if c == 0:
                            pe.wait_ge(woven, 2 * p + 2)
                        if g >= 2:
                            pe.wait_ge(evacuated, g - 1)
                        for o in range(4):
                            last = pe.transpose(PK[:, g % 2, o, :],
                                                KXI[:, 4 * c + o, :, :].rearrange("p s d -> p (s d)"),
                                                ident[:, :])
                        last.then_inc(turned, 1)
                    if 1 <= g <= 4 * NCH:
                        e = g - 1
                        w = 512 if e % NCH < 16 else QS
                        pe.wait_ge(evacuated, e + 1)
                        if e >= 2:
                            pe.wait_ge(rectified, e - 1)
                        pe.matmul(PS[:, e % 2, 0:w],
                                  QB[:, e // NCH].rearrange("p h s q -> p (h s q)"),
                                  KTC[:, e % 2, 0:w], start=True, stop=True).then_inc(dotted, 1)
                    if g >= 2:
                        e = g - 2
                        w = 512 if e % NCH < 16 else QS
                        pe.wait_ge(rectified, e + 1)
                        if e >= 2:
                            pe.wait_ge(placed, e - 1)
                        pe.matmul(PW[:, e % 2, 0:w], WB[:, e // NCH, :], RL[:, e % 2, 0:w],
                                  start=True, stop=True).then_inc(weighted, 1)

            @block.vector
            def _(dve):
                dve.wait_ge(small_in, 16 * 21)
                dve.tensor_scalar(idx[:, :], pt[:, :], 2.0, half[:, 0:1], ALU.mult, ALU.add)
                dve.drain().then_inc(idx_ready, 1)
                for p in range(4):
                    dve.tensor_scalar(WB[:, p, :], sel[:, :], wcol[:, p:p + 1], None, ALU.mult)
                dve.drain().then_inc(ready, 1)

                def place(e):
                    p, c = e // NCH, e % NCH
                    dve.wait_ge(weighted, e + 1)
                    if c == 0 and p >= 1:
                        dve.wait_ge(sent, 32 * p)
                    if c < 16:
                        dve.tensor_copy(
                            SC16[:, 0:PAST].rearrange("q (l o) -> q o l", o=64)[:, 4 * c:4 * c + 4, :],
                            PW[:, e % 2, :].rearrange("q (o l) -> q o l", o=4)).then_inc(placed, 1)
                    else:
                        dve.tensor_copy(SC16[:, PAST:PAST + QS], PW[:, e % 2, 0:QS]).then_inc(placed, 1)

                for g in range(4 * NCH):
                    p, c = g // NCH, g % NCH
                    if g >= 2:
                        dve.wait_ge(dotted, g - 1)
                    if c < 16:
                        dve.wait_ge(turned, 16 * p + c + 1)
                        dve.tensor_copy(KTC[:, g % 2, :],
                                        PK[:, g % 2].rearrange("p o l -> p (o l)")).then_inc(evacuated, 1)
                    else:
                        for s in range(2):
                            b = 2 * p + s
                            last = dve.tensor_copy(KTC[64 * s:64 * s + 64, g % 2, 0:QS],
                                                   KIT[64 * s:64 * s + 64, 8 * b:8 * b + 8])
                        last.then_inc(evacuated, 1)
                    if g >= 3:
                        place(g - 3)
                for e in range(4 * NCH - 3, 4 * NCH):
                    place(e)
                dve.wait_ge(sent, 128)
                dve.tensor_tensor(SC[64:128, HALF - QS:HALF], SC[64:128, HALF - QS:HALF], late[64:128, :],
                                  ALU.add).then_inc(late_done, 1)


def sample_topk(nc, I, TK, yrT, yr_dram, PHT, NM, ident):
    with ExitStack() as sc:
        sc.enter_context(nc.cleanup_on_exit())
        def sb(name, shape, dt=F32):
            return sc.enter_context(nc.sbuf_tensor(f"st_{name}", shape, dt))
        VAL, IDX = TK["VAL"], TK["IDX"]
        VB = sb("VB", [64, TOPK])
        IB = sb("IB", [64, TOPK])
        keep = sb("keep", [64, TOPK])
        key = sb("key", [64, TOPK])
        keyi = sb("keyi", [64, TOPK], I32)
        pgi = sb("pgi", [64, TOPK], I32)
        pg = sb("pg", [64, TOPK])
        hit = sb("hit", [64, 2, TOPK])
        row = sb("row", [64, TOPK])
        hit2 = sb("hit2", [64, 2, TOPK])
        row2 = sb("row2", [64, TOPK])
        pti = sb("pti", [64, NPAGES], I32)
        ptf = sb("ptf", [64, NPAGES])
        cnt = sb("cnt", [64, QS])
        PP = sc.enter_context(nc.psum_tensor("st_PP", [128, 2, 64], F32))
        pt_in, listed, moved, rows_done, turned, done = (
            nc.alloc_semaphore(name=f"st_{n}")
            for n in ("pt_in", "listed", "moved", "rows_done", "turned", "done"))
        yr_out, paged, shared = (nc.alloc_semaphore(name=f"st_{n}") for n in ("yr_out", "paged", "shared"))
        MINE = 44
        with nc.Block() as block:
            @block.sync
            def _(sp):
                sp.dma_start(pti[:, :], I["pt_query"]).then_inc(pt_in, 16)
                sp.dma_start(yr_dram, yrT).then_inc(yr_out, 16)
                sp.wait_ge(listed, 1)
                sp.dma_start(VB[:, :], VAL[64:128, :]).then_inc(moved, 16)
                sp.dma_start(IB[:, :], IDX[64:128, :]).then_inc(moved, 16)
                sp.wait_ge(moved, 32)
                sp.wait_ge(yr_out, 16)

            @block.tensor
            def _(pe):
                pe.wait_ge(rows_done, 1)
                for t in range(2):
                    last = pe.transpose(PP[:, t, :], row[:, 128 * t:128 * t + 128], ident[0:64, 0:64])
                last.then_inc(turned, 1)

            def look_up(eng, pages, hits, rows):
                for c in pages:
                    eng.tensor_scalar(hits[:, c % 2], pg[:, :], float(c), ptf[:, c:c + 1], ALU.is_equal,
                                      ALU.mult)
                    eng.drain()
                    eng.tensor_tensor(rows[:, :], rows[:, :], hits[:, c % 2], ALU.add)
                eng.drain()

            @block.gpsimd
            def _(pool):
                pool.memset(row2[:, :], 0.0)
                pool.drain()
                pool.wait_ge(paged, 1)
                look_up(pool, range(MINE, NPAGES), hit2, row2)
                pool.drain().then_inc(shared, 1)

            @block.vector
            def _(dve):
                dve.tensor_scalar(IDX[64:128, :], IDX[64:128, :], float(HALF), None, ALU.add)
                dve.drain().then_inc(listed, 1)
                dve.wait_ge(pt_in, 16)
                dve.tensor_copy(ptf[:, :], pti[:, :])
                dve.wait_ge(moved, 32)
                dve.tensor_tensor(keep[:, :], VAL[0:64, :], VB[:, ::-1], ALU.is_ge)
                dve.tensor_tensor(key[:, :], IDX[0:64, :], IB[:, ::-1], ALU.subtract)
                dve.drain()
                dve.tensor_tensor(key[:, :], key[:, :], keep[:, :], ALU.mult)
                dve.drain()
                dve.tensor_tensor(key[:, :], key[:, :], IB[:, ::-1], ALU.add)
                dve.drain()
                dve.tensor_copy(keyi[:, :], key[:, :])
                dve.drain()
                dve.tensor_scalar(pgi[:, :], keyi[:, :], 7, None, ALU.logical_shift_right)
                dve.drain()
                dve.tensor_copy(pg[:, :], pgi[:, :])
                dve.tensor_scalar(NM[:, 0:TOPK], key[:, :], float(PAST), -BIG, ALU.is_ge, ALU.mult)
                dve.drain()
                dve.scalar_tensor_tensor(row[:, :], pg[:, :], -float(PAGE), key[:, :], ALU.mult, ALU.add)
                dve.drain()
                dve.tensor_scalar(ptf[:, :], ptf[:, :], float(PAGE), None, ALU.mult)
                dve.drain().then_inc(paged, 1)
                look_up(dve, range(MINE), hit, row)
                dve.wait_ge(shared, 1)
                dve.tensor_tensor(row[:, :], row[:, :], row2[:, :], ALU.add)
                dve.drain().then_inc(rows_done, 1)
                for j in range(QS):
                    dve.tensor_scalar(hit[:, j % 2], key[:, :], float(PAST + j), None, ALU.is_equal)
                    dve.drain()
                    dve.reduce_sum(cnt[:, j:j + 1], hit[:, j % 2], AX.X)
                dve.drain()
                dve.tensor_scalar(NM[:, TOPK:TOPK + QS], cnt[:, :], BIG, -BIG, ALU.mult, ALU.add)
                dve.wait_ge(turned, 1)
                dve.tensor_copy(PHT[:, :, :], PP[:, :, :])
                dve.drain().then_inc(done, 1)


def sample_attend(nc, S, I, PHT, NM, ya, v_out, WB, WO, ident):
    NK = TOPK + QS
    with ExitStack() as sc:
        sc.enter_context(nc.cleanup_on_exit())
        def sb(name, shape, dt=F32):
            return sc.enter_context(nc.sbuf_tensor(f"sa_{name}", shape, dt))
        KG = sb("KG", [128, 16, 2, 256])
        VG = sb("VG", [128, 16, 2, 256])
        KGT = sb("KGT", [128, 2, 2, 256])
        QTS = sb("QTS", [128, 4, TS])
        KTS = sb("KTS", [128, 2, TS])
        VN = sb("VN", [QS, NSEQ, 256])
        QF = sb("QF", [128, 2, 2, 64])
        QZ = sb("QZ", [128, 2, 2, 8, 64])
        E8 = sb("E8", [64, NSEQ, 64])
        P = sb("P", [64, 2, NK])
        PTS = sb("PTS", [128, 2, 3, 64])
        st = sb("st", [64, 2, 4])
        YAS = sb("YAS", [128, 4, TS])
        PKT = sc.enter_context(nc.psum_tensor("sa_PKT", [128, 2, 2, 256], F32))
        PSS = sc.enter_context(nc.psum_tensor("sa_PSS", [64, 2, 512], F32))
        PPT = sc.enter_context(nc.psum_tensor("sa_PPT", [128, 2, 4, 128], F32))
        PY = sc.enter_context(nc.psum_tensor("sa_PY", [128, 2, 512], F32))
        small_in, q_ready, turned, evacuated, scored, peaked, expd, normed, tiled, untiled, summed, \
            y_done, sent = (
                nc.alloc_semaphore(name=f"sa_{n}") for n in (
                    "small_in", "q_ready", "turned", "evacuated", "scored", "peaked", "expd",
                    "normed", "tiled", "untiled", "summed", "y_done", "sent"))
        wm_in = nc.alloc_semaphore(name="sa_wm_in")
        k_in = [nc.alloc_semaphore(name=f"sa_k_in{i}") for i in range(4)]
        v_in = [nc.alloc_semaphore(name=f"sa_v_in{i}") for i in range(2)]
        with nc.Block() as block:
            @block.sync
            def _(sp):
                for dst, src in ((QTS[:, :, :], S["qT"]), (KTS[:, :, :], S["kT"]), (E8[:, :, :], I["expand8"]),
                                 (VN[:, :, :], v_out[TP:R, :].rearrange("(b q) c -> q b c", q=QS))):
                    sp.dma_start(dst, src).then_inc(small_in, 16)
                sp.dma_start(WB[:, 0], I["w_br_rwkv"].rearrange("(k p) n -> p k n", p=128)).then_inc(wm_in, 16)
                wa = I["w_br_attn"].rearrange("(m h g d) n -> h d m g n", m=2, h=2, g=2)
                for h in range(2):
                    for m in range(2):
                        sp.dma_start(WB[64 * h:64 * h + 64, 1, 2 * m:2 * m + 2, :],
                                     wa[h, :, m]).then_inc(wm_in, 16)
                sp.dma_start(WO[:, :, :], I["w_out"].rearrange("(k p) n -> p k n", p=128)).then_inc(wm_in, 16)
                sp.wait_ge(wm_in, 16 * 6)
                sp.wait_ge(y_done, NSEQ)
                sp.dma_start(ya[:, :, TP:R], YAS[:, :, :]).then_inc(sent, 16)
                sp.wait_ge(sent, 16)

            @block.gpsimd
            def _(pool):
                for n in range(TS):
                    if n >= 16 and n % 8 == 0:
                        pool.wait_ge(summed, n // 8 - 1)
                    for arrived, G, cache in ((k_in[n // 4 % 4], KG, "cache_k"),
                                              (v_in[n // 8 % 2], VG, "cache_v")):
                        for t in range(2):
                            pool.indirect_dma_start(
                                out=G[:, n % 16, t, :], out_offset=None, in_=I[cache],
                                in_offset=bass.IndirectOffsetOnAxis(ap=PHT[:, t, n:n + 1], axis=0)
                            ).then_inc(arrived, 16)

            @block.tensor
            def _(pe):
                pe.wait_ge(small_in, 64)

                def turn(n):
                    if n % 4 == 0:
                        pe.wait_ge(k_in[n // 4 % 4], 128 * (n // 16 + 1))
                    if n >= 2:
                        pe.wait_ge(evacuated, n - 1)
                    for m in range(2):
                        for t in range(2):
                            last = pe.transpose(PKT[:, n % 2, m, 128 * t:128 * t + 128],
                                                KG[:, n % 16, t, 128 * m:128 * m + 128], ident[:, :])
                    last.then_inc(turned, 1)

                turn(0)
                for b in range(NSEQ):
                    s = b % 2
                    pe.wait_ge(q_ready, b + 1)
                    if b >= 2:
                        pe.wait_ge(peaked, b - 1)
                        pe.wait_ge(expd, b - 1)
                    pe.matmul(PSS[:, s, 0:NK], E8[:, b, :], NM[:, :], start=True, stop=False)
                    for m in range(2):
                        pe.matmul(PSS[:, s, TOPK:NK], QF[:, s, m, :], KTS[:, m, 8 * b:8 * b + 8],
                                  start=False, stop=False)
                    for q in range(8):
                        n = 8 * b + q
                        if n + 1 < TS:
                            turn(n + 1)
                        pe.wait_ge(evacuated, n + 1)
                        for m in range(2):
                            last = pe.matmul(PSS[:, s, 0:TOPK], QZ[:, s, m, q, :], KGT[:, n % 2, m, :],
                                             start=False, stop=q == 7 and m == 1)
                        last.then_inc(scored, 1)
                    pe.wait_ge(normed, b + 1)
                    if b >= 2:
                        pe.wait_ge(untiled, b - 1)
                    for t, w in ((0, 128), (1, 128), (2, QS)):
                        last = pe.transpose(PPT[0:w, s, t, 0:64], P[:, s, 128 * t:128 * t + w],
                                            ident[0:64, 0:64])
                    last.then_inc(tiled, 1)
                    pe.wait_ge(untiled, b + 1)
                    if b >= 2:
                        pe.wait_ge(y_done, b - 1)
                    for m in range(2):
                        pe.matmul(PY[:, s, 64 * m:64 * m + 64], VN[:, b, 128 * m:128 * m + 128],
                                  PTS[0:QS, s, 2, :], start=m == 0, stop=False, skip_group_check=True)
                    pe.wait_ge(v_in[s], 256 * (b // 2 + 1))
                    for q in range(8):
                        n = 8 * b + q
                        for m in range(2):
                            for t in range(2):
                                last = pe.matmul(PY[:, s, 64 * m + 8 * q:64 * m + 8 * q + 8],
                                                 VG[:, n % 16, t, 128 * m:128 * m + 128],
                                                 PTS[:, s, t, 8 * q:8 * q + 8], start=False,
                                                 stop=q == 7 and m == 1 and t == 1, skip_group_check=True)
                    last.then_inc(summed, 1)

            @block.scalar
            def _(act):
                for b in range(NSEQ):
                    s = b % 2
                    for q in range(8):
                        n = 8 * b + q
                        act.wait_ge(turned, n + 1)
                        if n >= 2:
                            act.wait_ge(scored, n - 1)
                        act.activation(KGT[:, n % 2], PKT[:, n % 2], ACT.Copy).then_inc(evacuated, 1)
                    act.wait_ge(peaked, b + 1)
                    if b >= 2:
                        act.wait_ge(tiled, b - 1)
                    act.activation(P[:, s, :], PSS[:, s, 0:NK], ACT.Exp, bias=st[:, s, 1:2],
                                   scale=HD ** -0.5, accum_out=st[:, s, 2:3])
                    act.drain().then_inc(expd, 1)
                    act.wait_ge(tiled, b + 1)
                    if b >= 2:
                        act.wait_ge(summed, b - 1)
                    act.activation(PTS[:, s, 0:2, :], PPT[:, s, 0:2, 0:64], ACT.Copy)
                    act.activation(PTS[0:QS, s, 2, :], PPT[0:QS, s, 2, 0:64], ACT.Copy)
                    act.drain().then_inc(untiled, 1)

            @block.vector
            def _(dve):
                dve.memset(QF[:, :, :, :], 0.0)
                dve.memset(QZ[:, :, :, :, :], 0.0)
                dve.drain()
                dve.wait_ge(small_in, 64)

                def queries(b):
                    s = b % 2
                    if b >= 2:
                        dve.wait_ge(scored, 8 * (b - 1))
                    for m in range(2):
                        for g in range(2):
                            for h in range(2):
                                dve.tensor_copy(
                                    QF[64 * h:64 * h + 64, s, m, :].rearrange("p (q c) -> p c q", c=8)[
                                        :, 4 * m + 2 * h + g, :],
                                    QTS[64 * h:64 * h + 64, 2 * m + g, 8 * b:8 * b + 8])
                    dve.drain()
                    for m in range(2):
                        last = dve.tensor_copy(
                            QZ[:, s, m].rearrange("p q c -> p (q c)")[:, 0:504].rearrange(
                                "p (q c) -> p q c", c=72)[:, :, 0:8],
                            QF[:, s, m, 0:56].rearrange("p (q c) -> p q c", c=8))
                        last = dve.tensor_copy(QZ[:, s, m, 7, 56:64], QF[:, s, m, 56:64])
                    dve.drain().then_inc(q_ready, 1)

                queries(0)
                for b in range(NSEQ):
                    s = b % 2
                    if b + 1 < NSEQ:
                        queries(b + 1)
                    dve.wait_ge(scored, 8 * b + 8)
                    dve.reduce_max(st[:, s, 0:1], PSS[:, s, 0:NK], AX.X)
                    dve.drain()
                    dve.tensor_scalar(st[:, s, 1:2], st[:, s, 0:1], -HD ** -0.5, None, ALU.mult)
                    dve.drain().then_inc(peaked, 1)
                    dve.wait_ge(expd, b + 1)
                    dve.reciprocal(st[:, s, 3:4], st[:, s, 2:3])
                    dve.drain()
                    dve.tensor_scalar(P[:, s, :], P[:, s, :], st[:, s, 3:4], None, ALU.mult).then_inc(normed, 1)
                    dve.wait_ge(summed, b + 1)
                    for m in range(2):
                        for h in range(2):
                            y = PY[64 * h:64 * h + 64, s, 64 * m:64 * m + 64].rearrange("p (q c) -> p c q", c=8)
                            dve.tensor_copy(YAS[64 * h:64 * h + 64, 2 * m:2 * m + 2, 8 * b:8 * b + 8],
                                            y[:, 4 * m + 2 * h:4 * m + 2 * h + 2, :])
                    dve.drain().then_inc(y_done, 1)


CH = 64
COLS = [(0, 368), (368, 368), (736, 368)]


def rwkv_project(nc, I, xT_dram, xT, PM, PML, shift_out, gates, TK):
    NT = P_R // 128
    NG = 2 * D // 128
    ROUNDS = TOPK // 8
    with ExitStack() as sc:
        sc.enter_context(nc.cleanup_on_exit())
        def sb(name, shape, dt=F32):
            return sc.enter_context(nc.sbuf_tensor(f"rp_{name}", shape, dt))
        W = sb("W", [128, 2, KD, 256])
        PX = sb("PX", [128, 2, 1 + TP + NSEQ * 9])
        DF = sb("DF", [128, R])
        v8 = sb("v8", [128, 8])
        i8 = sb("i8", [128, 8], U32)
        mu = sb("mu", [128, NT])
        sh = sb("sh", [128, NT, NSEQ])
        SH = sb("SH", [128, NT, 1 + NSEQ])
        PG = sc.enter_context(nc.psum_tensor("rp_PG", [128, 6, 512], F32))
        w_in = [nc.alloc_semaphore(name=f"rp_w_in{i}") for i in range(2)]
        xT_in = [nc.alloc_semaphore(name=f"rp_xT_in{i}") for i in range(len(COLS))]
        gate_out = [nc.alloc_semaphore(name=f"rp_gate_out{i}") for i in range(2)]
        small_in, zeroed, product, copied, mixed, sent = (
            nc.alloc_semaphore(name=f"rp_{n}")
            for n in ("small_in", "zeroed", "product", "copied", "mixed", "sent"))
        with nc.Block() as block:
            @block.sync
            def _(sp):
                sp.dma_start(mu[:, :], I["mu"]).then_inc(small_in, 16)
                sp.dma_start(sh[:, :, :], I["shift"]).then_inc(small_in, 16)
                def send_gate(t):
                    sp.wait_ge(copied, 3 * t + 3)
                    sp.dma_start(gates[t - NT], PX[:, t % 2, 0:R]).then_inc(gate_out[t % 2], 16)

                for u in range((NT + NG) // 2):
                    if u >= 2:
                        sp.wait_ge(product, 6 * (u - 1))
                    c = 256 * u if 2 * u < NT else P_A + 256 * u
                    sp.dma_start(W[:, u % 2], I["w_in"].rearrange("(k p) n -> p k n", p=128)[
                        :, :, c:c + 256]).then_inc(w_in[u % 2], 16)
                    if u == 0:
                        for j, (x, w) in enumerate(COLS):
                            sp.dma_start(xT[:, :, x:x + w], xT_dram[:, :, x:x + w]).then_inc(xT_in[j], 16)
                    for t in (2 * u - 4, 2 * u - 3):
                        if t >= NT:
                            send_gate(t)
                for t in range(NT + NG - 4, NT + NG):
                    send_gate(t)
                for i in range(2):
                    sp.wait_ge(gate_out[i], 16 * (NG // 2))
                sp.wait_ge(mixed, NT)
                sp.dma_start(shift_out, SH[:, :, :]).then_inc(sent, 16)
                sp.wait_ge(sent, 16)

            @block.tensor
            def _(pe):
                for t in range(NT + NG):
                    pe.wait_ge(w_in[t // 2 % 2], 16 * (t // 4 + 1))
                    for j, (c, w) in enumerate(COLS):
                        if t == 0:
                            pe.wait_ge(xT_in[j], 16)
                        if t >= 2:
                            pe.wait_ge(copied, 3 * (t - 2) + j + 1)
                        for k in range(KD):
                            last = pe.matmul(PG[:, 3 * (t % 2) + j, 0:w],
                                             W[:, t // 2 % 2, k, 128 * (t % 2):128 * (t % 2) + 128],
                                             xT[:, k, c:c + w], start=k == 0, stop=k == KD - 1)
                        last.then_inc(product, 1)

            @block.scalar
            def _(act):
                act.wait_ge(zeroed, 1)
                act.wait_ge(small_in, 32)
                for t in range(NT + NG):
                    if t >= 2:
                        act.wait_ge(mixed, min(t - 1, NT))
                    px = PX[:, t % 2]
                    if t >= NT:
                        if t >= NT + 2:
                            act.wait_ge(gate_out[t % 2], 16 * ((t - NT) // 2))
                        for j, (c, w) in enumerate(COLS):
                            act.wait_ge(product, 3 * t + j + 1)
                            act.activation(px[:, c:c + w], PG[:, 3 * (t % 2) + j, 0:w],
                                           ACT.Sigmoid).then_inc(copied, 1)
                        continue
                    seqs = px[:, 1 + TP:].rearrange("p (b q) -> p b q", q=9)
                    act.activation(seqs[:, :, 0], sh[:, t], ACT.Copy)
                    for j, (c, w) in enumerate(COLS):
                        act.wait_ge(product, 3 * t + j + 1)
                        pg = PG[:, 3 * (t % 2) + j]
                        if c + w <= TP:
                            act.activation(px[:, 1 + c:1 + c + w], pg[:, 0:w], ACT.Copy).then_inc(copied, 1)
                        else:
                            act.activation(px[:, 1 + c:1 + TP], pg[:, 0:TP - c], ACT.Copy)
                            act.activation(seqs[:, :, 1:9], pg[:, TP - c:w].rearrange("p (b q) -> p b q", q=8),
                                           ACT.Copy)
                            act.drain().then_inc(copied, 1)

            @block.gpsimd
            def _(pool):
                for i in range(2):
                    pool.memset(PX[:, i, 0:1], 0.0)
                pool.drain().then_inc(zeroed, 1)
                pool.wait_ge(small_in, 32)
                for t in range(NT):
                    px = PX[:, t % 2]
                    pm = PM[:, t] if t < 12 else PML[:, t - 12]
                    seqs = px[:, 1 + TP:].rearrange("p (b q) -> p b q", q=9)
                    dseq = DF[:, TP:R].rearrange("p (b q) -> p b q", q=8)
                    pool.wait_ge(copied, 3 * t + 3)
                    pool.tensor_tensor(DF[:, 0:TP], px[:, 0:TP], px[:, 1:1 + TP], ALU.subtract)
                    pool.tensor_tensor(dseq, seqs[:, :, 0:8], seqs[:, :, 1:9], ALU.subtract)
                    pool.drain()
                    pool.tensor_scalar(DF[:, :], DF[:, :], mu[:, t:t + 1], None, ALU.mult)
                    pool.drain()
                    pool.tensor_tensor(pm[:, 0:TP], DF[:, 0:TP], px[:, 1:1 + TP], ALU.add)
                    pool.tensor_tensor(pm[:, TP:R].rearrange("p (b q) -> p b q", q=8), dseq,
                                       seqs[:, :, 1:9], ALU.add)
                    pool.tensor_copy(SH[:, t, 0:1], px[:, TP:TP + 1])
                    pool.tensor_copy(SH[:, t, 1:], seqs[:, :, 8])
                    pool.drain().then_inc(mixed, 1)

            @block.vector
            def _(dve):
                SC, VAL, IDX = TK["SC"], TK["VAL"], TK["IDX"]
                with dve.Fori(0, ROUNDS) as i:
                    dve.max(v8[:, :], SC[:, :])
                    dve.drain()
                    dve.max_index(i8[:, :], v8[:, :], SC[:, :])
                    dve.drain()
                    dve.match_replace(SC[:, :], v8[:, :], SC[:, :], TAKEN)
                    dve.tensor_copy(VAL[:, bass.ds(i * 8, 8)], v8[:, :])
                    dve.tensor_copy(IDX[:, bass.ds(i * 8, 8)], i8[:, :])
                    dve.drain()


def rwkv_factors(nc, I, PM, PML, F, PL):
    with ExitStack() as sc:
        sc.enter_context(nc.cleanup_on_exit())
        def sb(name, shape, dt=F32):
            return sc.enter_context(nc.sbuf_tensor(f"rf_{name}", shape, dt))
        vec = sb("vec", [128, 6, 4])
        wa2 = sb("wa2", [128, 512])
        g2 = sb("g2", [128, 512])
        keep = sb("keep", [128, R])
        ones = sb("ones", [128, 128])
        T1, T2, T3, EE = (sb(f"t{i}", [128, 2, R]) for i in range(4))
        PA = sc.enter_context(nc.psum_tensor("rf_PA", [128, 3, 512], F32))
        PB = sc.enter_context(nc.psum_tensor("rf_PB", [128, 3, 512], F32))
        small_in, squashed, w_done, w_read, a_done, a_read, g_done, g_read, squared, sq_done, rooted, \
            summed_log, exps, factored, root_done = (
                nc.alloc_semaphore(name=f"rf_{n}") for n in (
                    "small_in", "squashed", "w_done", "w_read", "a_done", "a_read", "g_done", "g_read",
                    "squared", "sq_done", "rooted", "summed_log", "exps", "factored", "root_done"))
        with nc.Block() as block:
            @block.sync
            def _(sp):
                for dst, src in ((vec[:, 0:4, :], I["rvec"][:, 0:4, :]), (vec[:, 5, :], I["rvec"][:, 4, :]),
                                 (wa2[0:64, :], I["w_w2"]), (wa2[64:128, :], I["w_a2"]), (g2[:, :], I["w_g2"]),
                                 (keep[:, :], I["keep"]), (ones[:, :], I["ones_pair"])):
                    sp.dma_start(dst, src).then_inc(small_in, 16)

            def product(pe, out, lhsT, rhs):
                for j, (c, w) in enumerate(COLS):
                    last = pe.matmul(out[:, j, 0:w], lhsT, rhs[:, c:c + w], start=True, stop=True)
                return last

            @block.tensor
            def _(pe):
                pe.wait_ge(small_in, 16 * 7)
                pe.wait_ge(squashed, 1)
                for c in range(4):
                    ch = slice(128 * c, 128 * c + 128)
                    if c >= 1:
                        pe.wait_ge(g_read, c)
                    product(pe, PA, wa2[0:64, ch], PML[0:64, 0]).then_inc(w_done, 1)
                    if c >= 1:
                        pe.wait_ge(rooted, c)
                    product(pe, PB, wa2[64:128, ch], PML[64:128, 0]).then_inc(a_done, 1)
                    pe.wait_ge(w_read, c + 1)
                    product(pe, PA, g2[:, ch], PML[:, 1]).then_inc(g_done, 1)
                    pe.wait_ge(a_read, c + 1)
                    pe.wait_ge(squared, c + 1)
                    product(pe, PB, ones[:, :], T1[:, c % 2]).then_inc(sq_done, 1)

            def evac(act, out, ps, func, bias=0.0, scale=1.0):
                for j, (c, w) in enumerate(COLS):
                    last = act.activation(out[:, c:c + w], ps[:, j, 0:w], func, bias=bias, scale=scale)
                return last

            @block.scalar
            def _(act):
                act.wait_ge(small_in, 16 * 7)
                act.activation(PML[0:64, 0, :], PML[0:64, 0, :], ACT.Tanh)
                act.activation(PML[:, 1, :], PML[:, 1, :], ACT.Sigmoid)
                act.drain().then_inc(squashed, 1)

                def maps(c):
                    act.wait_ge(w_done, c + 1)
                    if c >= 2:
                        act.wait_ge(factored, c - 1)
                    evac(act, EE[:, c % 2], PA, ACT.Sigmoid, bias=vec[:, 0, c:c + 1]).then_inc(w_read, 1)
                    act.wait_ge(a_done, c + 1)
                    evac(act, F["B"][:, c], PB, ACT.Sigmoid, bias=vec[:, 1, c:c + 1]).then_inc(a_read, 1)
                    act.activation(T1[:, c % 2], PM[:, 4 + c, :], ACT.Square,
                                   scale=vec[:, 2, c:c + 1]).then_inc(squared, 1)
                    act.wait_ge(g_done, c + 1)
                    evac(act, F["G"][:, c], PA, ACT.Copy).then_inc(g_read, 1)

                maps(0)
                for c in range(4):
                    if c + 1 < 4:
                        maps(c + 1)
                    t1, t2, t3, E = (t[:, c % 2] for t in (T1, T2, T3, EE))
                    act.wait_ge(rooted, c + 1)
                    act.activation(t1, t1, ACT.Sqrt).then_inc(root_done, 1)
                    act.wait_ge(summed_log, c + 1)
                    act.activation(E, t2, ACT.Exp)
                    act.activation(t2, t2, ACT.Exp, scale=-1.0)
                    act.activation(t3, t3, ACT.Exp)
                    act.drain().then_inc(exps, 1)

            @block.vector
            def _(dve):
                dve.wait_ge(small_in, 16 * 7)
                dve.tensor_scalar(vec[:, 4, :], vec[:, 3, :], -1.0, 1.0, ALU.mult, ALU.add)
                dve.drain()

                def sums(c):
                    t1, t2, t3, E = (t[:, c % 2] for t in (T1, T2, T3, EE))
                    dve.wait_ge(sq_done, c + 1)
                    for j, (s, w) in enumerate(COLS):
                        dve.tensor_scalar(t1[:, s:s + w], PB[:, j, 0:w], 1e-24, None, ALU.max)
                    dve.drain().then_inc(rooted, 1)
                    dve.wait_ge(squared, c + 1)
                    dve.tensor_scalar(F["A"][:, c], PM[:, 4 + c], vec[:, 2, c:c + 1], None, ALU.mult)
                    dve.wait_ge(w_read, c + 1)
                    dve.tensor_scalar(E, E, -float(2.718281828459045 ** -0.5), None, ALU.mult)
                    dve.drain()
                    dve.tensor_tensor_scan(t2, keep[:, :], E, 0.0, ALU.mult, ALU.add)
                    dve.drain()
                    dve.tensor_tensor(t3, t2, E, ALU.subtract)
                    dve.drain().then_inc(summed_log, 1)

                sums(0)
                for c in range(4):
                    if c + 1 < 4:
                        sums(c + 1)
                    r, k, B, A = PM[:, c], PM[:, 4 + c], F["B"][:, c], F["A"][:, c]
                    t1, t2, t3, E = (t[:, c % 2] for t in (T1, T2, T3, EE))
                    dve.wait_ge(root_done, c + 1)
                    dve.reciprocal(t1, t1)
                    dve.wait_ge(a_read, c + 1)
                    kf = F["RKK"][:, c]
                    dve.tensor_scalar(kf, B, vec[:, 3, c:c + 1], vec[:, 4, c:c + 1], ALU.mult, ALU.add)
                    dve.drain()
                    dve.tensor_tensor(A, A, t1, ALU.mult)
                    dve.tensor_tensor(k, k, kf, ALU.mult)
                    dve.drain()
                    dve.tensor_tensor(B, B, A, ALU.mult)
                    dve.scalar_tensor_tensor(kf, r, vec[:, 5, c:c + 1], k, ALU.mult, ALU.mult)
                    dve.drain()
                    dve.wait_ge(exps, c + 1)
                    dve.scalar_tensor_tensor(A, A, -1.0, t3, ALU.mult, ALU.mult)
                    dve.tensor_tensor(B, B, t2, ALU.mult)
                    dve.tensor_tensor(k, k, t2, ALU.mult)
                    dve.tensor_tensor(r, r, E, ALU.mult)
                    dve.tensor_copy(PL[:, c, 0:16], E[:, CH - 1:SEQ:CH])
                    dve.tensor_copy(PL[:, c, 16:17], E[:, TP - 1:TP])
                    dve.tensor_copy(PL[:, c, 17:25], E[:, TP + QS - 1:R:QS])
                    dve.drain().then_inc(factored, 1)


def rwkv_chunks(nc, I, PM, F, PL, s_out, ss_out, ident):
    with ExitStack() as sc:
        sc.enter_context(nc.cleanup_on_exit())
        def sb(name, shape, dt=F32):
            return sc.enter_context(nc.sbuf_tensor(f"rc_{name}", shape, dt))
        EX = sb("EX", [128, 2, 6, 4, 2, CH])
        masks = sb("masks", [128, 14, 128])
        Mlo, ZT, Q = (sb(n, [128, 4, 128]) for n in ("Mlo", "ZT", "Q"))
        Z2, NT2, RK2, RB2, brow2, krow2 = (sb(n, [128, 2, 4, 128]) for n in (
            "Z2", "NT2", "RK2", "RB2", "brow2", "krow2"))
        V2 = sb("V2", [128, 2, 4, CH])
        W1, U, Y, Y2 = (sb(n, [128, 4, CH]) for n in ("W1", "U", "Y", "Y2"))
        YE = sb("YE", [128, 4, 2, CH])
        ST = sb("ST", [128, 4, CH])
        seqm = sb("seqm", [128, NSEQ])
        lng, lnb = sb("lng", [128, 4, CH]), sb("lnb", [128, 4, CH])
        mhalf = sb("mhalf", [128, 4])
        stat = sb("stat", [128, 3, 4])
        bonus = sb("bonus", [128, 2, 4])
        stack = sb("stack", [128, CH])
        ones = sb("ones", [128, 1])
        spare = EX[:, 0].rearrange("p o c h n -> p (o c h n)")
        SS = spare[:, 0:2048].rearrange("p (c b v) -> p c b v", c=4, b=NSEQ)
        big = spare[:, 2048:2560].rearrange("p (b v) -> p b v", b=NSEQ)
        big2 = spare[:, 2560:3072].rearrange("p (b v) -> p b v", b=NSEQ)
        P0, P1, P2, P3, P4, P5, P6, P7 = (
            sc.enter_context(nc.psum_tensor(f"rc_P{i}", [128, 512], F32)) for i in range(8))
        names = ("small_in", "started", "expanded", "gram_m", "gram_r", "rows", "rows_read", "z_ready",
                 "masked", "q_done", "q_read", "zq_done", "zq_read", "w1_done", "w1_read", "u_done",
                 "u_read", "y_done", "y_read", "s_done", "s_read", "var_done", "rstd_done", "ye_done",
                 "yt_done", "yt_read", "big_done", "big_read", "spread", "sent", "ss_in")
        (small_in, started, expanded, gram_m, gram_r, rows, rows_read, z_ready, masked, q_done, q_read,
         zq_done, zq_read, w1_done, w1_read, u_done, u_read, y_done, y_read, s_done, s_read, var_done,
         rstd_done, ye_done, yt_done, yt_read, big_done, big_read, spread, sent, ss_in) = (
            nc.alloc_semaphore(name=f"rc_{n}") for n in names)
        MU, ML, MI, M1, M1T, MID, MQ, SMU = 0, 1, 2, 3, 4, 5, 6, 11
        pair = lambda P: P[:, :].rearrange("p (c n) -> p c n", c=4)
        half = lambda P: P[:, 0:4 * CH].rearrange("p (c n) -> p c n", c=4)
        SAMPLE = 17
        NCK = 18
        levels = lambda c: 2 if c == SAMPLE else 5
        before = lambda c: sum(levels(x) for x in range(c))
        row0 = lambda c: TP if c == SAMPLE else CH * c
        width = lambda c: 16 if c == 16 else CH
        operands = lambda c: [EX[:, c % 2, o].rearrange("p c h n -> p c (h n)") for o in range(6)]

        with nc.Block() as block:
            @block.sync
            def _(sp):
                for dst, src in ((masks[:, :, :], I["masks"]), (seqm[:, :], I["seqm"]),
                                 (lng[:, :, :], I["lng"]), (lnb[:, :, :], I["lnb"]),
                                 (stack[:, :], I["stack"])):
                    sp.dma_start(dst, src).then_inc(small_in, 16)
                sp.wait_ge(s_done, 17)
                sp.wait_ge(y_done, 17)
                sp.dma_start(SS, I["state"]).then_inc(ss_in, 16)
                sp.wait_ge(s_read, 17)
                sp.dma_start(s_out, ST[:, :, :]).then_inc(sent, 16)
                sp.wait_ge(s_read, 18)
                sp.dma_start(ss_out, SS).then_inc(sent, 16)
                sp.wait_ge(sent, 32)

            @block.gpsimd
            def _(pool):
                pool.memset(EX[:, :], 0.0)
                pool.memset(YE[:, :], 0.0)
                pool.memset(ST[:, :], 0.0)
                pool.memset(ones[:, :], 1.0)
                pool.memset(mhalf[:, :], -0.5)
                pool.drain().then_inc(started, 1)

                def expand(c):
                    if c >= 2:
                        pool.wait_ge(s_done, c - 1)
                        pool.wait_ge(y_done, c - 1)
                    if width(c) < CH:
                        pool.memset(EX[:, c % 2], 0.0)
                        pool.drain()
                    r, w = row0(c), width(c)
                    for h in range(2):
                        for o, src in enumerate((F["A"], F["B"], PM[:, 4:8], PM[:, 0:4], PM[:, 8:12],
                                                 F["RKK"])):
                            pool.tensor_copy(EX[64 * h:64 * h + 64, c % 2, o, :, h, 0:w],
                                             src[64 * h:64 * h + 64, :, r:r + w])
                        last = pool.drain()
                    last.then_inc(expanded, 1)

                expand(0)
                expand(1)
                for c in range(NCK):
                    if c + 2 < NCK:
                        expand(c + 2)
                    pool.wait_ge(var_done, c + 1)
                    pool.tensor_tensor(stat[:, 2, :], stat[:, 1, :], mhalf[:, :], ALU.pow)
                    pool.drain().then_inc(rstd_done, 1)

            @block.tensor
            def _(pe):
                def each(out, lhsT, rhs, n=128):
                    for p in range(4):
                        last = pe.matmul(out[:, n * p:n * p + n], lhsT[:, p], rhs[:, p], start=True, stop=True)
                    return last

                def grams(c):
                    al, be, ka, rh, vv, rk = operands(c)
                    pe.wait_ge(expanded, c + 1)
                    if c >= 1:
                        pe.wait_ge(zq_read, before(c))
                        pe.wait_ge(rows_read, c)
                    each(P0, be, al)
                    each(P1, al, be).then_inc(gram_m, 1)
                    each(P2, ka, al)
                    each(P3, ka, rh)
                    each(P4, be, rh).then_inc(gram_r, 1)

                def row_forms(c):
                    al, be, ka, rh, vv, rk = operands(c)
                    pe.wait_ge(masked, c + 1)
                    for p in range(4):
                        pe.transpose(P3[:, 128 * p:128 * p + 128], be[:, p], ident[:, :])
                        pe.transpose(P4[:, 128 * p:128 * p + 128], ka[:, p], ident[:, :])
                    for p in range(4):
                        pe.matmul(P2[:, CH * p:CH * p + CH], vv[:, p], stack[:, :], start=True, stop=True)
                        last = pe.matmul(P2[:, 256 + p:257 + p], rk[:, p], ones[:, :], start=True, stop=True)
                    last.then_inc(rows, 1)

                def level_q(c, l):
                    n = before(c) + l
                    if l == 0:
                        pe.wait_ge(z_ready, c + 1)
                    else:
                        pe.wait_ge(zq_read, n)
                    each(P0, Mlo, Z2[:, c % 2]).then_inc(q_done, 1)

                def level_z(c, l):
                    n = before(c) + l
                    if l == 0:
                        pe.wait_ge(rows_read, c + 1)
                    pe.wait_ge(q_read, n + 1)
                    last = each(P1, ZT, Q)
                    if l < levels(c) - 1:
                        last = each(P2, Q, ZT)
                    last.then_inc(zq_done, 1)

                def chain_w(c):
                    al, s = operands(c)[0], c % 2
                    if c >= 1:
                        pe.wait_ge(s_read, c)
                    pe.wait_ge(rows_read, c + 1)
                    pe.wait_ge(masked, c + 1)
                    if c < SAMPLE:
                        for p in range(4):
                            o = slice(CH * p, CH * p + CH)
                            pe.matmul(P5[:, o], al[:, p], ST[:, p], start=True, stop=False)
                            last = pe.matmul(P5[:, o], NT2[:, s, p], V2[:, s, p], start=False, stop=True)
                        last.then_inc(w1_done, 1)
                    else:
                        each(P5, NT2[:, s], V2[:, s], CH).then_inc(w1_done, 1)
                        pe.wait_ge(ss_in, 16)
                        for j, x in enumerate((al, operands(c)[3])):
                            for p in range(4):
                                i = 4 * j + p
                                if i >= 1:
                                    pe.wait_ge(big_read, i)
                                pe.matmul(P4[:, :], x[:, p], SS[:, p].rearrange("k b v -> k (b v)"),
                                          start=True, stop=True).then_inc(big_done, 1)

                def chain_u(c):
                    pe.wait_ge(w1_read, c + 1)
                    pe.wait_ge(zq_read, before(c + 1))
                    if c >= 1:
                        pe.wait_ge(yt_read, c)
                    each(P6, Z2[:, c % 2], W1, CH).then_inc(u_done, 1)

                def chain_y(c):
                    rh, s = operands(c)[3], c % 2
                    pe.wait_ge(u_read, c + 1)
                    if c >= 1:
                        pe.wait_ge(y_read, c)
                    for p in range(4):
                        o = slice(CH * p, CH * p + CH)
                        if c < SAMPLE:
                            pe.matmul(P7[:, o], rh[:, p], ST[:, p], start=True, stop=False)
                        pe.matmul(P7[:, o], RB2[:, s, p], U[:, p], start=c == SAMPLE, stop=False)
                        last = pe.matmul(P7[:, o], RK2[:, s, p], V2[:, s, p], start=False, stop=True)
                    last.then_inc(y_done, 1)
                    if c < SAMPLE:
                        for p in range(4):
                            o = slice(CH * p, CH * p + CH)
                            pe.matmul(P5[:, o], brow2[:, s, p], U[:, p], start=True, stop=False)
                            last = pe.matmul(P5[:, o], krow2[:, s, p], V2[:, s, p], start=False, stop=True)
                        last.then_inc(s_done, 1)
                    else:
                        for p in range(4):
                            pe.wait_ge(spread, p + 1)
                            pe.matmul(P5[:, :], brow2[:, s, p], big.rearrange("k b v -> k (b v)"),
                                      start=True, stop=False)
                            last = pe.matmul(P5[:, :], krow2[:, s, p], big2.rearrange("k b v -> k (b v)"),
                                             start=False, stop=True)
                            last.then_inc(s_done, 1)

                def turn_y(c):
                    pe.wait_ge(ye_done, c + 1)
                    for p in range(4):
                        last = pe.matmul(P6[:, CH * p:CH * p + CH], YE[:, p].rearrange("t h v -> t (h v)"),
                                         stack[:, :], start=True, stop=True)
                    last.then_inc(yt_done, 1)

                pe.wait_ge(small_in, 16 * 5)
                pe.wait_ge(started, 1)
                grams(0)
                level_q(0, 0)
                row_forms(0)
                level_z(0, 0)
                for l in range(1, levels(0)):
                    level_q(0, l)
                    level_z(0, l)
                for c in range(NCK):
                    n = c + 1
                    nl = levels(n) if n < NCK else 0
                    chain_w(c)
                    if nl:
                        grams(n)
                    chain_u(c)
                    if nl:
                        level_q(n, 0)
                        row_forms(n)
                    chain_y(c)
                    if nl:
                        level_z(n, 0)
                        level_q(n, 1)
                        level_z(n, 1)
                    if nl > 2:
                        level_q(n, 2)
                        level_z(n, 2)
                        level_q(n, 3)
                    turn_y(c)
                    if nl > 2:
                        level_z(n, 3)
                        level_q(n, 4)
                        level_z(n, 4)

            @block.scalar
            def _(act):
                def read_rows(c):
                    s = c % 2
                    act.wait_ge(rows, c + 1)
                    if c >= 2:
                        act.wait_ge(s_done, c - 1)
                        act.wait_ge(ye_done, c - 1)
                    act.activation(brow2[:, s], pair(P3), ACT.Copy)
                    act.activation(krow2[:, s], pair(P4), ACT.Copy)
                    act.activation(V2[:, s], half(P2), ACT.Copy)
                    act.activation(bonus[:, s, :], P2[:, 256:260], ACT.Copy)
                    act.drain().then_inc(rows_read, 1)

                read_rows(0)
                for c in range(NCK):
                    if c < SAMPLE:
                        act.wait_ge(w1_done, c + 1)
                        act.activation(W1[:, :, :], half(P5), ACT.Copy).then_inc(w1_read, 1)
                    act.wait_ge(u_done, c + 1)
                    act.activation(U[:, :, :], half(P6), ACT.Copy).then_inc(u_read, 1)
                    if c + 1 < NCK:
                        read_rows(c + 1)
                    if c < SAMPLE:
                        act.wait_ge(y_done, c + 1)
                        if c >= 1:
                            act.wait_ge(ye_done, c)
                        act.activation(Y[:, :, :], half(P7), ACT.Copy).then_inc(y_read, 1)

            @block.vector
            def _(dve):
                mask = lambda i: masks[:, i:i + 1, :].to_broadcast([128, 4, 128])
                wide = lambda t: t.rearrange("p (c a) -> p c a", a=1).to_broadcast([128, 4, CH])
                own = seqm[:, :].rearrange("p (b a) -> p b a", a=1).to_broadcast([128, NSEQ, CH])

                def prepare(c):
                    s = c % 2
                    mu, ml, mi = (SMU, SMU + 1, SMU + 2) if c == SAMPLE else (MU, ML, MI)
                    dve.wait_ge(gram_m, c + 1)
                    dve.tensor_tensor(Z2[:, s], pair(P0), mask(M1), ALU.mult)
                    dve.tensor_tensor(ZT[:, :, :], pair(P1), mask(M1T), ALU.mult)
                    dve.tensor_tensor(Mlo[:, :, :], pair(P1), mask(ml), ALU.mult)
                    dve.drain()
                    dve.tensor_tensor(Z2[:, s], Z2[:, s], mask(MID), ALU.add)
                    dve.tensor_tensor(ZT[:, :, :], ZT[:, :, :], mask(MID), ALU.add)
                    dve.drain().then_inc(z_ready, 1)
                    dve.wait_ge(gram_r, c + 1)
                    dve.tensor_tensor(NT2[:, s], pair(P2), mask(mu), ALU.mult)
                    dve.tensor_tensor(RK2[:, s], pair(P3), mask(mi), ALU.mult)
                    dve.tensor_tensor(RB2[:, s], pair(P4), mask(mi), ALU.mult)
                    dve.drain().then_inc(masked, 1)

                def level_q(c, l):
                    dve.wait_ge(q_done, before(c) + l + 1)
                    dve.tensor_tensor(Q[:, :, :], pair(P0), mask(MQ + l), ALU.mult)
                    dve.drain().then_inc(q_read, 1)

                def level_z(c, l):
                    s = c % 2
                    dve.wait_ge(zq_done, before(c) + l + 1)
                    dve.tensor_tensor(Z2[:, s], Z2[:, s], pair(P1), ALU.add)
                    if l < levels(c) - 1:
                        dve.tensor_tensor(ZT[:, :, :], ZT[:, :, :], pair(P2), ALU.add)
                    dve.drain().then_inc(zq_read, 1)

                def pick_states(c):
                    dve.wait_ge(w1_done, c + 1)
                    for i in range(8):
                        j, p = i // 4, i % 4
                        dve.wait_ge(big_done, i + 1)
                        dve.tensor_tensor(big, P4[:, :].rearrange("p (b v) -> p b v", b=8), own, ALU.mult)
                        dve.drain().then_inc(big_read, 1)
                        dve.tensor_reduce((W1, Y2)[j][:, p], big.rearrange("p b v -> p v b"), AX.X, ALU.add)
                        dve.drain()
                    dve.tensor_tensor(W1[:, :, :], W1[:, :, :], half(P5), ALU.add)
                    dve.drain().then_inc(w1_read, 1)
                    dve.wait_ge(y_done, c + 1)
                    dve.tensor_tensor(Y[:, :, :], Y2[:, :, :], half(P7), ALU.add)
                    dve.drain().then_inc(y_read, 1)

                def next_state(c):
                    s = c % 2
                    if c < SAMPLE:
                        dve.wait_ge(s_done, c + 1)
                        dve.tensor_tensor(ST[:, :, :], ST[:, :, :], half(P5), ALU.add)
                        dve.drain()
                        dve.tensor_tensor(ST[:, :, :], ST[:, :, :],
                                          PL[:, :, c:c + 1].to_broadcast([128, 4, CH]), ALU.mult)
                        dve.drain().then_inc(s_read, 1)
                        return
                    for p in range(4):
                        if p:
                            dve.wait_ge(s_done, SAMPLE + p)
                        for dst, src in ((big, U[:, :, :]), (big2, V2[:, s])):
                            dve.tensor_tensor(dst, src[:, p:p + 1, :].to_broadcast([128, NSEQ, CH]), own, ALU.mult)
                        dve.drain().then_inc(spread, 1)
                        dve.wait_ge(s_done, SAMPLE + p + 1)
                        dve.tensor_tensor(SS[:, p], SS[:, p], P5[:, :].rearrange("p (b v) -> p b v", b=8), ALU.add)
                        dve.drain()
                        dve.tensor_tensor(SS[:, p], SS[:, p], PL[:, p, 17:25].rearrange(
                            "p (b a) -> p b a", a=1).to_broadcast([128, NSEQ, CH]), ALU.mult)
                        last = dve.drain()
                    last.then_inc(s_read, 1)

                def statistics(c):
                    dve.wait_ge(y_read, c + 1)
                    dve.reduce_sum(stat[:, 0, :], Y[:, :, :], AX.X)
                    dve.drain()
                    dve.tensor_scalar(stat[:, 0, :], stat[:, 0, :], -1.0 / CH, None, ALU.mult)
                    dve.drain()
                    dve.tensor_tensor(Y[:, :, :], Y[:, :, :], wide(stat[:, 0, :]), ALU.add)
                    dve.drain()
                    dve.tensor_tensor(Y2[:, :, :], Y[:, :, :], Y[:, :, :], ALU.mult)
                    dve.drain()
                    dve.reduce_sum(stat[:, 1, :], Y2[:, :, :], AX.X)
                    dve.drain()
                    dve.tensor_scalar(stat[:, 1, :], stat[:, 1, :], 1.0 / CH, 64e-5, ALU.mult, ALU.add)
                    dve.drain().then_inc(var_done, 1)

                def finish(c):
                    dve.tensor_tensor(Y[:, :, :], Y[:, :, :], lng[:, :, :], ALU.mult)
                    dve.tensor_tensor(Y2[:, :, :], V2[:, c % 2], wide(bonus[:, c % 2, :]), ALU.mult)
                    dve.drain()
                    dve.tensor_tensor(Y2[:, :, :], Y2[:, :, :], lnb[:, :, :], ALU.add)
                    dve.wait_ge(rstd_done, c + 1)
                    dve.tensor_tensor(Y[:, :, :], Y[:, :, :], wide(stat[:, 2, :]), ALU.mult)
                    dve.drain()
                    if c >= 1:
                        dve.wait_ge(yt_done, c)
                    for h in range(2):
                        o = slice(64 * h, 64 * h + 64)
                        dve.tensor_tensor(YE[o, :, h, :], Y[o, :, :], Y2[o, :, :], ALU.add)
                    dve.drain().then_inc(ye_done, 1)

                def gate(c):
                    dve.wait_ge(yt_done, c + 1)
                    r, w = row0(c), width(c)
                    dve.tensor_tensor(F["G"][:, :, r:r + w], half(P6)[:, :, 0:w], F["G"][:, :, r:r + w], ALU.mult)
                    dve.drain().then_inc(yt_read, 1)

                dve.wait_ge(small_in, 16 * 5)
                dve.wait_ge(started, 1)
                prepare(0)
                for l in range(levels(0)):
                    level_q(0, l)
                    level_z(0, l)
                for c in range(NCK):
                    n = c + 1
                    nl = levels(n) if n < NCK else 0
                    if nl:
                        prepare(n)
                        level_q(n, 0)
                    if c == SAMPLE:
                        pick_states(c)
                    next_state(c)
                    if nl:
                        level_z(n, 0)
                        level_q(n, 1)
                    statistics(c)
                    if nl:
                        level_z(n, 1)
                    if nl > 2:
                        level_q(n, 2)
                        level_z(n, 2)
                    finish(c)
                    if nl > 2:
                        level_q(n, 3)
                    gate(c)
                    if nl > 2:
                        level_z(n, 3)
                        level_q(n, 4)
                        level_z(n, 4)


def merge(nc, I, WB, WO, gates, yr_dram, ya_dram, x1):
    with ExitStack() as sc:
        sc.enter_context(nc.cleanup_on_exit())
        def sb(name, shape, dt=F32):
            return sc.enter_context(nc.sbuf_tensor(f"mg_{name}", shape, dt))
        YT = sb("YT", [128, 2, 4, R])
        MT = sb("MT", [128, KD, R])
        G = sb("G", [128, 4, R])
        X = sb("X", [128, 2, D])
        PB = sc.enter_context(nc.psum_tensor("mg_PB", [128, 2, 3, 512], F32))
        PO = sc.enter_context(nc.psum_tensor("mg_PO", [128, 2, 512], F32))
        g_in = [nc.alloc_semaphore(name=f"mg_g_in{i}") for i in range(4)]
        x_in = [nc.alloc_semaphore(name=f"mg_x_in{i}") for i in range(2)]
        x_out = [nc.alloc_semaphore(name=f"mg_x_out{i}") for i in range(2)]
        ra_in = [nc.alloc_semaphore(name=f"mg_branch_in{i}") for i in range(2)]
        branched, branch_read, projected, added = (
            nc.alloc_semaphore(name=f"mg_{n}") for n in (
                "branched", "branch_read", "projected", "added"))
        with nc.Block() as block:
            @block.sync
            def _(sp):
                sp.dma_start(YT[:, 0], yr_dram).then_inc(ra_in[0], 16)
                sp.dma_start(YT[:, 1], ya_dram).then_inc(ra_in[1], 16)
                for u in range(2 * KD):
                    if u >= 4:
                        sp.wait_ge(branch_read, u - 3)
                    sp.dma_start(G[:, u % 4, :], gates[KD * (u % 2) + u // 2]).then_inc(g_in[u % 4], 16)
                for b, (r, n) in enumerate(BLOCKS):
                    if b >= 2:
                        sp.wait_ge(x_out[b % 2], 16 * (b // 2))
                    sp.dma_start(X[0:n, b % 2, :], I["x"][r:r + n, :]).then_inc(x_in[b % 2], 16)
                    if b >= 1:
                        q, m = BLOCKS[b - 1]
                        sp.wait_ge(x_in[(b - 1) % 2], 16 * ((b + 1) // 2))
                        sp.wait_ge(added, b)
                        sp.dma_start(x1[q:q + m, :], X[0:m, (b - 1) % 2, :]).then_inc(x_out[(b - 1) % 2], 16)
                q, m = BLOCKS[NB - 1]
                sp.wait_ge(x_in[(NB - 1) % 2], 16 * ((NB + 1) // 2))
                sp.wait_ge(added, NB)
                sp.dma_start(x1[q:q + m, :], X[0:m, (NB - 1) % 2, :]).then_inc(x_out[(NB - 1) % 2], 16)
                for i in range(2):
                    sp.wait_ge(x_out[i], 16 * ((NB + 1 - i) // 2))

            @block.tensor
            def _(pe):
                for u in range(2 * KD):
                    t, j = u // 2, u % 2
                    if t == 0:
                        pe.wait_ge(ra_in[j], 16)
                    if u >= 2:
                        pe.wait_ge(branch_read, u - 1)
                    for i, (c, w) in enumerate(COLS):
                        for k in range(4):
                            last = pe.matmul(PB[:, u % 2, i, 0:w], WB[:, j, k, 128 * t:128 * t + 128],
                                             YT[:, j, k, c:c + w], start=k == 0, stop=k == 3)
                    last.then_inc(branched, 1)
                pe.wait_ge(branch_read, 2 * KD)
                for b, (r, n) in enumerate(BLOCKS):
                    if b >= 1:
                        pe.wait_ge(added, b)
                    for j in range(2):
                        for k in range(KD):
                            last = pe.matmul(PO[0:n, j, :], MT[:, k, r:r + n], WO[:, k, 512 * j:512 * j + 512],
                                             start=k == 0, stop=k == KD - 1)
                    last.then_inc(projected, 1)

            @block.vector
            def _(dve):
                for u in range(2 * KD):
                    t, j = u // 2, u % 2
                    g = G[:, u % 4, :]
                    dve.wait_ge(g_in[u % 4], 16 * (u // 4 + 1))
                    dve.wait_ge(branched, u + 1)
                    for i, (c, w) in enumerate(COLS):
                        dve.tensor_tensor((MT[:, t, c:c + w], g[:, c:c + w])[j], g[:, c:c + w],
                                          PB[:, u % 2, i, 0:w], ALU.mult)
                    if j:
                        dve.drain()
                        dve.tensor_tensor(MT[:, t, :], MT[:, t, :], g, ALU.add)
                    dve.drain().then_inc(branch_read, 1)
                for b, (r, n) in enumerate(BLOCKS):
                    dve.wait_ge(x_in[b % 2], 16 * (b // 2 + 1))
                    dve.wait_ge(projected, b + 1)
                    dve.tensor_tensor(X[0:n, b % 2, :].rearrange("p (j c) -> p j c", j=2),
                                      X[0:n, b % 2, :].rearrange("p (j c) -> p j c", j=2), PO[0:n],
                                      ALU.add).then_inc(added, 1)


NF = DFF // 128
EARLY = 9


def ffn_up(nc, I, xT, HT, WD, conv_out):
    with ExitStack() as sc:
        sc.enter_context(nc.cleanup_on_exit())
        def sb(name, shape, dt=F32):
            return sc.enter_context(nc.sbuf_tensor(f"fu_{name}", shape, dt))
        W = sb("W", [128, 2, KD, 2, 128])
        AX = sb("AX", [128, 2, 2 + TP + NSEQ * 10])
        C = sb("C", [128, 2, R])
        cw = sb("cw", [128, 4, NF])
        cst = sb("cst", [128, NF, NSEQ, 2])
        CL = sb("CL", [128, NF, 1 + NSEQ, 2])
        PA = sc.enter_context(nc.psum_tensor("fu_PA", [128, 3, 512], F32))
        PB = sc.enter_context(nc.psum_tensor("fu_PB", [128, 3, 512], F32))
        w_in = [nc.alloc_semaphore(name=f"fu_w_in{i}") for i in range(2)]
        wd_in = nc.alloc_semaphore(name="fu_wd_in")
        small_in, zeroed, a_done, a_read, b_done, convolved, curved, finished, sent = (
            nc.alloc_semaphore(name=f"fu_{n}") for n in (
                "small_in", "zeroed", "a_done", "a_read", "b_done", "convolved", "curved", "finished", "sent"))
        with nc.Block() as block:
            @block.sync
            def _(sp):
                sp.dma_start(cw[:, :, :], I["conv_wb"]).then_inc(small_in, 16)
                sp.dma_start(cst[:, :, :, :], I["conv_state"]).then_inc(small_in, 16)
                wv = I["w_up"].rearrange("(k p) n -> p k n", p=128)
                for t in range(NF):
                    if t >= 2:
                        sp.wait_ge(b_done, t - 1)
                    for j in range(2):
                        c = DFF * j + 128 * t
                        sp.dma_start(W[:, t % 2, :, j, :], wv[:, :, c:c + 128]).then_inc(w_in[t % 2], 16)
                    if 2 <= t < 2 + EARLY:
                        f = t - 2
                        sp.dma_start(WD[:, f, :], I["w_down"][128 * f:128 * f + 128, :]).then_inc(wd_in, 16)
                sp.wait_ge(wd_in, 16 * EARLY)
                sp.wait_ge(convolved, NF)
                sp.dma_start(conv_out, CL[:, :, :, :]).then_inc(sent, 16)
                sp.wait_ge(sent, 16)

            @block.tensor
            def _(pe):
                for t in range(NF):
                    pe.wait_ge(w_in[t % 2], 32 * (t // 2 + 1))
                    for j, (P, done, free) in enumerate(((PA, a_done, a_read), (PB, b_done, finished))):
                        if t >= 1:
                            pe.wait_ge(free, t)
                        for i, (c, w) in enumerate(COLS):
                            for k in range(KD):
                                last = pe.matmul(P[:, i, 0:w], W[:, t % 2, k, j, :], xT[:, k, c:c + w],
                                                 start=k == 0, stop=k == KD - 1)
                        last.then_inc(done, 1)

            @block.scalar
            def _(act):
                act.wait_ge(zeroed, 1)
                act.wait_ge(small_in, 32)

                def curve(t):
                    act.wait_ge(convolved, t + 1)
                    act.activation(C[:, t % 2, :], C[:, t % 2, :], ACT.Gelu).then_inc(curved, 1)

                for t in range(NF):
                    ax = AX[:, t % 2]
                    seqs = ax[:, 2 + TP:].rearrange("p (b q) -> p b q", q=10)
                    if t >= 2:
                        act.wait_ge(convolved, t - 1)
                    act.activation(seqs[:, :, 0:2], cst[:, t], ACT.Copy)
                    act.wait_ge(a_done, t + 1)
                    for i, (c, w) in enumerate(COLS):
                        if c + w <= TP:
                            act.activation(ax[:, 2 + c:2 + c + w], PA[:, i, 0:w], ACT.Copy)
                        else:
                            act.activation(ax[:, 2 + c:2 + TP], PA[:, i, 0:TP - c], ACT.Copy)
                            act.activation(seqs[:, :, 2:10], PA[:, i, TP - c:w].rearrange(
                                "p (b q) -> p b q", q=8), ACT.Copy)
                    act.drain().then_inc(a_read, 1)
                    curve(t)

            @block.vector
            def _(dve):
                for i in range(2):
                    dve.memset(AX[:, i, 0:2], 0.0)
                dve.drain().then_inc(zeroed, 1)
                dve.wait_ge(small_in, 32)
                for t in range(NF):
                    ax = AX[:, t % 2]
                    seqs = ax[:, 2 + TP:].rearrange("p (b q) -> p b q", q=10)
                    cseq = C[:, t % 2, TP:R].rearrange("p (b q) -> p b q", q=8)
                    dve.wait_ge(a_read, t + 1)
                    dve.tensor_scalar(C[:, t % 2, 0:TP], ax[:, 0:TP], cw[:, 0, t:t + 1], cw[:, 3, t:t + 1],
                                      ALU.mult, ALU.add)
                    dve.tensor_scalar(cseq, seqs[:, :, 0:8], cw[:, 0, t:t + 1], cw[:, 3, t:t + 1],
                                      ALU.mult, ALU.add)
                    dve.drain()
                    for j in (1, 2):
                        dve.scalar_tensor_tensor(C[:, t % 2, 0:TP], ax[:, j:j + TP], cw[:, j, t:t + 1],
                                                 C[:, t % 2, 0:TP], ALU.mult, ALU.add)
                        dve.scalar_tensor_tensor(cseq, seqs[:, :, j:j + 8], cw[:, j, t:t + 1], cseq,
                                                 ALU.mult, ALU.add)
                        dve.drain()
                    dve.tensor_copy(CL[:, t, 0, :], ax[:, TP:TP + 2])
                    dve.tensor_copy(CL[:, t, 1:, :], seqs[:, :, 8:10])
                    dve.drain().then_inc(convolved, 1)
                    dve.wait_ge(curved, t + 1)
                    dve.wait_ge(b_done, t + 1)
                    for i, (c, w) in enumerate(COLS):
                        last = dve.tensor_tensor(HT[:, t, c:c + w], C[:, t % 2, c:c + w], PB[:, i, 0:w], ALU.mult)
                    dve.drain().then_inc(finished, 1)


def ffn_down(nc, I, HT, WD, x1, y):
    with ExitStack() as sc:
        sc.enter_context(nc.cleanup_on_exit())
        def sb(name, shape, dt=F32):
            return sc.enter_context(nc.sbuf_tensor(f"fd_{name}", shape, dt))
        W = sb("W", [128, NF - EARLY, D])
        X = sb("X", [128, 2, D])
        gain = sb("gain", [128, D])
        ss = sb("ss", [128, NB])
        mhalf = sb("mhalf", [128, 1])
        PO = sc.enter_context(nc.psum_tensor("fd_PO", [128, 2, 2, 512], F32))
        PJ = sc.enter_context(nc.psum_tensor("fd_PJ", [128, 2, 512], F32))
        lots = [(f, min(2, NF - f)) for f in range(EARLY, NF, 2)]
        w_in = [nc.alloc_semaphore(name=f"fd_w_in{i}") for i in range(len(lots))]
        x_in = [nc.alloc_semaphore(name=f"fd_x_in{i}") for i in range(2)]
        y_out = [nc.alloc_semaphore(name=f"fd_y_out{i}") for i in range(2)]
        gain_in, product, added, squared, rooted, scaled = (
            nc.alloc_semaphore(name=f"fd_{n}") for n in (
                "gain_in", "product", "added", "squared", "rooted", "scaled"))
        with nc.Block() as block:
            @block.sync
            def _(sp):
                sp.dma_start(X[:, 0, :], x1[0:128, :]).then_inc(x_in[0], 16)
                sp.dma_start(gain[:, :], I["final_g"].rearrange("(a n) -> a n", a=1).to_broadcast([128, D])
                             ).then_inc(gain_in, 16)
                for i, (f, k) in enumerate(lots):
                    sp.dma_start(W[:, f - EARLY:f - EARLY + k, :], I["w_down"][128 * f:128 * (f + k), :].rearrange(
                        "(k p) n -> p k n", p=128)).then_inc(w_in[i], 16)
                for b, (r, n) in enumerate(BLOCKS):
                    if b + 1 < NB:
                        q, m = BLOCKS[b + 1]
                        if b >= 1:
                            sp.wait_ge(y_out[(b + 1) % 2], 16 * ((b + 1) // 2))
                        sp.dma_start(X[0:m, (b + 1) % 2, :], x1[q:q + m, :]).then_inc(x_in[(b + 1) % 2], 16)
                    sp.wait_ge(x_in[b % 2], 16 * (b // 2 + 1))
                    sp.wait_ge(scaled, b + 1)
                    sp.dma_start(y[r:r + n, :], X[0:n, b % 2, :]).then_inc(y_out[b % 2], 16)
                for i in range(2):
                    sp.wait_ge(y_out[i], 16 * ((NB + 1 - i) // 2))

            @block.tensor
            def _(pe):
                for b, (r, n) in enumerate(BLOCKS):
                    if b >= 2:
                        pe.wait_ge(added, b - 1)
                    for f in range(NF):
                        w = WD[:, f] if f < EARLY else W[:, f - EARLY]
                        if b == 0 and f >= EARLY and (f - EARLY) % 2 == 0:
                            pe.wait_ge(w_in[(f - EARLY) // 2], 16)
                        for j in range(2):
                            last = pe.matmul(PO[0:n, b % 2, j, :], HT[:, f, r:r + n],
                                             w[:, 512 * j:512 * j + 512], start=f == 0, stop=f == NF - 1)
                    last.then_inc(product, 1)

            @block.scalar
            def _(act):
                for b, (r, n) in enumerate(BLOCKS):
                    act.wait_ge(added, b + 1)
                    act.activation(PJ[0:n].rearrange("p j c -> p (j c)"), X[0:n, b % 2, :], ACT.Square,
                                   accum_out=ss[0:n, b:b + 1])
                    act.drain().then_inc(squared, 1)

            @block.gpsimd
            def _(pool):
                pool.memset(mhalf[:, :], -0.5)
                pool.drain()
                for b, (r, n) in enumerate(BLOCKS):
                    pool.wait_ge(squared, b + 1)
                    pool.tensor_scalar(ss[0:n, b:b + 1], ss[0:n, b:b + 1], 1.0 / D, EPS, ALU.mult, ALU.add)
                    pool.drain()
                    pool.tensor_tensor(ss[0:n, b:b + 1], ss[0:n, b:b + 1], mhalf[0:n, :],
                                       ALU.pow).then_inc(rooted, 1)

            @block.vector
            def _(dve):
                dve.wait_ge(gain_in, 16)
                for b, (r, n) in enumerate(BLOCKS):
                    dve.wait_ge(x_in[b % 2], 16 * (b // 2 + 1))
                    dve.wait_ge(product, b + 1)
                    halves = X[0:n, b % 2, :].rearrange("p (j c) -> p j c", j=2)
                    dve.tensor_tensor(halves, halves, PO[0:n, b % 2], ALU.add)
                    dve.drain().then_inc(added, 1)
                    dve.wait_ge(rooted, b + 1)
                    dve.scalar_tensor_tensor(X[0:n, b % 2, :], X[0:n, b % 2, :], ss[0:n, b:b + 1],
                                             gain[0:n, :], ALU.mult, ALU.mult).then_inc(scaled, 1)


def program(nc, I, O, stop=99):
    ctx = ExitStack()
    with ctx:
        def sb(name, shape, dt=F32):
            return ctx.enter_context(nc.sbuf_tensor(name, shape, dt))

        def scratch(name, shape):
            return nc.dram_tensor(name, shape, F32).ap()

        ident = sb("ident", [128, 128])
        S = {"qT": scratch("qT", (128, 4, TS)), "qiT": scratch("qiT", (128, 4, TS)),
             "kT": scratch("kT", (128, 2, TS)), "kiT": scratch("kiT", (128, TS)), "wi": scratch("wi", (TS, 8))}
        xT_dram = scratch("xT_dram", (128, KD, R))
        yr_dram, ya_dram = scratch("yr_dram", (128, 4, R)), scratch("ya_dram", (128, 4, R))
        gates = scratch("gates", (2 * D // 128, 128, R))
        x1 = scratch("x1_dram", (R, D))
        copy(nc, I["ident"], ident[:, :], "ident_in")
        with ExitStack() as hold:
            def sh(name, shape):
                return hold.enter_context(nc.sbuf_tensor(name, shape, F32))
            T = {"QT": sh("QT", [128, 4, R]), "QIT": sh("QIT", [128, 4, R]), "KT": sh("KT", [128, 2, R]),
                 "KIT": sh("KIT", [128, R]), "V": sh("V", [128, NB, 256]), "WI": sh("WI", [128, NB, 8])}
            with ExitStack() as first:
                xT = first.enter_context(nc.sbuf_tensor("xT", [128, KD, R], F32))
                norm(nc, first, KD, "n1", I["x"], I["norm1_g"], xT, ident)
                dsa_project(nc, I["w_in"], I["cos"], I["sin"], xT, xT_dram, ident, T,
                            O["k"], O["v"], O["ki"], S)
            yaT = sh("yaT", [128, 4, TP])
            dsa_prompt(nc, T, yaT, ident)
            copy(nc, yaT[:, :, :], ya_dram[:, :, 0:TP], "ya_out")
        with ExitStack() as lists:
            VAL = lists.enter_context(nc.sbuf_tensor("VAL", [128, TOPK], F32))
            IDX = lists.enter_context(nc.sbuf_tensor("IDX", [128, TOPK], F32))
            PHT = lists.enter_context(nc.sbuf_tensor("PHT", [128, 2, TS], I32))
            NM = lists.enter_context(nc.sbuf_tensor("NM", [TS, TOPK + QS], F32))
            with ExitStack() as hold:
                def sr(name, shape):
                    return hold.enter_context(nc.sbuf_tensor(name, shape, F32))
                PM = sr("PM", [128, 12, R])
                with ExitStack() as lowrank:
                    PML = lowrank.enter_context(nc.sbuf_tensor("PML", [128, 2, R], F32))
                    with ExitStack() as first:
                        SC = first.enter_context(nc.sbuf_tensor("SC", [128, HALF], F32))
                        sample_scores(nc, S, I, SC, ident)
                        xT = first.enter_context(nc.sbuf_tensor("xT2", [128, KD, R], F32))
                        rwkv_project(nc, I, xT_dram, xT, PM, PML, O["shift"], gates, {"SC": SC, "VAL": VAL, "IDX": IDX})
                    F = {n: lowrank.enter_context(nc.sbuf_tensor(f"F{n}", [128, 4, R], F32))
                         for n in ("A", "B", "G", "RKK")}
                    PL = lowrank.enter_context(nc.sbuf_tensor("PL", [128, 4, 25], F32))
                    rwkv_factors(nc, I, PM, PML, F, PL)
                    rwkv_chunks(nc, I, PM, F, PL, O["state_p"], O["state_s"], ident)
                    sample_topk(nc, I, {"VAL": VAL, "IDX": IDX}, F["G"][:, :, :], yr_dram, PHT, NM, ident)
            with ExitStack() as hold:
                WB = hold.enter_context(nc.sbuf_tensor("WB", [128, 2, 4, D], F32))
                WO = hold.enter_context(nc.sbuf_tensor("WO", [128, KD, D], F32))
                sample_attend(nc, S, I, PHT, NM, ya_dram, O["v"], WB, WO, ident)
                merge(nc, I, WB, WO, gates, yr_dram, ya_dram, x1)
        HT = sb("HT", [128, NF, R])
        with ExitStack() as hold:
            WD = hold.enter_context(nc.sbuf_tensor("WD", [128, EARLY, D], F32))
            with ExitStack() as up:
                xT = up.enter_context(nc.sbuf_tensor("xT4", [128, KD, R], F32))
                norm(nc, up, KD, "n2", x1, I["norm2_g"], xT, ident)
                ffn_up(nc, I, xT, HT, WD, O["conv"])
            ffn_down(nc, I, HT, WD, x1, O["y"])


def copy(nc, t, o, name):
    with nc.cleanup_on_exit():
        d = nc.alloc_semaphore(name=name)
        with nc.Block() as block:
            @block.sync
            def _(sp):
                sp.dma_start(o, t).then_inc(d, 16)
                sp.wait_ge(d, 16)


def shape_constants():
    import numpy as np
    f = np.float32
    half = HD // 8
    inv = f(500000.0) ** (-np.arange(half, dtype=f) / half)
    pos = np.concatenate([np.arange(TP), np.tile(PAST + np.arange(QS), NSEQ)]).astype(f)
    angle = pos[:, None] * inv.astype(f)[None, :]

    def by_block(a):
        out = np.zeros((NB * 128, half), f)
        out[:R] = a
        return out.reshape(NB, 128, half).transpose(1, 0, 2)

    p = np.arange(128)
    h, s, q = p // 16, p // 8 % 2, p % 8
    expand = np.zeros((NSEQ, QS, NSEQ, QS, 8), f)
    for b in range(NSEQ):
        for i in range(QS):
            expand[b, i, b, i, :] = 1
    head, row = p // 64, p % 64
    S1, T1 = row[:, None], row[None, :]
    same = head[:, None] == head[None, :]
    beside = lambda b: same & (S1 // b % 2 == 0) & (T1 // b == S1 // b + 1)
    seq = S1 // QS == T1 // QS
    masks = [same & (S1 < T1), same & (S1 > T1), same & (S1 <= T1), beside(1), beside(1).T,
             np.eye(128, dtype=bool)] + [beside(2 ** l) for l in range(1, 6)]
    masks += [m & seq for m in masks[:3]]
    keep = np.ones(R, f)
    keep[0:TP:CH] = 0
    keep[TP:R:QS] = 0
    return {
        "cos": by_block(np.cos(angle)), "sin": by_block(np.sin(angle)), "ident": np.eye(128, dtype=f),
        "half": (p % 2).astype(f)[:, None], "sel16": ((s * 8 + q)[:, None] == np.arange(16)).astype(f),
        "late": np.where(np.arange(QS)[None, :] > (p % QS)[:, None], f(LOW), f(0)),
        "expand8": expand.reshape(TS, NSEQ, TS), "masks": np.stack(masks, 1).astype(f),
        "seqm": (row[:, None] // QS == np.arange(NSEQ)).astype(f),
        "stack": (row[:, None] == np.arange(CH)).astype(f), "ones_pair": same.astype(f),
        "keep": np.tile(keep, (128, 1)),
    }


def laid_out(a):
    import numpy as np
    col = lambda v, n: v.reshape(n, 128).T
    by_head_row = lambda v: np.repeat(v.reshape(4, 2, 64).transpose(1, 0, 2), 64, 0)
    pt = a["page_table"]
    vecs = [a[n][0].reshape(-1) for n in ("rwkv_w0", "rwkv_a0", "rwkv_k_k", "rwkv_k_a", "rwkv_r_k")]
    return {
        "x": np.concatenate([a["meta_tokens"], a["x_prompt"][0], a["x_sample"].reshape(TS, D)]),
        "norm1_g": a["norm1_g"][0], "norm2_g": a["norm2_g"][0], "final_g": a["final_norm_g"],
        "w_in": a["w_in"][0], "w_br_rwkv": a["w_br_rwkv"][0], "w_br_attn": a["w_br_attn"][0],
        "w_out": a["w_out"][0], "w_up": a["w_up"][0], "w_down": a["w_down"][0],
        "w_w2": a["rwkv_w_w2"][0], "w_a2": a["rwkv_w_a2"][0], "w_g2": a["rwkv_w_g2"][0],
        "cache_kidx": a["cache_kidx"].reshape(NPOOL * 2, PAGE // 2 * HD),
        "cache_k": a["cache_k"].reshape(NPOOL * PAGE, 256),
        "cache_v": a["cache_v"].reshape(NPOOL * PAGE, 256),
        "pt_half": pt[:, np.arange(128) // 2].T, "pt_query": np.repeat(pt, QS, 0),
        "mu": col(a["rwkv_mu"][0], 14),
        "shift": a["state_rwkv_shift"][0].reshape(NSEQ, 14, 128).transpose(2, 1, 0),
        "rvec": np.stack([col(v, 4) for v in vecs], 1),
        "lng": by_head_row(a["rwkv_lnx_g"][0]), "lnb": by_head_row(a["rwkv_lnx_b"][0]),
        "state": a["state_rwkv"][0].reshape(NSEQ, 4, 2, 64, 64).transpose(2, 4, 1, 0, 3).reshape(128, 4, NSEQ, 64),
        "conv_wb": np.stack([col(a["conv_w"][0, j], NF) for j in range(3)] + [col(a["conv_b"][0], NF)], 1),
        "conv_state": a["state_ffn_conv"][0].reshape(NSEQ, 2, NF, 128).transpose(3, 2, 0, 1),
    }


_OUTS = {"y": (R, D), "k": (R, 256), "v": (R, 256), "ki": (R, 64), "shift": (128, 14, 1 + NSEQ),
         "state_p": (128, 4, 64), "state_s": (128, 4, NSEQ, 64), "conv": (128, NF, 1 + NSEQ, 2)}


def kernel(**inputs):
    import numpy as np
    import concourse.bacc as bacc
    from concourse.bass_utils import run_bass_kernel_spmd

    nc = bacc.Bacc("TRN2", target_bir_lowering=False, num_devices=1)
    arrays, args = {}, {}
    given = {n: np.asarray(v) for n, v in inputs.items()}
    for name, v in {**shape_constants(), **laid_out(given)}.items():
        v = np.ascontiguousarray(v)
        arrays[f"in_{name}"] = v
        args[name] = nc.dram_tensor(f"in_{name}", v.shape, mybir.dt.from_np(v.dtype), kind="ExternalInput").ap()
    outs = {n: nc.dram_tensor(f"out_{n}", s, F32, kind="ExternalOutput").ap() for n, s in _OUTS.items()}
    program(nc, args, outs)
    got = run_bass_kernel_spmd(nc, [arrays], core_ids=[0]).results[0]
    y, k, v, ki, shift, sp, ss, conv = (np.asarray(got[f"out_{n}"]) for n in _OUTS)
    shift = shift.transpose(2, 1, 0).reshape(1 + NSEQ, P_R)
    sp = sp.reshape(2, 64, 4, 64).transpose(2, 0, 3, 1).reshape(1, 1, 8, 64, 64)
    ss = ss.reshape(2, 64, 4, NSEQ, 64).transpose(3, 2, 0, 4, 1).reshape(1, NSEQ, 8, 64, 64)
    conv = conv.transpose(2, 3, 1, 0).reshape(1 + NSEQ, 2, DFF)
    c = np.ascontiguousarray
    return (c(y[N_META:TP]).reshape(1, SEQ, D), c(y[TP:]).reshape(NSEQ, QS, D),
            c(k[:TP]).reshape(1, 1, TP, 4, 64), c(v[:TP]).reshape(1, 1, TP, 4, 64),
            c(ki[:TP]).reshape(1, 1, TP, 64), c(sp), c(shift[:1]).reshape(1, 1, P_R),
            c(conv[:1]).reshape(1, 1, 2, DFF),
            c(k[TP:]).reshape(1, NSEQ, QS, 4, 64), c(v[TP:]).reshape(1, NSEQ, QS, 4, 64),
            c(ki[TP:]).reshape(1, NSEQ, QS, 64), c(ss), c(shift[1:]).reshape(1, NSEQ, P_R),
            c(conv[1:]).reshape(1, NSEQ, 2, DFF))
```
